# Optimizing a Trainium2 kernel written in Bass

```python
import math
import jax, jax.numpy as jnp
from jax import lax
import numpy as np

D_MODEL = 2048
BATCH = 1
SEQ = 256
DEPTH = 1

MIX_WIDTH = D_MODEL
GW = MIX_WIDTH // 4
GDN_HEAD_DIM = 128
GDN_HEADS = GW // GDN_HEAD_DIM
GDN_CONV = 4
GDN_CHUNK = 64
SSM_HEAD_DIM = 64
SSM_HEADS = GW // SSM_HEAD_DIM
SSM_GROUPS = 2
SSM_STATE = 128
SSM_CONV = 4
SSM_CHUNK = 128
SSM_CONV_DIM = GW + 2 * SSM_GROUPS * SSM_STATE
ATTN_HEAD_DIM = 64
ATTN_Q_HEADS = GW // ATTN_HEAD_DIM
ATTN_KV_HEADS = ATTN_Q_HEADS // 4
WINDOW = 128
ROPE_THETA = 10000.0
SC_CONV = 3
SC_GROUPS = 4
MLP_HIDDEN = 4 * D_MODEL
EPS = 1e-6

IN_WIDTH = (4 * GW + 2 * GDN_HEADS) + (GW + SSM_CONV_DIM + SSM_HEADS) + (GW + 2 * ATTN_KV_HEADS * ATTN_HEAD_DIM) + 3 * GW

kernel_name = 'hymba_style_hybrid_gdn_ssd_swa_shortconv'

def in_proj_split_points():
    sizes = (GW, GW, GW, GW, GDN_HEADS, GDN_HEADS,
             GW, SSM_CONV_DIM, SSM_HEADS,
             GW, ATTN_KV_HEADS * ATTN_HEAD_DIM, ATTN_KV_HEADS * ATTN_HEAD_DIM,
             GW, GW, GW)
    return [int(s) for s in np.cumsum(sizes)[:-1]]

def rms_norm(x, w):
    xf = x.astype(jnp.float32)
    y = xf * lax.rsqrt(jnp.mean(xf * xf, axis=-1, keepdims=True) + EPS)
    return (y * w.astype(jnp.float32)).astype(x.dtype)

def l2_norm(x):
    return x * lax.rsqrt(jnp.sum(x * x, axis=-1, keepdims=True) + EPS)

def causal_dwconv(x, w):
    K, C = w.shape
    return lax.conv_general_dilated(x, w[:, None, :].astype(x.dtype), window_strides=(1,),
                                    padding=[(K - 1, 0)], dimension_numbers=('NWC', 'WIO', 'NWC'),
                                    feature_group_count=C)

def rope_tables(positions):
    inv_freq = ROPE_THETA ** (-jnp.arange(0, ATTN_HEAD_DIM, 2, dtype=jnp.float32) / ATTN_HEAD_DIM)
    ang = positions.astype(jnp.float32)[..., None] * inv_freq
    return jnp.cos(ang), jnp.sin(ang)

def apply_rope(x, cos, sin):
    x1, x2 = jnp.split(x, 2, axis=-1)
    return jnp.concatenate([x1 * cos - x2 * sin, x2 * cos + x1 * sin], axis=-1).astype(x.dtype)

def gated_deltanet(q, k, v, z, b, a, conv_w, a_log, dt_bias, norm_w):
    Bsz, L, _ = q.shape
    H, dk, Cs = GDN_HEADS, GDN_HEAD_DIM, GDN_CHUNK
    Nc = L // Cs
    f32 = jnp.float32
    qkv = jax.nn.silu(causal_dwconv(jnp.concatenate([q, k, v], axis=-1), conv_w))
    q, k, v = [t.reshape(Bsz, L, H, dk).astype(f32) for t in jnp.split(qkv, 3, axis=-1)]
    q = l2_norm(q) * (dk ** -0.5)
    k = l2_norm(k)
    beta = jax.nn.sigmoid(b.astype(f32))
    g = -jnp.exp(a_log.astype(f32)) * jax.nn.softplus(a.astype(f32) + dt_bias.astype(f32))

    def to_chunks(t):
        return t.reshape(Bsz, Nc, Cs, H, -1).transpose(0, 3, 1, 2, 4)

    q, k, v = to_chunks(q), to_chunks(k), to_chunks(v)
    beta = to_chunks(beta[..., None])[..., 0]
    gc = jnp.cumsum(to_chunks(g[..., None])[..., 0], axis=-1)
    tri_incl = jnp.tril(jnp.ones((Cs, Cs), dtype=bool))
    tri_strict = jnp.tril(jnp.ones((Cs, Cs), dtype=bool), -1)
    decay = jnp.exp(jnp.where(tri_incl, gc[..., :, None] - gc[..., None, :], -jnp.inf))
    k_beta = k * beta[..., None]
    m = jnp.where(tri_strict, jnp.einsum('bhncd,bhnsd->bhncs', k_beta, k) * decay, 0.0)
    eye = jnp.eye(Cs, dtype=f32)
    t_inv = lax.linalg.triangular_solve(eye + m, jnp.broadcast_to(eye, m.shape), left_side=True,
                                        lower=True, unit_diagonal=True)
    u = t_inv @ (v * beta[..., None])
    w = t_inv @ (k_beta * jnp.exp(gc)[..., None])
    attn = jnp.where(tri_incl, jnp.einsum('bhncd,bhnsd->bhncs', q, k) * decay, 0.0)
    q_dec = q * jnp.exp(gc)[..., None]
    k_dec = k * jnp.exp(gc[..., -1:] - gc)[..., None]
    chunk_dec = jnp.exp(gc[..., -1])

    def step(S, inp):
        u_c, w_c, qd_c, kd_c, at_c, cd_c = inp
        v_new = u_c - w_c @ S
        o = qd_c @ S + at_c @ v_new
        S = S * cd_c[..., None, None] + jnp.swapaxes(kd_c, -1, -2) @ v_new
        return S, o

    xs = tuple(jnp.moveaxis(t, 2, 0) for t in (u, w, q_dec, k_dec, attn, chunk_dec))
    _, o = lax.scan(step, jnp.zeros((Bsz, H, dk, dk), f32), xs)
    o = o.transpose(1, 0, 3, 2, 4).reshape(Bsz, L, H, dk)
    zf = z.reshape(Bsz, L, H, dk).astype(f32)
    o = rms_norm(o, norm_w) * jax.nn.silu(zf)
    return o.reshape(Bsz, L, GW).astype(z.dtype)

def mamba2_ssd(z, xbc, dt, conv_w, conv_b, a_log, dt_bias, d_skip, norm_w):
    Bsz, L, _ = z.shape
    G, R, P, N, Cs = SSM_GROUPS, SSM_HEADS // SSM_GROUPS, SSM_HEAD_DIM, SSM_STATE, SSM_CHUNK
    Nc = L // Cs
    f32 = jnp.float32
    xbc = jax.nn.silu(causal_dwconv(xbc, conv_w) + conv_b)
    xs, bm, cm = jnp.split(xbc.astype(f32), [GW, GW + G * N], axis=-1)
    xs = xs.reshape(Bsz, Nc, Cs, G, R, P)
    bm = bm.reshape(Bsz, Nc, Cs, G, N)
    cm = cm.reshape(Bsz, Nc, Cs, G, N)
    dt = jax.nn.softplus(dt.astype(f32) + dt_bias.astype(f32)).reshape(Bsz, Nc, Cs, G, R)
    a = -jnp.exp(a_log.astype(f32)).reshape(G, R)
    da_cs = jnp.cumsum((dt * a).transpose(0, 3, 4, 1, 2), axis=-1)
    tri = jnp.tril(jnp.ones((Cs, Cs), dtype=bool))
    lmat = jnp.exp(jnp.where(tri, da_cs[..., :, None] - da_cs[..., None, :], -jnp.inf))
    xdt = xs * dt[..., None]
    cb = jnp.einsum('bclgn,bcsgn->bgcls', cm, bm)
    y_diag = jnp.einsum('bgcls,bgrcls,bcsgrp->bclgrp', cb, lmat, xdt)
    decay_states = jnp.exp(da_cs[..., -1:] - da_cs)
    states = jnp.einsum('bclgn,bgrcl,bclgrp->bcgrpn', bm, decay_states, xdt)
    chunk_dec = jnp.exp(da_cs[..., -1])

    def step(S, inp):
        st, dec = inp
        return S * dec[..., None, None] + st, S

    _, prev = lax.scan(step, jnp.zeros((Bsz, G, R, P, N), f32),
                       (jnp.moveaxis(states, 1, 0), jnp.moveaxis(chunk_dec, 3, 0)))
    prev = jnp.moveaxis(prev, 0, 1)
    y_off = jnp.einsum('bclgn,bcgrpn,bgrcl->bclgrp', cm, prev, jnp.exp(da_cs))
    y = y_diag + y_off + xs * d_skip.astype(f32).reshape(G, R)[:, :, None]
    y = y.reshape(Bsz, L, GW) * jax.nn.silu(z.astype(f32))
    y = rms_norm(y.reshape(Bsz, L, G, GW // G), norm_w.reshape(G, GW // G))
    return y.reshape(Bsz, L, GW).astype(z.dtype)

def band_blocks(t):
    Bsz, L = t.shape[:2]
    cur = t.reshape(Bsz, L // WINDOW, WINDOW, *t.shape[2:])
    prev = jnp.pad(cur[:, :-1], ((0, 0), (1, 0), (0, 0), (0, 0), (0, 0)))
    return jnp.concatenate([prev, cur], axis=2)

def sliding_window_attention(q, k, v, sinks, cos, sin):
    Bsz, L, _ = q.shape
    Hkv, R, hd, W = ATTN_KV_HEADS, ATTN_Q_HEADS // ATTN_KV_HEADS, ATTN_HEAD_DIM, WINDOW
    nb = L // W
    q = apply_rope(q.reshape(Bsz, L, Hkv, R, hd), cos[:, :, None, None], sin[:, :, None, None])
    k = apply_rope(k.reshape(Bsz, L, Hkv, hd), cos[:, :, None], sin[:, :, None])
    v = v.reshape(Bsz, L, Hkv, hd)
    qb = q.reshape(Bsz, nb, W, Hkv, R, hd)
    kb, vb = band_blocks(k), band_blocks(v)
    s = jnp.einsum('bnqgrd,bnkgd->bngrqk', qb, kb, preferred_element_type=jnp.float32) * (hd ** -0.5)
    qi = jnp.arange(W)[:, None]
    kj = jnp.arange(2 * W)[None, :]
    rel = qi + W - kj
    band = (rel >= 0) & (rel < W)
    mask = band[None] & ((jnp.arange(nb)[:, None, None] > 0) | (kj >= W)[None])
    s = jnp.where(mask[None, :, None, None], s, -jnp.inf)
    sink = sinks.astype(jnp.float32).reshape(Hkv, R)[None, None, :, :, None, None]
    mx = jnp.maximum(jnp.max(s, axis=-1, keepdims=True), sink)
    p = jnp.exp(s - mx)
    p = p / (jnp.sum(p, axis=-1, keepdims=True) + jnp.exp(sink - mx))
    o = jnp.einsum('bngrqk,bnkgd->bnqgrd', p.astype(vb.dtype), vb)
    return o.reshape(Bsz, L, Hkv * R * hd)

def short_conv(b, c, h, conv_w):
    return b * causal_dwconv(c * h, conv_w)

def hybrid_mixer(h, cos, sin, w_in, w_out, gdn_conv_w, gdn_a_log, gdn_dt_bias, gdn_norm_w,
                 ssm_conv_w, ssm_conv_b, ssm_a_log, ssm_dt_bias, ssm_d, ssm_norm_w, attn_sinks, sc_conv_w):
    proj = h @ w_in
    (gq, gk, gv, gz, gb, ga, sz, sxbc, sdt, aq, ak, av, cb, cc, ch) = jnp.split(proj, in_proj_split_points(), axis=-1)
    y_a = gated_deltanet(gq, gk, gv, gz, gb, ga, gdn_conv_w, gdn_a_log, gdn_dt_bias, gdn_norm_w)
    y_b = mamba2_ssd(sz, sxbc, sdt, ssm_conv_w, ssm_conv_b, ssm_a_log, ssm_dt_bias, ssm_d, ssm_norm_w)
    y_c = sliding_window_attention(aq, ak, av, attn_sinks, cos, sin)
    y_d = short_conv(cb, cc, ch, sc_conv_w)
    return jnp.concatenate([y_a, y_b, y_c, y_d], axis=-1) @ w_out

def setup_inputs(seed: int = 0) -> dict:
    key = jax.random.key(seed)
    ks = jax.random.split(key, 26)
    f32 = jnp.float32

    def nrm(k, shape, s):
        return jax.random.normal(k, shape, f32) * s

    def gain(k, shape):
        return 1.0 + 0.05 * jax.random.normal(k, shape, f32)

    def dt_bias(k, shape):
        dt = jnp.exp(jax.random.uniform(k, shape, f32, math.log(1e-3), math.log(1e-1)))
        return dt + jnp.log(-jnp.expm1(-dt))

    def a_log(k, shape):
        return jnp.log(jax.random.uniform(k, shape, f32, 1.0, 16.0))

    return {
        'x': nrm(ks[0], (BATCH, SEQ, D_MODEL), 1.0),
        'c': nrm(ks[1], (BATCH, D_MODEL), 1.0),
        'positions': jnp.broadcast_to(jnp.arange(SEQ, dtype=jnp.int32), (BATCH, SEQ)),
        'ada_w': nrm(ks[2], (DEPTH, D_MODEL, 6 * D_MODEL), 0.5 * D_MODEL ** -0.5),
        'ada_b': nrm(ks[3], (DEPTH, 6 * D_MODEL), 0.02),
        'norm_pre_mix': gain(ks[4], (DEPTH, D_MODEL)),
        'norm_post_mix': gain(ks[5], (DEPTH, D_MODEL)),
        'norm_pre_mlp': gain(ks[6], (DEPTH, D_MODEL)),
        'norm_post_mlp': gain(ks[7], (DEPTH, D_MODEL)),
        'w_in': nrm(ks[8], (DEPTH, D_MODEL, IN_WIDTH), D_MODEL ** -0.5),
        'w_out': nrm(ks[9], (DEPTH, MIX_WIDTH, D_MODEL), MIX_WIDTH ** -0.5),
        'gdn_conv_w': nrm(ks[10], (DEPTH, GDN_CONV, 3 * GW), GDN_CONV ** -0.5),
        'gdn_a_log': a_log(ks[11], (DEPTH, GDN_HEADS)),
        'gdn_dt_bias': dt_bias(ks[12], (DEPTH, GDN_HEADS)),
        'gdn_norm_w': gain(ks[13], (DEPTH, GDN_HEAD_DIM)),
        'ssm_conv_w': nrm(ks[14], (DEPTH, SSM_CONV, SSM_CONV_DIM), SSM_CONV ** -0.5),
        'ssm_conv_b': nrm(ks[15], (DEPTH, SSM_CONV_DIM), 0.02),
        'ssm_a_log': a_log(ks[16], (DEPTH, SSM_HEADS)),
        'ssm_dt_bias': dt_bias(ks[17], (DEPTH, SSM_HEADS)),
        'ssm_d': gain(ks[18], (DEPTH, SSM_HEADS)),
        'ssm_norm_w': gain(ks[19], (DEPTH, GW)),
        'attn_sinks': nrm(ks[20], (DEPTH, ATTN_Q_HEADS), 0.5),
        'sc_conv_w': nrm(ks[21], (DEPTH, SC_CONV, GW), SC_CONV ** -0.5),
        'w_up': nrm(ks[22], (DEPTH, D_MODEL, MLP_HIDDEN), D_MODEL ** -0.5),
        'w_down': nrm(ks[23], (DEPTH, MLP_HIDDEN, D_MODEL), MLP_HIDDEN ** -0.5),
    }

def reference(x, c, positions, ada_w, ada_b, norm_pre_mix, norm_post_mix, norm_pre_mlp, norm_post_mlp,
              w_in, w_out, gdn_conv_w, gdn_a_log, gdn_dt_bias, gdn_norm_w, ssm_conv_w, ssm_conv_b,
              ssm_a_log, ssm_dt_bias, ssm_d, ssm_norm_w, attn_sinks, sc_conv_w, w_up, w_down):
    cos, sin = rope_tables(positions)
    c_act = jax.nn.silu(c)
    for i in range(DEPTH):
        mod = (c_act @ ada_w[i] + ada_b[i])[:, None, :]
        shift_a, scale_a, gate_a, shift_m, scale_m, gate_m = jnp.split(mod, 6, axis=-1)
        h = rms_norm(x, norm_pre_mix[i]) * (1.0 + scale_a) + shift_a
        y = hybrid_mixer(h, cos, sin, w_in[i], w_out[i], gdn_conv_w[i], gdn_a_log[i], gdn_dt_bias[i],
                         gdn_norm_w[i], ssm_conv_w[i], ssm_conv_b[i], ssm_a_log[i], ssm_dt_bias[i],
                         ssm_d[i], ssm_norm_w[i], attn_sinks[i], sc_conv_w[i])
        x = x + gate_a * rms_norm(y, norm_post_mix[i])
        h = rms_norm(x, norm_pre_mlp[i]) * (1.0 + scale_m) + shift_m
        y = jnp.square(jax.nn.relu(h @ w_up[i])) @ w_down[i]
        x = x + gate_m * rms_norm(y, norm_post_mlp[i])
    return x


_drawn_inputs = setup_inputs


def setup_inputs(seed=0):
    import zlib

    import numpy as np

    out = dict(_drawn_inputs(seed))
    spreads = {}
    factors = {'norm_post_mix': 3.575,
     'norm_pre_mlp': 3.597,
     'norm_post_mlp': 3.88,
     'gdn_a_log': 5.679,
     'gdn_norm_w': 8.0,
     'ssm_conv_b': 8.0,
     'ssm_d': 8.0,
     'ssm_norm_w': 6.804,
     'attn_sinks': 8.0}
    for name, (base, spread) in spreads.items():
        noise = np.random.default_rng([zlib.crc32(name.encode()), seed]).standard_normal(out[name].shape)
        drawn = base * np.exp(spread * noise) if base else spread * noise
        out[name] = __import__('jax').numpy.asarray(drawn.astype(out[name].dtype))
    for name, factor in factors.items():
        out[name] = (out[name] * factor).astype(out[name].dtype)
    return out
```

```python
from contextlib import ExitStack

import concourse.bass as bass
from concourse import mybir

F32 = mybir.dt.float32
F32R = mybir.dt.float32r
I32 = mybir.dt.int32
ALU = mybir.AluOpType
ACT = mybir.ActivationFunctionType
AX = mybir.AxisListType.X

P = 128
SEQ = 256
TT = SEQ // P
D = 2048
KT = D // P
GW = D // 4
H = 4
SH = 8
QH = 8
HD = 64
HIDDEN = 4 * D
QUARTERS = HIDDEN // D
IN_WIDTH = 5904
NB = 512
EPS = 1e-6
GK = 4
GROUPS = KT // GK
RING = 4
ADA_COLS = 2048

(IDENT, UINC, UINCB, SGT, SGTB, CH0, CH1, LV0, LV1, LV2, LV3, LV4, LV5, ONES, AMP, AMC) = range(16)
NCONST = 16
SUM_MASKS = (UINC, UINCB, SGT, SGTB, CH0, CH1)
CS_SSM, CS_GDN, REST_SSM, REST_GDN, TOT0, TOT1 = range(6)

P_DTB, P_ALOG, P_SD, P_SINK, P_FREQ, P_COLS = 0, 12, 24, 32, 40, 72

VA_C, VA_PRE_MIX, VA_PRE_MLP, VA_CONVB, VA_SC, VA_SSMN, VA_GDNN, VA_ROWS = 0, 16, 32, 48, 56, 68, 72, 73
VB_GDN, VB_SSM, VB_ROWS = 0, 48, 80

ROWS = [("c", 0, VA_C, KT), ("norm_pre_mix", 0, VA_PRE_MIX, KT), ("norm_pre_mlp", 0, VA_PRE_MLP, KT),
        ("ssm_conv_b", 0, VA_CONVB, 8), ("sc_conv_w", 0, VA_SC, 12), ("ssm_norm_w", 0, VA_SSMN, 4),
        ("gdn_norm_w", 0, VA_GDNN, 1), ("gdn_conv_w", 1, VB_GDN, 48), ("ssm_conv_w", 1, VB_SSM, 32)]
NVROWS = len(ROWS)
PRM = [("gdn_dt_bias", P_DTB, 4), ("ssm_dt_bias", P_DTB + 4, 8), ("gdn_a_log", P_ALOG, 4),
       ("ssm_a_log", P_ALOG + 4, 8), ("ssm_d", P_SD, 8), ("attn_sinks", P_SINK, 8), ("inv_freq", P_FREQ, 32)]
CHUNKS = [
    ("s1", 2048, 260), ("a1", 3592, 388), ("gq", 0, 512), ("gk", 512, 512), ("gv", 1024, 512),
    ("gz", 1536, 512), ("xbc0", 2568, 512), ("xbc1", 3080, 512), ("s2", 2308, 260), ("a2", 3980, 388),
    ("cc", 4880, 512), ("ch", 5392, 512), ("cb", 4368, 512),
]
CHUNK = {name: i for i, (name, _, _) in enumerate(CHUNKS)}
NCH = len(CHUNKS)
T_B, T_A, T_SZ, T_DT, T_AQ, T_AK, T_AV, T_GZ, T_COLS = 0, 4, 8, 520, 528, 1040, 1168, 1296, 1808
TM_AT = {"s1": 0, "s2": 260, "a1": 520, "a2": 908, "gz": T_GZ}
CONV = {"gq": (0, 0, 0), "gk": (1, 4, 4), "gv": (0, 8, 8), "xbc0": (1, 12, 0), "xbc1": (0, 16, 4)}
CONV_ORDER = ["gq", "gk", "gv", "xbc0", "xbc1"]
STAGED = ["gq", "gk", "gv", "xbc0", "xbc1", "cc", "cb"]
STG_OF = {"gq": 0, "gk": 1, "gv": 0, "xbc0": 1, "xbc1": 0, "cc": 1, "cb": 0}

SEGS = [0, 1, 3, 4, 2, 5]

W_GROUPS = NCH * GROUPS


TWO_PI = 6.283185307179586
PI2_A, PI2_B = 6.28125, 0.0019340515136718750
PI2_C = TWO_PI - PI2_A - PI2_B
PI_LOW = 3.1415925


def att_part(f):
    if f < 2:
        return 0, list(range(4 * f, 4 * f + 4)), [0]
    return 1, list(range(2 * (f - 2), 2 * (f - 2) + 2)), [0, 1]


def stream_plan():
    items = [("ada", a, k) for a in range(2) for k in range(KT)]
    rest = [("ada", a, k) for a in range(2, 6) for k in range(KT)]
    extra = len(rest) - W_GROUPS
    for g in range(W_GROUPS):
        items.append(("w", g // GROUPS, g % GROUPS))
        for _ in range(2 if g < extra else 1):
            items.append(rest.pop(0))
    return items


STREAM = stream_plan()
POS_OF = {item: pos for pos, item in enumerate(STREAM)}
POS1 = len(STREAM)
assert POS1 % RING == 0


def schedule():
    s = {g: [] for g in range(W_GROUPS)}

    def at(g, *names):
        s[min(g, W_GROUPS - 1)].extend(names)
    at(8, "softplus")
    at(9, "mod2", "sums")
    at(12, "conv_gq")
    at(13, "decay0", "decay1", "silu_gq")
    at(17, "silu_gk")
    at(21, "silu_gv")
    at(24, "silu_gz")
    at(29, "silu_xbc0")
    at(33, "silu_xbc1")
    at(36, "silu_sz")
    at(16, "conv_gk")
    at(14, "tm_q")
    at(18, "tm_k")
    at(20, "conv_gv")
    at(21, "mod3")
    at(22, "l2stat")
    at(22, "tm_v")
    at(24, "l2scale")
    at(25, "kqT")
    at(26, "kk", "qk")
    at(27, "lv0")
    for s_ in range(1, 6):
        at(26 + 2 * s_, f"invY{s_}")
        at(27 + 2 * s_, f"invX{s_}")
    at(28, "conv_xbc0")
    at(32, "conv_xbc1")
    at(38, "qdT", "uw")
    at(39, "gdn_v0", "gdn_s0")
    at(40, "gdn_v1")
    at(41, "gdn_s1", "gdn_o0")
    at(42, "gdn_v2")
    at(43, "gdn_s2")
    at(44, "gdn_v3")
    at(45, "gdn_o1")
    at(46, "gdn_gate")
    at(47, "gdn_out")
    at(48, "conv_cc")
    at(51, "mul_cb")
    at(51, "ssm_tm", "ssm_cb", "ssm_state")
    at(51, *[f"ssm_y{i}" for i in range(4)])
    at(51, "ssm_gate", "ssm_out", "rope", "att_T")
    at(51, *[f"att_s{f}" for f in range(6)])
    at(51, "att_out")
    return [s[g] for g in range(W_GROUPS)]


SCHEDULE = schedule()


def with_moves(g):
    return ([f"evac{g // GROUPS}"] if g % GROUPS == GROUPS - 1 else []) + SCHEDULE[g]

FILLS = {
    "conv_gq": 2, "conv_gk": 2, "conv_gv": 2, "conv_xbc0": 2, "conv_xbc1": 2, "conv_cc": 2, "mul_cb": 2,
    "mod0": 1, "mod1": 1, "mod2": 1, "mod3": 1, "sums": 1, "decay0": 2, "decay1": 2,
    "tm_q": 2, "tm_k": 2, "tm_v": 2, "kqT": 4, "kk": 2, "qk": 2, "lv0": 2,
    "invY1": 2, "invY2": 2, "invY3": 2, "invY4": 2, "invY5": 2,
    "invX1": 4, "invX2": 4, "invX3": 4, "invX4": 4, "invX5": 2,
    "qdT": 2, "uw": 4, "gdn_v0": 0, "gdn_v1": 2, "gdn_v2": 2, "gdn_v3": 2,
    "gdn_s0": 1, "gdn_s1": 1, "gdn_s2": 1, "gdn_o0": 1, "gdn_o1": 1, "gdn_out": 2,
    "ssm_tm": 3, "ssm_cb": 1, "ssm_state": 2, "ssm_y0": 2, "ssm_y1": 2, "ssm_y2": 2, "ssm_y3": 2,
    "ssm_out": 2, "att_T": 4, "att_s0": 3, "att_s1": 3, "att_s2": 3, "att_s3": 3, "att_s4": 3,
    "att_s5": 3, "att_out": 2, "vecT": 1, "xT": 8, "gate_a": 4, "h2T": 8,
}
ORDER = ["vecT", "xT", "mod0", "mod1"] + [n for slot in SCHEDULE for n in slot] + ["gate_a", "h2T"]


def fill_plan():
    at, n = {}, 0
    for name in ORDER:
        for i in range(FILLS.get(name, 0)):
            at[name, i] = (n % 4, n // 4)
            n += 1
    return at, n


FILL_AT, NFILLS = fill_plan()


def mlp_fill(f):
    return (NFILLS + f) % 4, (NFILLS + f) // 4


def fill_of(name, i):
    return FILL_AT[name, i]


def build(nc, a):
    with ExitStack() as ctx:
        cursor = [nc.sbuf_base + (-nc.sbuf_base) % 64]

        def place(name, shape, dt, offset):
            return nc.alloc_sbuf_tensor_at(name, shape, dt, offset=offset)

        def sb(name, shape, dt=F32):
            size = 4
            for n in shape[1:]:
                size *= n
            t = place(name, shape, dt, cursor[0])
            cursor[0] += size + (-size) % 64
            return t

        def sem(name):
            return ctx.enter_context(nc.semaphore(name))

        cst = sb("cst", [P, NCONST, P])
        vcol = sb("vcol", [P, 2, P])
        prm = sb("prm", [P, P_COLS])
        epsc = sb("epsc", [P, 2])
        cact = sb("cact", [P, KT])
        modc = sb("modc", [P, 4, KT])
        st = sb("st", [P, 64])
        trig = sb("trig", [P, 2, TT, 32])
        raw = sb("raw", [P, RING, GK * NB])
        whi = sb("whi", [P, 2, 2, NB], F32R)
        wlo = sb("wlo", [P, 2, 2, NB], F32R)
        hhi = sb("hhi", [P, KT, SEQ], F32R)
        hlo = sb("hlo", [P, KT, SEQ], F32R)
        acc = sb("acc", [P, 2, ADA_COLS])
        base = cursor[0]

        def zone(start):
            at = [start]

            def take(name, shape, dt=F32):
                size = 4
                for n in shape[1:]:
                    size *= n
                t = place(name, shape, dt, at[0])
                at[0] += size + (-size) % 64
                assert at[0] <= nc.sbuf_usable_end, (name, at[0])
                return t
            take.at = at
            return take
        z0 = zone(base)
        x0 = z0("x0", [P, TT, D])
        xn0 = z0("xn0", [P, TT, D])
        xT = z0("xT", [P, KT, SEQ])
        vrow = z0("vrow", [P, 2, P])
        posi = z0("posi", [P, TT], I32)
        posf = z0("posf", [P, TT])
        ang = z0("ang", [P, 4, TT, 32])
        angi = z0("angi", [P, TT, 32], I32)
        junk0 = z0("junk0", [P, D])

        z1 = zone(base)
        mixT = z1("mixT", [P, KT, SEQ])
        stg = z1("stg", [P, 2, TT, NB])
        ptm = z1("ptm", [P, TT, T_COLS])
        cvo = z1("cvo", [P, 20, SEQ])
        dec = z1("dec", [P, 10, TT, 12])
        sums = z1("sums", [P, len(SUM_MASKS), TT, 12])
        shared = z1.at[0]
        tm = z1("tm", [P, 3, TT, H, P])
        Dm = z1("Dm", [P, TT, H, P])
        Dt = z1("Dt", [P, TT, H, P])
        Cm = z1("Cm", [P, TT, H, P])
        Xm = z1("Xm", [P, TT, H, P])
        Xt = z1("Xt", [P, TT, H, P])
        Ym = z1("Ym", [P, TT, H, P])
        Sm = z1("Sm", [P, H, P])
        qnT = cvo[:, 0:4, :].rearrange("p j (t n) -> p (j t n)", t=TT).rearrange("p (t h n) -> p t h n", t=TT, h=H)
        knT = cvo[:, 4:8, :].rearrange("p j (t n) -> p (j t n)", t=TT).rearrange("p (t h n) -> p t h n", t=TT, h=H)
        kbg = cvo[:, 8:12, :].rearrange("p j (t n) -> p (j t n)", t=TT).rearrange("p (t h n) -> p t h n", t=TT, h=H)
        qdT = qnT
        U, WT, O, VZ = Xm, Dm, Ym, Cm

        z2 = zone(shared)
        xs = z2("xs", [P, TT, GW])
        xdt = z2("xdt", [P, TT, SH, HD])
        xdd = z2("xdd", [P, SH, HD])
        btm = z2("btm", [P, 2, P])
        CBm = z2("CBm", [P, 4, P])
        M1s = z2("M1s", [P, 2, 4, P])
        Es = z2("Es", [P, 2, 4, P])
        stt_ = z2("stt_", [P, 2, SEQ])
        yb = z2("yb", [P, TT, GW])
        ytmp = z2("ytmp", [P, TT, GW])
        assert z2.at[0] - shared <= z1.at[0] - shared
        z3 = zone(shared)
        rq = z3("rq", [P, TT, 10, HD])
        rtmp = z3("rtmp", [P, 2, TT, 10, 32])
        kz = z3("kz", [P, TT, 2, 2, P])
        qT2 = z3("qT2", [P, TT, 4, P])
        kzT = z3("kzT", [P, 4, SEQ])
        sc = z3("sc", [P, 2, NB])
        PT = z3("PT", [P, 2, 4, P])
        ats = z3("ats", [P, 6, 16])
        yc = z3("yc", [P, TT, GW])

        z4 = zone(base)
        x1 = z4("x1", [P, TT, D])
        y = z4("y", [P, TT, D])
        grow = z4("grow", [P, D])
        hful = z4("hful", [P, 2, 2, SEQ])
        rst = z4("rst", [P, 2, TT, NB])
        ahi = z4("ahi", [P, KT, SEQ], F32R)
        alo = z4("alo", [P, KT, SEQ], F32R)

        gps = [ctx.enter_context(nc.psum_tensor(f"gps{i}", [P, TT, NB], F32)) for i in range(2)]
        mx = [ctx.enter_context(nc.psum_tensor(f"mx{i}", [P, NB], F32)) for i in range(4)]

        raw_in = [sem(f"raw_in{i}") for i in range(RING)]
        slot_claimed = sem("slot_claimed")
        ada_used = sem("ada_used")
        hi_ready = sem("hi_ready")
        lo_ready = sem("lo_ready")
        halves_done = sem("halves_done")
        gemm_free = [sem(f"gemm_free{i}") for i in range(2)]
        bank_full = [sem(f"bank_full{i}") for i in range(4)]
        bank_free = [sem(f"bank_free{i}") for i in range(4)]
        cst_in, vrow_in, prm_in, x_in, pos_in = (sem(n) for n in ("cst_in", "vrow_in", "prm_in", "x_in", "pos_in"))
        rows_zero = sem("rows_zero")
        acc_zero = sem("acc_zero")
        acc_seed = [sem(f"acc_seed{i}") for i in range(2)]
        acc_full = sem("acc_full")
        vec_step = sem("vec_step")
        act_step = sem("act_step")
        pool_step = sem("pool_step")
        v_eps = sem("v_eps")
        a_ss, a_rstd, v_xn, a_cact = (sem(n) for n in ("a_ss", "a_rstd", "v_xn", "a_cact"))
        a_hi, v_hmod, v_lo = sem("a_hi"), sem("v_hmod"), sem("v_lo")
        a_silu = sem("a_silu")
        v_taps = sem("v_taps")
        a_tap = sem("a_tap")
        v_dec, a_dec = sem("v_dec"), sem("a_dec")
        p_m1 = sem("p_m1")
        p_dmask = sem("p_dmask")
        v_ss, a_rn, v_qkn, p_kbg, p_qd, v_rn = (sem(n) for n in ("v_ss", "a_rn", "v_qkn", "p_kbg", "p_qd", "v_rn"))
        p_C, v_X, p_vz, v_vz = (sem(n) for n in ("p_C", "v_X", "p_vz", "v_vz"))
        v_oss, a_orn, v_og, a_gz = (sem(n) for n in ("v_oss", "a_orn", "v_og", "a_gz"))
        v_xdt, p_ms1, v_es, v_yss, a_yrn, v_yg, a_sz = (
            sem(n) for n in ("v_xdt", "p_ms1", "v_es", "v_yss", "a_yrn", "v_yg", "a_sz"))
        p_rope, v_sc, a_p, v_yc, v_aneg, a_es = (sem(n) for n in ("p_rope", "v_sc", "a_p", "v_yc", "v_aneg", "a_es"))
        v_ang, a_trig = sem("v_ang"), sem("a_trig")
        mix_hi, mix_lo = sem("mix_hi"), sem("mix_lo")
        xr_in, wpost_in = sem("xr_in"), sem("wpost_in")
        a_yss, a_yr, v_x1, a_x1r, v_x1n, a_h2, h2_hi, h2_lo = (
            sem(n) for n in ("a_yss", "a_yr", "v_x1", "a_x1r", "v_x1n", "a_h2", "h2_hi", "h2_lo"))
        y_zero = sem("y_zero")
        a_relu, v_sq, act_hi = sem("a_relu"), sem("v_sq"), sem("act_hi")
        v_out, out_done = sem("v_out"), sem("out_done")

        block = ctx.enter_context(nc.Block())

        def tap_col(c, tap, j):
            row = (VB_GDN + tap * 12 if c[0] == "g" else VB_SSM + tap * 8) + CONV[c][2] + j
            return vcol[:, 1, row:row + 1]

        def c_(i):
            return cst[:, i, :]

        def over_heads(ap, n=H):
            return ap.unsqueeze(1).broadcast_to([P, n, ap.shape[1]])

        def over_cols(ap, n):
            return ap.unsqueeze(2).broadcast_to([P, ap.shape[1], n])

        def wait_chunk_taken(eng, ci):
            eng.wait_ge(gemm_free[ci % 2], ci // 2 + 1)

        def wait_full(eng, name, i):
            b, n = fill_of(name, i)
            eng.wait_ge(bank_full[b], n + 1)
            return mx[b]

        def wait_taken(eng, name, i):
            b, n = fill_of(name, i)
            eng.wait_ge(bank_free[b], n + 1)

        def taken(ins, name, i):
            ins.then_inc(bank_free[fill_of(name, i)[0]], 1)

        def slab(b, n=4):
            return b[:, :].rearrange("p (h n) -> p h n", h=n)

        ada_v = a["ada_w"][0].rearrange("(k p) n -> k p n", p=P)
        adab_v = a["ada_b"]
        win_v = a["w_in"][0].rearrange("(g k p) n -> g p k n", k=GK, p=P)
        wout_v = a["w_out"][0].rearrange("(g k p) n -> g p k n", k=GK, p=P)
        wup_v = a["w_up"][0].rearrange("(g k p) n -> g p k n", k=GK, p=P)
        wdn_v = a["w_down"][0].rearrange("(q g k p) n -> q g p k n", q=QUARTERS, k=GK, p=P)
        x_v = a["x"][0].rearrange("(t p) n -> p t n", p=P)
        out_v = a["out"][0].rearrange("(t p) n -> p t n", p=P)
        WOUT_ORDER = (3, 0, 1, 2)

        @block.sync
        def _(sp):
            sp.dma_start(x0[:, :, :], x_v).then_inc(x_in, 16)
            sp.dma_start(cst[:, :, :], a["consts"].rearrange("p (c n) -> p c n", n=P)).then_inc(cst_in, 16)

            def slot(i):
                return raw[:, i, :].rearrange("p (k n) -> p k n", k=GK)

            for pos, (kind, i, j) in enumerate(STREAM):
                if kind == "ada" and j == 0:
                    sp.wait_ge(acc_zero, i + 1)
                    s0 = SEGS[i] * ADA_COLS
                    sp.dma_start(acc[0:1, i % 2, :], adab_v[:, s0:s0 + ADA_COLS]).then_inc(acc_seed[i % 2], 16)
                if pos >= RING:
                    last = STREAM[pos - RING]
                    if last[0] == "ada":
                        sp.wait_ge(ada_used, last[1] * KT + last[2] + 1)
                    else:
                        sp.wait_ge(lo_ready, 2 * (last[1] * GROUPS + last[2]) + 2)
                if kind == "ada":
                    s0 = SEGS[i] * ADA_COLS
                    sp.dma_start(raw[:, pos % RING, :], ada_v[j, :, s0:s0 + ADA_COLS]).then_inc(raw_in[pos % RING], 16)
                else:
                    _, c0, w = CHUNKS[i]
                    sp.dma_start(slot(pos % RING)[:, :, 0:w], win_v[j, :, :, c0:c0 + w]).then_inc(raw_in[pos % RING], 16)
            h1 = 2 * W_GROUPS
            sp.wait_ge(ada_used, 6 * KT)
            sp.wait_ge(lo_ready, h1)
            with sp.Fori(0, 2) as it:
                for c in range(2):
                    for g in range(GROUPS):
                        i = c * GROUPS + g
                        col = sp.snap(it * (2 * NB) + c * NB)
                        split_before = sp.snap(it * (4 * GROUPS) + (h1 + 2 * (i - RING + 1)))
                        sp.wait_ge(lo_ready, split_before)
                        sp.sem_inc(slot_claimed, 1)
                        sp.dma_start(slot(i % RING), wout_v[WOUT_ORDER[g], :, :, bass.ds(col, NB)])\
                            .then_inc(raw_in[i % RING], 16)
            h2 = h1 + 8 * GROUPS
            with sp.Fori(0, QUARTERS) as q:
                for c in range(8):
                    for g in range(GROUPS):
                        i = c * GROUPS + g
                        if c < 4:
                            col = sp.snap(q * D + c * NB)
                            src = wup_v[g, :, :, bass.ds(col, NB)]
                        else:
                            src = wdn_v[bass.ds(q, 1), g, :, :, (c - 4) * NB:(c - 3) * NB]\
                                .rearrange("o p k n -> p (o k) n")
                        split_before = sp.snap(q * (16 * GROUPS) + (h2 + 2 * (i - RING + 1)))
                        sp.wait_ge(lo_ready, split_before)
                        sp.sem_inc(slot_claimed, 1)
                        sp.dma_start(slot(i % RING), src).then_inc(raw_in[i % RING], 16)
            for m in range(TT):
                sp.wait_ge(v_out, m + 1)
                sp.dma_start(out_v[:, m, :], y[:, m, :]).then_inc(out_done, 16)
            sp.wait_ge(out_done, 16 * TT)

        @block.tensor
        def _(pe):
            def fill(name, i, *extra):
                b, n = fill_of(name, i)
                if n:
                    pe.wait_ge(bank_free[b], n)
                return mx[b]

            def full(ins, name, i):
                ins.then_inc(bank_full[fill_of(name, i)[0]], 1)

            def group(psum, lhs_hi, lhs_lo, kg, g, w, h0):
                for hh in range(2):
                    pe.wait_ge(lo_ready, h0 + (hh + 1))
                    for kk in range(2):
                        k = kg * GK + hh * 2 + kk
                        for m in range(TT):
                            o = psum[:, m, 0:w]
                            xh = lhs_hi[:, k, m * P:(m + 1) * P]
                            xl = lhs_lo[:, k, m * P:(m + 1) * P]
                            first = g == 0 and hh == 0 and kk == 0
                            final = g == GROUPS - 1 and hh == 1 and kk == 1
                            pe.matmul(o, xh, whi[:, hh, kk, 0:w], start=first, stop=False)
                            pe.matmul(o, xh, wlo[:, hh, kk, 0:w], start=False, stop=False)
                            mm = pe.matmul(o, xl, whi[:, hh, kk, 0:w], start=False, stop=final)
                    mm.then_inc(halves_done, 1)

            def stage(name):
                if name.startswith("conv_") or name == "mul_cb":
                    c = name.split("_")[1]
                    if c == "cc":
                        wait_chunk_taken(pe, CHUNK["ch"])
                        s = stg[:, 1]
                    else:
                        wait_chunk_taken(pe, CHUNK[c])
                        s = stg[:, STG_OF[c]]
                    for i in range(2):
                        b = fill(name, i)
                        for j in range(2):
                            for t in range(TT):
                                mm = pe.transpose(b[:, j * SEQ + t * P:j * SEQ + (t + 1) * P],
                                                  s[:, t, (2 * i + j) * P:(2 * i + j + 1) * P], c_(IDENT))
                        full(mm, name, i)
                elif name.startswith("mod"):
                    n = int(name[3])
                    pe.wait_ge(acc_full, n + 1)
                    b = fill(name, 0)
                    for k in range(KT):
                        mm = pe.matmul(b[:, k:k + 1], acc[:, n % 2, k * P:(k + 1) * P], cst[:, ONES, 0:1], start=True, stop=True)
                    full(mm, name, 0)
                elif name == "sums":
                    pe.wait_ge(v_dec, 3)
                    b = fill(name, 0)
                    for i, m in enumerate(SUM_MASKS):
                        mm = pe.matmul(b[:, i * 24:(i + 1) * 24], c_(m), dec[:, 9, :, :].rearrange("p t n -> p (t n)"),
                                       start=True, stop=True)
                    full(mm, name, 0)
                elif name.startswith("decay"):
                    t = int(name[5])
                    pe.wait_ge(p_m1, t + 1)
                    b = fill(name, 0)
                    mm = pe.matmul(b[:, :], c_(UINC), Cm[:, t].rearrange("p h n -> p (h n)"), start=True, stop=True)
                    full(mm, name, 0)
                    b = fill(name, 1)
                    for h in range(H):
                        mm = pe.matmul(b[:, h * P:(h + 1) * P], Cm[:, t, h, :], c_(UINC), start=True, stop=True)
                    full(mm, name, 1)
                elif name.startswith("tm_"):
                    w = "qkv".index(name[3])
                    pe.wait_ge(a_silu, w + 1)
                    for t in range(TT):
                        b = fill(name, t)
                        for h in range(H):
                            mm = pe.transpose(b[:, h * P:(h + 1) * P], cvo[:, w * 4 + h, t * P:(t + 1) * P], c_(IDENT))
                        full(mm, name, t)
                elif name == "kqT":
                    pe.wait_ge(v_qkn, 2)
                    for w in range(2):
                        for t in range(TT):
                            b = fill(name, w * 2 + t)
                            for h in range(H):
                                mm = pe.transpose(b[:, h * P:(h + 1) * P], tm[:, 1 - w, t, h, :], c_(IDENT))
                            full(mm, name, w * 2 + t)
                elif name in ("kk", "qk"):
                    for t in range(TT):
                        wait_taken(pe, "kqT", t)
                        wait_taken(pe, "kqT", 2 + t)
                        b = fill(name, t)
                        for h in range(H):
                            r = knT if name == "kk" else qnT
                            mm = pe.matmul(b[:, h * P:(h + 1) * P], knT[:, t, h, :], r[:, t, h, :], start=True, stop=True)
                        full(mm, name, t)
                elif name == "lv0":
                    for t in range(TT):
                        pe.wait_ge(p_C, t + 1)
                        b = fill(name, t)
                        for h in range(H):
                            mm = pe.matmul(b[:, h * P:(h + 1) * P], Cm[:, t, h, :], c_(IDENT), start=True, stop=True)
                        full(mm, name, t)
                elif name.startswith("invY"):
                    lv = int(name[4])
                    for t in range(TT):
                        pe.wait_ge(p_C, 2 * lv + t + 1)
                        pe.wait_ge(v_X, 2 * (lv - 1) + t + 1)
                        b = fill(name, t)
                        for h in range(H):
                            mm = pe.matmul(b[:, h * P:(h + 1) * P], Cm[:, t, h, :], Xt[:, t, h, :], start=True, stop=True)
                        full(mm, name, t)
                elif name.startswith("invX"):
                    lv = int(name[4])
                    for t in range(TT):
                        wait_taken(pe, f"invY{lv}", t)
                        b = fill(name, t)
                        for h in range(H):
                            mm = pe.matmul(b[:, h * P:(h + 1) * P], Xm[:, t, h, :], Ym[:, t, h, :], start=True, stop=True)
                        full(mm, name, t)
                    if lv < 5:
                        for t in range(TT):
                            b = fill(name, 2 + t)
                            for h in range(H):
                                mm = pe.matmul(b[:, h * P:(h + 1) * P], Ym[:, t, h, :], Xm[:, t, h, :], start=True, stop=True)
                            full(mm, name, 2 + t)
                elif name == "qdT":
                    pe.wait_ge(p_qd, 1)
                    for t in range(TT):
                        b = fill(name, t)
                        for h in range(H):
                            mm = pe.transpose(b[:, h * P:(h + 1) * P], tm[:, 0, t, h, :], c_(IDENT))
                        full(mm, name, t)
                elif name == "uw":
                    pe.wait_ge(p_kbg, 1)
                    for t in range(TT):
                        pe.wait_ge(v_X, 2 * 5 + t + 1)
                        wait_taken(pe, "tm_v", t)
                        b = fill(name, 2 * t)
                        for h in range(H):
                            mm = pe.matmul(b[:, h * P:(h + 1) * P], Xt[:, t, h, :], tm[:, 2, t, h, :], start=True, stop=True)
                        full(mm, name, 2 * t)
                        b = fill(name, 2 * t + 1)
                        for h in range(H):
                            mm = pe.matmul(b[:, h * P:(h + 1) * P], kbg[:, t, h, :], Xt[:, t, h, :], start=True, stop=True)
                        full(mm, name, 2 * t + 1)
                elif name.startswith("gdn_v"):
                    c = int(name[5])
                    if c:
                        t = c // 2
                        wait_taken(pe, f"gdn_s{c - 1}", 0)
                        wait_taken(pe, "uw", 2 * t + 1)
                        wait_taken(pe, "qdT", t)
                        for i, lhs in enumerate((WT, qdT)):
                            b = fill(name, i)
                            for h in range(H):
                                mm = pe.matmul(b[:, h * P:(h + 1) * P], lhs[:, t, h, :], Sm[:, h, :], start=True, stop=True)
                            full(mm, name, i)
                elif name.startswith("gdn_s"):
                    c = int(name[5])
                    pe.wait_ge(v_vz, c + 1)
                    b = fill(name, 0)
                    for h in range(H):
                        mm = pe.matmul(b[:, h * P:(h + 1) * P], tm[:, 1, c // 2, h, :], VZ[:, c % 2, h, :], start=True, stop=True)
                    full(mm, name, 0)
                elif name in ("gdn_o0", "gdn_o1"):
                    t = int(name[5])
                    pe.wait_ge(v_vz, 2 * t + 2)
                    b = fill(name, 0)
                    for h in range(H):
                        for cc in range(2):
                            mm = pe.matmul(b[:, h * P:(h + 1) * P], Dt[:, t, h, :], VZ[:, cc, h, :], start=(cc == 0), stop=(cc == 1))
                    full(mm, name, 0)
                elif name == "gdn_out":
                    pe.wait_ge(v_og, 1)
                    for t in range(TT):
                        b = fill(name, t)
                        for h in range(H):
                            mm = pe.transpose(b[:, h * P:(h + 1) * P], O[:, t, h, :], c_(IDENT))
                        full(mm, name, t)
                elif name == "ssm_tm":
                    pe.wait_ge(a_silu, 5)
                    for t in range(TT):
                        b = fill(name, t)
                        for j in range(4):
                            mm = pe.transpose(b[:, j * P:(j + 1) * P], cvo[:, 12 + j, t * P:(t + 1) * P], c_(IDENT))
                        full(mm, name, t)
                    b = fill(name, 2)
                    for g in range(2):
                        mm = pe.transpose(b[:, g * P:(g + 1) * P], cvo[:, 16 + g, 0:P], c_(IDENT))
                    full(mm, name, 2)
                elif name == "ssm_cb":
                    b = fill(name, 0)
                    for t in range(TT):
                        for g in range(2):
                            mm = pe.matmul(b[:, (t * 2 + g) * P:(t * 2 + g + 1) * P], cvo[:, 16 + g, t * P:(t + 1) * P],
                                           cvo[:, 18 + g, t * P:(t + 1) * P], start=True, stop=True)
                    full(mm, name, 0)
                elif name == "ssm_state":
                    pe.wait_ge(v_xdt, 1)
                    wait_taken(pe, "ssm_tm", 2)
                    b = fill(name, 0)
                    for g in range(2):
                        mm = pe.matmul(b[:, g * SEQ:(g + 1) * SEQ], btm[:, g, :],
                                       xdd[:, 4 * g:4 * g + 4, :].rearrange("p h n -> p (h n)"), start=True, stop=True)
                    full(mm, name, 0)
                    wait_taken(pe, "ssm_state", 0)
                    b = fill(name, 1)
                    for g in range(2):
                        mm = pe.matmul(b[:, g * SEQ:(g + 1) * SEQ], cvo[:, 18 + g, P:SEQ], stt_[:, g, :], start=True, stop=True)
                    full(mm, name, 1)
                elif name.startswith("ssm_y"):
                    i = int(name[5])
                    t, g = i // 2, i % 2
                    pe.wait_ge(p_ms1, i + 1)
                    b = fill(name, 0)
                    for h in range(4):
                        mm = pe.matmul(b[:, h * P:(h + 1) * P], M1s[:, i % 2, h, :], c_(UINC), start=True, stop=True)
                    full(mm, name, 0)
                    pe.wait_ge(v_es, i + 1)
                    b = fill(name, 1)
                    for h in range(4):
                        mm = pe.matmul(b[:, h * HD:(h + 1) * HD], Es[:, i % 2, h, :], xdt[:, t, g * 4 + h, :], start=True, stop=True)
                    full(mm, name, 1)
                elif name == "ssm_out":
                    pe.wait_ge(v_yg, 1)
                    for t in range(TT):
                        b = fill(name, t)
                        for j in range(4):
                            mm = pe.transpose(b[:, j * P:(j + 1) * P], yb[:, t, j * P:(j + 1) * P], c_(IDENT))
                        full(mm, name, t)
                elif name == "att_T":
                    pe.wait_ge(p_rope, 1)
                    for t in range(TT):
                        b = fill(name, t)
                        for j in range(4):
                            mm = pe.transpose(b[:, j * P:(j + 1) * P], rq[:, t, 2 * j:2 * j + 2, :].rearrange("p h n -> p (h n)"), c_(IDENT))
                        full(mm, name, t)
                    for t in range(TT):
                        b = fill(name, 2 + t)
                        for gz in range(4):
                            mm = pe.transpose(b[:, gz * P:(gz + 1) * P], kz[:, t, gz // 2, gz % 2, :], c_(IDENT))
                        full(mm, name, 2 + t)
                elif name.startswith("att_s"):
                    f = int(name[5])
                    n, heads, blocks = att_part(f)
                    if f == 0:
                        for i in range(4):
                            wait_taken(pe, "att_T", i)
                    w = len(blocks) * P
                    b = fill(name, 0)
                    for i, h in enumerate(heads):
                        g, z = h // 4, h % 2
                        mm = pe.matmul(b[:, i * w:(i + 1) * w], qT2[:, n, h // 2, :], kzT[:, g * 2 + z, blocks[0] * P:blocks[0] * P + w],
                                       start=True, stop=True)
                    full(mm, name, 0)
                    pe.wait_ge(a_p, f + 1)
                    b = fill(name, 1)
                    for i in range(4):
                        mm = pe.transpose(b[:, i * P:(i + 1) * P], sc[:, f % 2, i * P:(i + 1) * P], c_(IDENT))
                    full(mm, name, 1)
                    wait_taken(pe, name, 1)
                    b = fill(name, 2)
                    for i, h in enumerate(heads):
                        for j, kb in enumerate(blocks):
                            mm = pe.matmul(b[:, i * HD:(i + 1) * HD], PT[:, f % 2, i * len(blocks) + j, :],
                                           ptm[:, kb, T_AV + (h // 4) * HD:T_AV + (h // 4 + 1) * HD],
                                           start=(j == 0), stop=(j == len(blocks) - 1))
                    full(mm, name, 2)
                elif name == "att_out":
                    wait_taken(pe, "att_s5", 2)
                    for t in range(TT):
                        b = fill(name, t)
                        for j in range(4):
                            mm = pe.transpose(b[:, j * P:(j + 1) * P], yc[:, t, j * P:(j + 1) * P], c_(IDENT))
                        full(mm, name, t)

            pe.wait_ge(cst_in, 16)
            pe.wait_ge(rows_zero, 1)
            pe.wait_ge(vrow_in, 16 * NVROWS)
            b = fill("vecT", 0)
            for i in range(2):
                mm = pe.transpose(b[:, i * P:(i + 1) * P], vrow[:, i, :], c_(IDENT))
            full(mm, "vecT", 0)
            pe.wait_ge(v_xn, TT)
            for j in range(8):
                b = fill("xT", j)
                for kk in range(2):
                    for t in range(TT):
                        k = 2 * j + kk
                        mm = pe.transpose(b[:, kk * SEQ + t * P:kk * SEQ + (t + 1) * P], xn0[:, t, k * P:(k + 1) * P], c_(IDENT))
                full(mm, "xT", j)
            stage("mod0")
            stage("mod1")

            for g in range(W_GROUPS):
                ci, gi = divmod(g, GROUPS)
                if gi == 0 and ci >= 2:
                    pe.wait_ge(gemm_free[ci % 2], ci // 2)
                if ci == 0:
                    pe.wait_ge(v_lo, gi + 1)
                group(gps[ci % 2], hhi, hlo, gi, gi, CHUNKS[ci][2], 2 * g)
                for name in SCHEDULE[g]:
                    stage(name)

            h1 = 2 * W_GROUPS
            with pe.Fori(0, 2) as it:
                for c in range(2):
                    ci = NCH + c
                    pe.wait_ge(gemm_free[ci % 2], it + ci // 2)
                    for g in range(GROUPS):
                        if c == 0:
                            pe.wait_ge(mix_lo, g + 1)
                        group(gps[ci % 2], hhi, hlo, WOUT_ORDER[g], g, NB, it * (4 * GROUPS) + (h1 + (c * GROUPS + g) * 2))

            for j in range(4):
                b = fill("gate_a", j)
                pe.wait_ge(acc_full, 5)
                mm = pe.matmul(b[:, :], c_(ONES), acc[:, 0, j * NB:(j + 1) * NB], start=True, stop=True)
                full(mm, "gate_a", j)
            for j in range(8):
                if j % 4 == 0:
                    pe.wait_ge(v_x1n, TT)
                b = fill("h2T", j)
                for kk in range(2):
                    for t in range(TT):
                        k = 2 * j + kk
                        mm = pe.transpose(b[:, kk * SEQ + t * P:kk * SEQ + (t + 1) * P], y[:, t, k * P:(k + 1) * P], c_(IDENT))
                full(mm, "h2T", j)

            h2 = h1 + 8 * GROUPS
            with pe.Fori(0, QUARTERS) as q:
                def turn(c):
                    pe.wait_ge(v_sq, q * 4 + (c + 1))
                    for i in range(2):
                        f = 2 * c + i
                        bank, n = mlp_fill(f)
                        b = mx[bank]
                        pe.wait_ge(bank_free[bank], q * 2 + n)
                        for j in range(2):
                            for t in range(TT):
                                mm = pe.transpose(b[:, j * SEQ + t * P:j * SEQ + (t + 1) * P],
                                                  rst[:, c % 2, t, (2 * i + j) * P:(2 * i + j + 1) * P], c_(IDENT))
                        mm.then_inc(bank_full[bank], 1)
                for c in range(8):
                    ci = NCH + 4 + c
                    pe.wait_ge(gemm_free[ci % 2], q * 4 + ci // 2)
                    for g in range(GROUPS):
                        if c == 0:
                            pe.wait_ge(h2_lo, 2 * g + 2)
                        if c == 4 and g in (0, 3):
                            b, n = mlp_fill(5 if g == 0 else 7)
                            pe.wait_ge(bank_free[b], q * 2 + (n + 1))
                        group(gps[ci % 2], hhi if c < 4 else ahi, hlo if c < 4 else alo, g, g, NB,
                              q * (16 * GROUPS) + (h2 + (c * GROUPS + g) * 2))
                        if g == 1 and 1 <= c <= 4:
                            turn(c - 1)

            pe.wait_ge(acc_full, 6)
            for j in range(4):
                b, n = mlp_fill(8 * QUARTERS + j)
                pe.wait_ge(bank_free[b], n)
                pe.matmul(mx[b][:, :], c_(ONES), acc[:, 1, j * NB:(j + 1) * NB], start=True, stop=True)\
                    .then_inc(bank_full[b], 1)

        @block.gpsimd
        def _(pool):
            pool.memset(vrow[:, :, :], 0.0).then_inc(rows_zero, 1)
            pool.memset(epsc[:, 0:1], EPS).then_inc(v_eps, 1)
            pool.memset(acc[:, 0, :], 0.0).then_inc(acc_zero, 1)
            pool.memset(acc[:, 1, :], 0.0).then_inc(acc_zero, 1)

            def level(t, lv):
                pool.tensor_tensor(Cm[:, t], Dm[:, t], over_heads(c_(LV0 + lv)), ALU.mult).then_inc(p_C, 1)

            def m1s(i):
                t, g = i // 2, i % 2
                pool.tensor_tensor(M1s[:, i % 2], over_heads(c_(SGT)), over_cols(dec[:, 9, t, 4 + 4 * g:8 + 4 * g], P),
                                   ALU.mult).then_inc(p_ms1, 1)

            def stage(name):
                if name.startswith("mod"):
                    n = int(name[3])
                    wait_full(pool, name, 0)
                    pool.memset(acc[:, n % 2, :], 0.0).then_inc(acc_zero, 1)
                elif name == "sums":
                    pool.wait_ge(v_dec, 3)
                    for t in range(TT):
                        pool.tensor_tensor(Cm[:, t], over_heads(c_(SGT)), over_cols(dec[:, 9, t, 0:H], P), ALU.mult)\
                            .then_inc(p_m1, 1)
                elif name.startswith("decay"):
                    t = int(name[5])
                    wait_taken(pool, name, 0)
                    pool.tensor_tensor(Dm[:, t], Dm[:, t], over_heads(c_(SGTB)), ALU.mult).then_inc(p_dmask, 1)
                    wait_taken(pool, name, 1)
                    pool.tensor_tensor(Dt[:, t], Dt[:, t], over_heads(c_(UINCB)), ALU.mult).then_inc(p_dmask, 1)
                elif name == "l2scale":
                    pool.wait_ge(v_qkn, 2)
                    pool.wait_ge(v_rn, 1)
                    for t in range(TT):
                        wait_taken(pool, "tm_v", t)
                        ins = pool.tensor_tensor(kbg[:, t], tm[:, 1, t], over_cols(dec[:, 8, t, 4:8], P), ALU.mult)
                    ins.then_inc(p_kbg, 1)
                elif name == "kqT":
                    for t in range(TT):
                        wait_full(pool, name, 2 + t)
                        pool.tensor_tensor(tm[:, 0, t], tm[:, 0, t], over_cols(sums[:, CS_GDN, t, 0:H], P), ALU.mult)\
                            .then_inc(p_qd, 1)
                    pool.wait_ge(p_kbg, 1)
                    for t in range(TT):
                        pool.tensor_tensor(tm[:, 1, t], tm[:, 1, t], over_cols(sums[:, REST_GDN, t, 0:H], P), ALU.mult)\
                            .then_inc(p_qd, 1)
                elif name == "kk":
                    for t in range(TT):
                        wait_taken(pool, "kk", t)
                        level(t, 0)
                elif name == "lv0":
                    for t in range(TT):
                        wait_full(pool, "lv0", t)
                        level(t, 1)
                elif name.startswith("invY"):
                    lv = int(name[4])
                    for t in range(TT):
                        wait_full(pool, name, t)
                        if lv < 5:
                            level(t, lv + 1)
                elif name == "invX5":
                    for t in range(TT):
                        wait_full(pool, name, t)
                    pool.memset(VZ[:, :, :, :], 0.0).then_inc(p_vz, 1)
                    pool.memset(O[0:64, 0], 0.0).then_inc(p_vz, 1)
                elif name == "ssm_tm":
                    wait_full(pool, "gdn_out", 1)
                    m1s(0)
                    m1s(1)
                elif name in ("ssm_y0", "ssm_y1"):
                    wait_full(pool, name, 0)
                    m1s(int(name[5]) + 2)
                elif name == "rope":
                    wait_full(pool, "ssm_out", 1)
                    pool.wait_ge(a_trig, 1)
                    wait_chunk_taken(pool, CHUNK["a2"])
                    pool.memset(kz[:, :, :, :, :], 0.0).then_inc(pool_step, 1)
                    qk = ptm[:, :, T_AQ:T_AV].rearrange("p t (h s n) -> p t h s n", h=10, s=2)
                    out = rq[:, :, :, :].rearrange("p t h (s n) -> p t h s n", s=2)
                    n = 1
                    for t in range(TT):
                        cos = trig[:, 0, t, :].unsqueeze(1).broadcast_to([P, 10, 32])
                        sin = trig[:, 1, t, :].unsqueeze(1).broadcast_to([P, 10, 32])
                        for s, (first, second, op) in enumerate(((cos, sin, ALU.subtract), (sin, cos, ALU.add))):
                            pool.tensor_tensor(rtmp[:, 0, t], qk[:, t, :, 0], first, ALU.mult).then_inc(pool_step, 1)
                            pool.tensor_tensor(rtmp[:, 1, t], qk[:, t, :, 1], second, ALU.mult).then_inc(pool_step, 1)
                            n += 2
                            pool.wait_ge(pool_step, n)
                            pool.tensor_tensor(out[:, t, :, s], rtmp[:, 0, t], rtmp[:, 1, t], op).then_inc(pool_step, 1)
                            n += 1
                            pool.wait_ge(pool_step, n)
                    for z in range(2):
                        for t in range(TT):
                            ins = pool.tensor_copy(kz[:, t, :, z, z * HD:(z + 1) * HD], rq[:, t, 8:10, :])
                    ins.then_inc(p_rope, 1)

            stage("mod0")
            stage("mod1")
            for slot in SCHEDULE:
                for name in slot:
                    stage(name)
            wait_full(pool, "h2T", 7)
            pool.memset(y[:, :, :], 0.0).then_inc(y_zero, 1)

        @block.scalar
        def _(act):
            steps = [0]

            def step(ins):
                ins.then_inc(act_step, 1)
                steps[0] += 1
                act.wait_ge(act_step, steps[0])

            for name, stack, row, n in ROWS:
                src = a[name] if name in ("c",) else a[name][0]
                if len(src.shape) == 1:
                    src = src.rearrange("(r n) -> r n", n=P)
                else:
                    src = src.rearrange("k (r n) -> (k r) n", n=P)
                if row == VA_C and stack == 0:
                    act.wait_ge(rows_zero, 1)
                act.dma_start(vrow[row:row + n, stack, :], src).then_inc(vrow_in, 16)
            for name, col, n in PRM:
                src = a[name] if name == "inv_freq" else a[name][0]
                act.dma_start(prm[:, col:col + n], src.partition_broadcast(P)).then_inc(prm_in, 16)
            act.dma_start(posi[:, :], a["positions"][0].rearrange("(t p) -> p t", p=P),
                          allow_slow_non_contiguous=True).then_inc(pos_in, 16)

            def rstd(ap, n, done):
                step(act.activation(ap, ap, ACT.Ln, bias=epsc[:, 0:1], scale=1.0 / n))
                act.activation(ap, ap, ACT.Exp, scale=-0.5).then_inc(done, 1)

            act.wait_ge(x_in, 16)
            act.wait_ge(v_eps, 1)
            for t in range(TT):
                step(act.activation(junk0[:, :], x0[:, t, :], ACT.Square, accum_out=st[:, t:t + 1]))
            rstd(st[:, 0:2], D, a_rstd)
            act.wait_ge(prm_in, 16 * len(PRM))
            act.activation(prm[:, P_ALOG:P_ALOG + 12], prm[:, P_ALOG:P_ALOG + 12], ACT.Exp).then_inc(a_rstd, 1)
            wait_full(act, "vecT", 0)
            taken(act.activation(vcol[:, :, :], mx[fill_of("vecT", 0)[0]][:, 0:2 * P].rearrange("p (v n) -> p v n", v=2), ACT.Copy), "vecT", 0)
            wait_taken(act, "vecT", 0)
            act.activation(cact[:, :], vcol[:, 0, VA_C:VA_C + KT], ACT.Silu).then_inc(a_cact, 1)
            act.wait_ge(v_ang, 1)
            act.activation(trig[:, 0], ang[:, 1], ACT.Sin)
            act.activation(trig[:, 1], ang[:, 3], ACT.Sin).then_inc(a_trig, 1)
            for j in range(8):
                b = wait_full(act, "xT", j)
                taken(act.activation(xT[:, 2 * j:2 * j + 2, :], b[:, :].rearrange("p (k n) -> p k n", k=2), ACT.Copy), "xT", j)
            for part in range(4):
                act.wait_ge(v_hmod, part + 1)
                act.activation(hhi[:, 4 * part:4 * part + 4, :], xT[:, 4 * part:4 * part + 4, :], ACT.Copy).then_inc(a_hi, 1)

            def split(slot, w, h0, n_in, count):
                for hh in range(2):
                    if hh == 0:
                        act.wait_ge(raw_in[slot], n_in)
                    if count is None or count + hh >= 2:
                        act.wait_ge(halves_done, h0 + (hh - 1))
                    src = raw[:, slot, :].rearrange("p (k n) -> p k n", k=GK)[:, 2 * hh:2 * hh + 2, 0:w]
                    act.activation(whi[:, hh, :, 0:w], src, ACT.Copy).then_inc(hi_ready, 1)

            def split_at(g):
                ci, gi = divmod(g, GROUPS)
                pos = POS_OF["w", ci, gi]
                split(pos % RING, CHUNKS[ci][2], 2 * g, 16 * (pos // RING + 1), 2 * g)

            staged = {}
            for i, c in enumerate(STAGED):
                before = [s for s in STAGED[:i] if STG_OF[s] == STG_OF[c]]
                staged[c] = before[-1] if before else None

            def evacuate(ci):
                name, _, w = CHUNKS[ci]
                if name == "ch":
                    return
                act.wait_ge(halves_done, 2 * GROUPS * (ci + 1))
                if name in STG_OF:
                    if staged[name]:
                        wait_full(act, ("mul_" if staged[name] == "cb" else "conv_") + staged[name], 1)
                    dst = stg[:, STG_OF[name], :, :]
                else:
                    dst = ptm[:, :, TM_AT[name]:TM_AT[name] + w]
                act.activation(dst, gps[ci % 2][:, :, 0:w], ACT.Copy).then_inc(gemm_free[ci % 2], 1)

            def copy_out(dst, name, i, func=ACT.Copy, **kw):
                b = wait_full(act, name, i)
                shape = dst.shape
                src = b[:, :] if len(shape) == 2 else b[:, 0:shape[1] * shape[2]].rearrange("p (h n) -> p h n", h=shape[1])
                taken(act.activation(dst, src, func, **kw), name, i)

            def stage(name):
                if name.startswith("evac"):
                    evacuate(int(name[4:]))
                elif name.startswith("conv_"):
                    c = name[5:]
                    for i in range(2):
                        b = wait_full(act, name, i)
                        for jj in range(2):
                            j = 2 * i + jj
                            if c == "cc":
                                w = vcol[:, 0, VA_SC + 2 * 4 + j:VA_SC + 2 * 4 + j + 1]
                                dst = mixT[:, 12 + j, :]
                            else:
                                tile0 = CONV[c][1]
                                w = tap_col(c, 3, j)
                                dst = cvo[:, tile0 + j, :]
                            ins = act.activation(dst, b[:, jj * SEQ:(jj + 1) * SEQ], ACT.Copy, scale=w)
                        ins.then_inc(a_tap, 1)
                elif name.startswith("silu_"):
                    c = name[5:]
                    if c == "gz":
                        wait_chunk_taken(act, CHUNK["gz"])
                        act.activation(ptm[:, :, T_GZ:T_GZ + GW], ptm[:, :, T_GZ:T_GZ + GW], ACT.Silu).then_inc(a_gz, 1)
                    elif c == "sz":
                        wait_chunk_taken(act, CHUNK["s2"])
                        act.activation(ptm[:, :, T_SZ:T_SZ + GW], ptm[:, :, T_SZ:T_SZ + GW], ACT.Silu).then_inc(a_sz, 1)
                    else:
                        tile0 = CONV[c][1]
                        wait_taken(act, "conv_" + c, 1)
                        if c[0] == "g":
                            act.activation(cvo[:, tile0:tile0 + 4, :], cvo[:, tile0:tile0 + 4, :], ACT.Silu).then_inc(a_silu, 1)
                        else:
                            for j in range(4):
                                t_ = tile0 + j
                                ins = act.activation(cvo[:, t_, :], cvo[:, t_, :], ACT.Silu,
                                                     bias=vcol[:, 0, VA_CONVB + t_ - 12:VA_CONVB + t_ - 11])
                            ins.then_inc(a_silu, 1)
                elif name == "softplus":
                    act.wait_ge(v_dec, 1)
                    act.activation(dec[:, 8, :, 8:12], ptm[:, :, T_B:T_B + 4], ACT.Exp, scale=-1.0)
                    act.activation(dec[:, 2], dec[:, 1], ACT.Exp, scale=-1.0).then_inc(a_dec, 1)
                    act.wait_ge(v_dec, 2)
                    act.activation(dec[:, 6], dec[:, 3], ACT.Ln).then_inc(a_dec, 1)
                elif name == "sums":
                    b = wait_full(act, name, 0)
                    taken(act.activation(sums[:, :, :, :].rearrange("p s t n -> p (s t n)"), b[:, 0:len(SUM_MASKS) * 24], ACT.Exp), name, 0)
                elif name.startswith("decay"):
                    t = int(name[5])
                    copy_out(Dm[:, t], name, 0, ACT.Exp)
                    copy_out(Dt[:, t], name, 1, ACT.Exp)
                elif name in ("tm_q", "tm_k"):
                    for t in range(TT):
                        copy_out(tm[:, "qk".index(name[3]), t], name, t)
                elif name == "l2stat":
                    act.wait_ge(v_ss, 2)
                    step(act.activation(st[:, 20:36], st[:, 4:20], ACT.Ln, bias=epsc[:, 0:1]))
                    act.activation(st[:, 20:36], st[:, 20:36], ACT.Exp, scale=-0.5).then_inc(a_rn, 1)
                elif name == "kqT":
                    for t in range(TT):
                        copy_out(knT[:, t], name, t)
                    for t in range(TT):
                        copy_out(qnT[:, t], name, 2 + t)
                elif name.startswith("invY"):
                    for t in range(TT):
                        copy_out(Ym[:, t], name, t)
                elif name == "qdT":
                    for t in range(TT):
                        copy_out(qdT[:, t], name, t)
                elif name == "uw":
                    for t in range(TT):
                        copy_out(U[:, t], name, 2 * t)
                        copy_out(WT[:, t], name, 2 * t + 1)
                elif name in ("gdn_v1", "gdn_v2", "gdn_v3"):
                    c = int(name[5])
                    r0 = (c % 2) * 64
                    b = wait_full(act, name, 1)
                    taken(act.activation(O[r0:r0 + 64, c // 2], slab(b)[r0:r0 + 64], ACT.Copy), name, 1)
                elif name == "gdn_gate":
                    act.wait_ge(v_oss, 1)
                    rstd(st[:, 36:44], P, a_orn)
                elif name == "gdn_out":
                    for t in range(TT):
                        copy_out(mixT[:, 0:4, t * P:(t + 1) * P], name, t, scale=vcol[:, 0, VA_GDNN:VA_GDNN + 1])
                elif name == "ssm_tm":
                    for t in range(TT):
                        b = wait_full(act, name, t)
                        taken(act.activation(xs[:, t, :], b[:, :], ACT.Copy), name, t)
                    copy_out(btm[:, :, :], name, 2)
                elif name == "ssm_state":
                    copy_out(stt_[:, :, :], name, 0)
                elif name.startswith("ssm_y"):
                    copy_out(Es[:, int(name[5]) % 2], name, 0, ACT.Exp)
                elif name == "ssm_gate":
                    act.wait_ge(v_yss, 1)
                    rstd(st[:, 44:48], SEQ, a_yrn)
                elif name == "att_T":
                    for t in range(TT):
                        copy_out(qT2[:, t], name, t)
                    for t in range(TT):
                        copy_out(kzT[:, :, t * P:(t + 1) * P], name, 2 + t)
                elif name.startswith("att_s"):
                    f = int(name[5])
                    n, heads, blocks = att_part(f)
                    w = len(blocks) * P
                    act.wait_ge(v_aneg, f + 1)
                    act.activation(ats[:, f, 8:8 + len(heads)], ats[:, f, 8:8 + len(heads)], ACT.Exp)
                    for i in range(len(heads)):
                        s = sc[:, f % 2, i * w:(i + 1) * w]
                        ins = act.activation(s, s, ACT.Exp, bias=ats[:, f, 4 + i:5 + i], accum_out=ats[:, f, 12 + i:13 + i])
                    ins.then_inc(a_p, 1)
                    copy_out(PT[:, f % 2], name, 1)
                elif name == "att_out":
                    for t in range(TT):
                        copy_out(mixT[:, 8:12, t * P:(t + 1) * P], name, t)

            split_at(0)
            for g in range(W_GROUPS):
                if g + 1 < W_GROUPS:
                    split_at(g + 1)
                for name in with_moves(g):
                    stage(name)

            act.wait_ge(halves_done, 2 * W_GROUPS)
            for i, kg in enumerate(WOUT_ORDER):
                if kg == 3:
                    wait_taken(act, "mul_cb", 1)
                if kg == 1:
                    wait_taken(act, "ssm_out", 1)
                if kg == 0:
                    wait_taken(act, "gdn_out", 1)
                if kg == 2:
                    wait_taken(act, "att_out", 1)
                act.activation(hhi[:, 4 * kg:4 * kg + 4, :], mixT[:, 4 * kg:4 * kg + 4, :], ACT.Copy).then_inc(mix_hi, 1)
            act.wait_ge(mix_lo, 4)
            act.dma_start(x1[:, :, :], x_v).then_inc(xr_in, 16)
            act.dma_start(grow[:, :], a["norm_post_mix"][0].partition_broadcast(P)).then_inc(wpost_in, 16)

            h1 = 2 * W_GROUPS
            n1 = 16 * (POS1 // RING + 1)
            with act.Fori(0, 2) as it:
                for c in range(2):
                    ci = NCH + c
                    for g in range(GROUPS):
                        i = c * GROUPS + g
                        split(i % RING, NB, it * (4 * GROUPS) + (h1 + 2 * i), it * 32 + (n1 + 16 * (i // RING)), None)
                    act.wait_ge(halves_done, it * (4 * GROUPS) + (h1 + 2 * GROUPS * (c + 1)))
                    act.activation(y[:, :, bass.ds(it * (2 * NB) + c * NB, NB)], gps[ci % 2][:, :, :], ACT.Copy)\
                        .then_inc(gemm_free[ci % 2], 1)

            junk = rst[:, :, :, :].rearrange("p b t n -> p (b t n)")
            wait_chunk_taken(act, NCH + 2)
            wait_chunk_taken(act, NCH + 3)
            for t in range(TT):
                step(act.activation(junk, y[:, t, :], ACT.Square, accum_out=st[:, 48 + t:49 + t]))
            rstd(st[:, 48:50], D, a_yr)
            for t in range(TT):
                act.wait_ge(v_x1, t + 1)
                step(act.activation(junk, x1[:, t, :], ACT.Square, accum_out=st[:, 52 + t:53 + t]))
                rstd(st[:, 52 + t:53 + t], D, a_x1r)
            act.dma_start(grow[:, :], a["norm_post_mlp"][0].partition_broadcast(P)).then_inc(wpost_in, 16)
            wait_taken(act, "mod2", 0)
            wait_taken(act, "mod3", 0)
            for j in range(8):
                b = wait_full(act, "h2T", j)
                if j >= 2:
                    act.wait_ge(h2_lo, j - 1)
                for kk in range(2):
                    k = 2 * j + kk
                    ins = act.activation(hful[:, j % 2, kk, :], b[:, kk * SEQ:(kk + 1) * SEQ], ACT.Identity,
                                         bias=modc[:, 2, k:k + 1], scale=modc[:, 3, k:k + 1])
                taken(ins, "h2T", j)
                wait_taken(act, "h2T", j)
                act.activation(hhi[:, 2 * j:2 * j + 2, :], hful[:, j % 2], ACT.Copy).then_inc(h2_hi, 1)

            h2 = h1 + 8 * GROUPS
            n2 = n1 + 64
            with act.Fori(0, QUARTERS) as q:
                def relu(c):
                    ci = NCH + 4 + c
                    act.wait_ge(halves_done, q * (16 * GROUPS) + (h2 + 2 * GROUPS * (c + 1)))
                    f = 2 * ((c + 2) % 4) + 1
                    b, n = mlp_fill(f)
                    act.wait_ge(bank_full[b], q * 2 + (n + 1 - (2 if c < 2 else 0)))
                    act.activation(rst[:, c % 2], gps[ci % 2][:, :, :], ACT.Relu).then_inc(gemm_free[ci % 2], 1)
                for c in range(8):
                    for g in range(GROUPS):
                        i = c * GROUPS + g
                        split(i % RING, NB, q * (16 * GROUPS) + (h2 + 2 * i), q * 128 + (n2 + 16 * (i // RING)), None)
                        if g == 0 and 1 <= c <= 4:
                            relu(c - 1)
                        if g == 2 and 1 <= c <= 4:
                            for i2 in range(2):
                                f = 2 * (c - 1) + i2
                                b, n = mlp_fill(f)
                                act.wait_ge(bank_full[b], q * 2 + (n + 1))
                                act.activation(ahi[:, 2 * f:2 * f + 2, :], mx[b][:, :].rearrange("p (k n) -> p k n", k=2),
                                               ACT.Copy).then_inc(act_hi, 1)
            wait_chunk_taken(act, NCH + 4 + 8 * QUARTERS - 2)
            wait_chunk_taken(act, NCH + 4 + 8 * QUARTERS - 1)
            for t in range(TT):
                step(act.activation(junk, y[:, t, :], ACT.Square, accum_out=st[:, 56 + t:57 + t]))
                rstd(st[:, 56 + t:57 + t], D, a_yss)

        @block.vector
        def _(dve):
            steps = [0]

            def step(ins):
                ins.then_inc(vec_step, 1)
                steps[0] += 1
                dve.wait_ge(vec_step, steps[0])

            dve.wait_ge(pos_in, 16)
            dve.wait_ge(prm_in, 16 * len(PRM))
            step(dve.tensor_copy(posf[:, :], posi[:, :]))
            for t in range(TT):
                ins = dve.tensor_scalar(ang[:, 0, t, :], prm[:, P_FREQ:P_FREQ + 32], posf[:, t:t + 1], None, ALU.mult)
            step(ins)
            for quarter, dst in ((0.25, 1), (0.0, 3)):
                step(dve.tensor_scalar(ang[:, 2], ang[:, 0], 1.0 / TWO_PI, quarter, ALU.mult, ALU.add))
                step(dve.tensor_copy(angi[:, :, :], ang[:, 2]))
                step(dve.tensor_copy(ang[:, 2], angi[:, :, :]))
                step(dve.scalar_tensor_tensor(out=ang[:, dst], in0=ang[:, 2], scalar=-PI2_A, in1=ang[:, 0], op0=ALU.mult, op1=ALU.add))
                step(dve.scalar_tensor_tensor(out=ang[:, dst], in0=ang[:, 2], scalar=-PI2_B, in1=ang[:, dst], op0=ALU.mult, op1=ALU.add))
                step(dve.scalar_tensor_tensor(out=ang[:, dst], in0=ang[:, 2], scalar=-PI2_C, in1=ang[:, dst], op0=ALU.mult, op1=ALU.add))
                step(dve.tensor_scalar(ang[:, dst], ang[:, dst], quarter * TWO_PI, PI_LOW, ALU.add, ALU.min))
                ins = dve.tensor_scalar(ang[:, dst], ang[:, dst], -PI_LOW, None, ALU.max)
                if dst == 3:
                    ins.then_inc(v_ang, 1)
                else:
                    step(ins)
            dve.wait_ge(a_rstd, 1)
            for t in range(TT):
                dve.tensor_scalar(xn0[:, t, :], x0[:, t, :], st[:, 2 * 0 + t:t + 1], None, ALU.mult).then_inc(v_xn, 1)

            def ada(a_, k, pos):
                if a_ == 0 and k == 0:
                    dve.wait_ge(a_cact, 1)
                if k == 0:
                    dve.wait_ge(acc_seed[a_ % 2], 16 * (a_ // 2 + 1))
                else:
                    dve.wait_ge(ada_used, a_ * KT + k)
                dve.wait_ge(raw_in[pos % RING], 16 * (pos // RING + 1))
                dve.scalar_tensor_tensor(out=acc[:, a_ % 2, :], in0=raw[:, pos % RING, :], scalar=cact[:, k:k + 1],
                                         in1=acc[:, a_ % 2, :], op0=ALU.mult, op1=ALU.add).then_inc(ada_used, 1)
                if k == KT - 1:
                    dve.wait_ge(ada_used, a_ * KT + KT)
                    dve.sem_inc(acc_full, 1)

            def split(slot, w, h0, n_in):
                dve.wait_ge(raw_in[slot], n_in)
                for hh in range(2):
                    dve.wait_ge(hi_ready, h0 + (hh + 1))
                    src = raw[:, slot, :].rearrange("p (k n) -> p k n", k=GK)[:, 2 * hh:2 * hh + 2, 0:w]
                    dve.tensor_tensor(wlo[:, hh, :, 0:w], src, whi[:, hh, :, 0:w].bitcast(F32), ALU.subtract)\
                        .then_inc(lo_ready, 1)

            def split_at(g):
                ci, gi = divmod(g, GROUPS)
                pos = POS_OF["w", ci, gi]
                split(pos % RING, CHUNKS[ci][2], 2 * g, 16 * (pos // RING + 1))
                for later in range(pos + 1, POS1):
                    if STREAM[later][0] == "w":
                        break
                    ada(STREAM[later][1], STREAM[later][2], later)

            def lower(dst_lo, src, src_hi):
                return dve.tensor_tensor(dst_lo, src, src_hi.bitcast(F32), ALU.subtract)

            def taps(name, i, dst, w_of, n_taps):
                b = wait_full(dve, name, i)
                for back in range(1, n_taps):
                    for jj in range(2):
                        d = dst(2 * i + jj)[:, back:SEQ]
                        ins = dve.scalar_tensor_tensor(out=d, in0=b[:, jj * SEQ:(jj + 1) * SEQ - back],
                                                       scalar=w_of(n_taps - 1 - back, 2 * i + jj), in1=d, op0=ALU.mult, op1=ALU.add)
                        if back == n_taps - 1 and jj == 1:
                            taken(ins, name, i)
                        elif jj == 1:
                            step(ins)

            def stage(name):
                if name == "evac" + str(CHUNK["ch"]):
                    ci = CHUNK["ch"]
                    dve.wait_ge(halves_done, 2 * GROUPS * (ci + 1))
                    wait_chunk_taken(dve, CHUNK["cc"])
                    s = stg[:, STG_OF["cc"]]
                    dve.tensor_tensor(s, gps[ci % 2][:, :, :], s, ALU.mult).then_inc(gemm_free[ci % 2], 1)
                elif name.startswith("mod"):
                    n = int(name[3])
                    b = wait_full(dve, name, 0)
                    if n % 2 == 0:
                        taken(dve.tensor_copy(modc[:, n, :], b[:, 0:KT]), name, 0)
                    else:
                        row = VA_PRE_MIX if n == 1 else VA_PRE_MLP
                        taken(dve.scalar_tensor_tensor(out=modc[:, n, :], in0=b[:, 0:KT], scalar=1.0,
                                                       in1=vcol[:, 0, row:row + KT], op0=ALU.add, op1=ALU.mult), name, 0)
                elif name.startswith("conv_"):
                    c = name[5:]
                    for i in range(2):
                        dve.wait_ge(a_tap, 2 * (CONV_ORDER + ["cc"]).index(c) + i + 1)
                        if c == "cc":
                            taps(name, i, lambda j: mixT[:, 12 + j, :],
                                 lambda tap, j: vcol[:, 0, VA_SC + tap * 4 + j:VA_SC + tap * 4 + j + 1], 3)
                        else:
                            tile0 = CONV[c][1]
                            taps(name, i, lambda j: cvo[:, tile0 + j, :], lambda tap, j: tap_col(c, tap, j), 4)
                elif name == "mul_cb":
                    for i in range(2):
                        b = wait_full(dve, name, i)
                        wait_taken(dve, "conv_cc", i)
                        d = mixT[:, 12 + 2 * i:14 + 2 * i, :]
                        taken(dve.tensor_tensor(d, b[:, :].rearrange("p (k n) -> p k n", k=2), d, ALU.mult), name, i)
                elif name == "softplus":
                    wait_chunk_taken(dve, CHUNK["s1"])
                    wait_chunk_taken(dve, CHUNK["a1"])
                    dve.wait_ge(a_rstd, 2)
                    z, ax, e, u, num, den, ln, sp = (dec[:, i] for i in range(8))
                    for col, n, at in ((T_A, 4, 0), (T_DT, 8, 4)):
                        ins = dve.tensor_tensor(z[:, :, at:at + n], ptm[:, :, col:col + n],
                                                prm[:, P_DTB + at:P_DTB + at + n].unsqueeze(1).broadcast_to([P, TT, n]), ALU.add)
                    step(ins)
                    dve.scalar_tensor_tensor(out=ax, in0=z, scalar=-1.0, in1=z, op0=ALU.mult, op1=ALU.max).then_inc(v_dec, 1)
                    dve.wait_ge(a_dec, 1)
                    dve.tensor_scalar(dec[:, 8, :, 8:12], dec[:, 8, :, 8:12], 1.0, None, ALU.add)
                    dve.tensor_scalar(u, e, 1.0, None, ALU.add).then_inc(v_dec, 1)
                    dve.wait_ge(v_dec, 2)
                    step(dve.tensor_scalar(den, u, -1.0, None, ALU.add))
                    step(dve.tensor_scalar(num, den, 0.0, None, ALU.is_equal))
                    step(dve.tensor_tensor(den, den, num, ALU.add))
                    step(dve.reciprocal(den, den))
                    dve.wait_ge(a_dec, 2)
                    step(dve.tensor_tensor(num, num, ln, ALU.add))
                    step(dve.tensor_tensor(num, num, e, ALU.mult))
                    step(dve.tensor_tensor(num, num, den, ALU.mult))
                    dve.reciprocal(dec[:, 8, :, 0:4], dec[:, 8, :, 8:12])
                    step(dve.scalar_tensor_tensor(out=sp, in0=z, scalar=0.0, in1=num, op0=ALU.max, op1=ALU.add))
                    dve.scalar_tensor_tensor(out=dec[:, 9], in0=sp, scalar=-1.0,
                                             in1=prm[:, P_ALOG:P_ALOG + 12].unsqueeze(1).broadcast_to([P, TT, 12]),
                                             op0=ALU.mult, op1=ALU.mult).then_inc(v_dec, 1)
                elif name == "sums":
                    wait_taken(dve, "sums", 0)
                    dve.wait_ge(v_dec, 3)
                    dve.tensor_tensor(dec[:, 8, :, 4:8], dec[:, 8, :, 0:4], sums[:, CS_GDN, :, 0:H], ALU.mult).then_inc(v_rn, 1)
                elif name in ("tm_q", "tm_k"):
                    w = "qk".index(name[3])
                    for t in range(TT):
                        wait_taken(dve, name, t)
                        step(dve.tensor_tensor(Ym[:, t], tm[:, w, t], tm[:, w, t], ALU.mult))
                        ins = dve.tensor_reduce(st[:, 4 + 8 * w + 4 * t:8 + 8 * w + 4 * t], Ym[:, t], AX, ALU.add)
                    ins.then_inc(v_ss, 1)
                elif name == "tm_v":
                    for t in range(TT):
                        b = wait_full(dve, name, t)
                        taken(dve.tensor_tensor(tm[:, 2, t], slab(b), over_cols(dec[:, 8, t, 0:4], P), ALU.mult), name, t)
                elif name == "l2scale":
                    dve.wait_ge(a_rn, 1)
                    for w in (0, 1):
                        n = tm[:, w].rearrange("p t h n -> p (t h) n")
                        r = over_cols(st[:, 20 + 8 * w:28 + 8 * w], P)
                        if w == 0:
                            step(dve.tensor_scalar(st[:, 20:28], st[:, 20:28], float(P) ** -0.5, None, ALU.mult))
                        dve.tensor_tensor(n, n, r, ALU.mult).then_inc(v_qkn, 1)
                elif name == "kk":
                    for t in range(TT):
                        dve.wait_ge(p_dmask, 2 * t + 1)
                        b = wait_full(dve, name, t)
                        for h in range(H):
                            ins = dve.scalar_tensor_tensor(out=Dm[:, t, h], in0=b[:, h * P:(h + 1) * P], scalar=dec[:, 8, t, h:h + 1],
                                                           in1=Dm[:, t, h], op0=ALU.mult, op1=ALU.mult)
                        taken(ins, name, t)
                elif name == "qk":
                    for t in range(TT):
                        dve.wait_ge(p_dmask, 2 * t + 2)
                        b = wait_full(dve, name, t)
                        taken(dve.tensor_tensor(Dt[:, t], slab(b), Dt[:, t], ALU.mult), name, t)
                elif name == "lv0":
                    for t in range(TT):
                        dve.wait_ge(p_C, t + 1)
                        b = wait_full(dve, name, t)
                        step(dve.scalar_tensor_tensor(out=Xt[:, t], in0=slab(b), scalar=-1.0, in1=over_heads(c_(IDENT)),
                                                      op0=ALU.mult, op1=ALU.add))
                        step(dve.tensor_tensor(Xm[:, t], Dm[:, t], over_heads(c_(LV0)), ALU.mult))
                        step(dve.scalar_tensor_tensor(out=Xm[:, t], in0=Xm[:, t], scalar=-1.0, in1=over_heads(c_(IDENT)),
                                                      op0=ALU.mult, op1=ALU.add))
                        dve.sem_inc(bank_free[fill_of(name, t)[0]], 1)
                        dve.sem_inc(v_X, 1)
                elif name.startswith("invX"):
                    lv = int(name[4])
                    for t in range(TT):
                        b = wait_full(dve, name, t)
                        ins = dve.tensor_tensor(Xt[:, t], Xt[:, t], slab(b), ALU.subtract)
                        taken(ins, name, t)
                        if lv < 5:
                            b = wait_full(dve, name, 2 + t)
                            taken(dve.tensor_tensor(Xm[:, t], Xm[:, t], slab(b), ALU.subtract), name, 2 + t)
                            wait_taken(dve, name, 2 + t)
                        wait_taken(dve, name, t)
                        dve.sem_inc(v_X, 1)
                elif name.startswith("gdn_v"):
                    c = int(name[5])
                    t, r0 = c // 2, (c % 2) * 64
                    wait_taken(dve, "uw", 2 * t)
                    if c == 0:
                        dve.wait_ge(p_vz, 2)
                        dve.tensor_copy(VZ[0:64, 0], U[0:64, 0]).then_inc(v_vz, 1)
                    else:
                        if c == 2:
                            wait_full(dve, "gdn_o0", 0)
                        b = wait_full(dve, name, 0)
                        step(dve.tensor_tensor(VZ[r0:r0 + 64, c % 2], U[r0:r0 + 64, t], slab(b)[r0:r0 + 64], ALU.subtract))
                        dve.sem_inc(bank_free[fill_of(name, 0)[0]], 1)
                        dve.sem_inc(v_vz, 1)
                elif name.startswith("gdn_s"):
                    c = int(name[5])
                    b = wait_full(dve, name, 0)
                    if c == 0:
                        taken(dve.tensor_copy(Sm[:, :, :], slab(b)), name, 0)
                    else:
                        wait_taken(dve, f"gdn_s{c - 1}", 0)
                        for h in range(H):
                            ins = dve.scalar_tensor_tensor(out=Sm[:, h], in0=Sm[:, h], scalar=sums[:, TOT0 + c % 2, c // 2, h:h + 1],
                                                           in1=b[:, h * P:(h + 1) * P], op0=ALU.mult, op1=ALU.add)
                        taken(ins, name, 0)
                elif name in ("gdn_o0", "gdn_o1"):
                    t = int(name[5])
                    b = wait_full(dve, name, 0)
                    dve.wait_ge(p_vz, 2)
                    wait_taken(dve, f"gdn_v{2 * t + 1}", 1)
                    if t:
                        wait_taken(dve, "gdn_v2", 1)
                    taken(dve.tensor_tensor(O[:, t], O[:, t], slab(b), ALU.add), name, 0)
                elif name == "gdn_gate":
                    wait_taken(dve, "gdn_o0", 0)
                    wait_taken(dve, "gdn_o1", 0)
                    step(dve.tensor_tensor(Xt[:, :, :, :], O[:, :, :, :], O[:, :, :, :], ALU.mult))
                    dve.tensor_reduce(st[:, 36:44], Xt[:, :, :, :].rearrange("p t h n -> p (t h) n"), AX, ALU.add).then_inc(v_oss, 1)
                    dve.wait_ge(a_orn, 1)
                    o = O[:, :, :, :].rearrange("p t h n -> p (t h) n")
                    step(dve.tensor_tensor(o, o, over_cols(st[:, 36:44], P), ALU.mult))
                    dve.wait_ge(a_gz, 1)
                    o = O[:, :, :, :].rearrange("p t h n -> p t (h n)")
                    dve.tensor_tensor(o, o, ptm[:, :, T_GZ:T_GZ + GW], ALU.mult).then_inc(v_og, 1)
                elif name == "ssm_tm":
                    for t in range(TT):
                        wait_taken(dve, name, t)
                    x3 = xs[:, :, :].rearrange("p t (h n) -> p t h n", h=SH)
                    for t in range(TT):
                        dve.tensor_tensor(yb[:, t, :].rearrange("p (h n) -> p h n", h=SH), x3[:, t],
                                          over_cols(prm[:, P_SD:P_SD + 8], HD), ALU.mult)
                    for t in range(TT):
                        ins = dve.tensor_tensor(xdt[:, t], x3[:, t], over_cols(dec[:, 7, t, 4:12], HD), ALU.mult)
                    step(ins)
                    dve.tensor_tensor(xdd[:, :, :], xdt[:, 0], over_cols(sums[:, REST_SSM, 0, 4:12], HD), ALU.mult).then_inc(v_xdt, 1)
                elif name == "ssm_cb":
                    b = wait_full(dve, name, 0)
                    taken(dve.tensor_tensor(CBm[:, :, :], slab(b), over_heads(c_(UINC)), ALU.mult), name, 0)
                elif name == "ssm_state":
                    b = wait_full(dve, name, 1)
                    step(dve.tensor_tensor(ytmp[:, 0, :].rearrange("p (h n) -> p h n", h=SH), b[:, :].rearrange("p (h n) -> p h n", h=SH),
                                           over_cols(sums[:, CS_SSM, 1, 4:12], HD), ALU.mult))
                    taken(dve.tensor_tensor(yb[:, 1, :], yb[:, 1, :], ytmp[:, 0, :], ALU.add), name, 1)
                elif name.startswith("ssm_y"):
                    i = int(name[5])
                    t, g = i // 2, i % 2
                    wait_taken(dve, "ssm_cb", 0)
                    wait_taken(dve, name, 0)
                    dve.tensor_tensor(Es[:, i % 2], Es[:, i % 2], over_heads(CBm[:, 2 * t + g, :]), ALU.mult).then_inc(v_es, 1)
                    b = wait_full(dve, name, 1)
                    wait_taken(dve, "ssm_state", 1)
                    d = yb[:, t, g * SEQ:(g + 1) * SEQ]
                    taken(dve.tensor_tensor(d, d, b[:, 0:SEQ], ALU.add), name, 1)
                elif name == "ssm_gate":
                    for i in range(4):
                        wait_taken(dve, f"ssm_y{i}", 1)
                    dve.wait_ge(a_sz, 1)
                    step(dve.tensor_tensor(yb[:, :, :], yb[:, :, :], ptm[:, :, T_SZ:T_SZ + GW], ALU.mult))
                    step(dve.tensor_tensor(ytmp[:, :, :], yb[:, :, :], yb[:, :, :], ALU.mult))
                    dve.tensor_reduce(st[:, 44:48], ytmp[:, :, :].rearrange("p t (g n) -> p (t g) n", g=2), AX, ALU.add).then_inc(v_yss, 1)
                    dve.wait_ge(a_yrn, 1)
                    o = yb[:, :, :].rearrange("p t (g n) -> p (t g) n", g=2)
                    dve.tensor_tensor(o, o, over_cols(st[:, 44:48], SEQ), ALU.mult).then_inc(v_yg, 1)
                elif name == "ssm_out":
                    for t in range(TT):
                        b = wait_full(dve, name, t)
                        taken(dve.tensor_tensor(mixT[:, 4:8, t * P:(t + 1) * P], slab(b), over_cols(vcol[:, 0, VA_SSMN:VA_SSMN + 4], P),
                                                ALU.mult), name, t)
                elif name.startswith("att_s"):
                    f = int(name[5])
                    n, heads, blocks = att_part(f)
                    nh, w = len(heads), len(blocks) * P
                    b = wait_full(dve, name, 0)
                    mask = cst[:, AMC, :] if len(blocks) == 1 else cst[:, AMP:AMC + 1, :].rearrange("p a n -> p (a n)")
                    s = sc[:, f % 2, :].rearrange("p (h n) -> p h n", h=nh)
                    step(dve.scalar_tensor_tensor(out=s, in0=slab(b, nh), scalar=float(HD) ** -0.5, in1=over_heads(mask, nh),
                                                  op0=ALU.mult, op1=ALU.add))
                    dve.sem_inc(bank_free[fill_of(name, 0)[0]], 1)
                    step(dve.tensor_reduce(ats[:, f, 0:nh], s, AX, ALU.max))
                    sink = prm[:, P_SINK + heads[0]:P_SINK + heads[0] + nh]
                    step(dve.tensor_tensor(ats[:, f, 0:nh], ats[:, f, 0:nh], sink, ALU.max))
                    step(dve.tensor_scalar(ats[:, f, 4:4 + nh], ats[:, f, 0:nh], -1.0, None, ALU.mult))
                    dve.tensor_tensor(ats[:, f, 8:8 + nh], ats[:, f, 4:4 + nh], sink, ALU.add).then_inc(v_aneg, 1)
                    dve.wait_ge(a_p, f + 1)
                    step(dve.tensor_tensor(ats[:, f, 12:12 + nh], ats[:, f, 12:12 + nh], ats[:, f, 8:8 + nh], ALU.add))
                    step(dve.reciprocal(ats[:, f, 12:12 + nh], ats[:, f, 12:12 + nh]))
                    b = wait_full(dve, name, 2)
                    taken(dve.tensor_tensor(yc[:, n, heads[0] * HD:(heads[0] + nh) * HD].rearrange("p (h n) -> p h n", h=nh),
                                            b[:, 0:nh * HD].rearrange("p (h n) -> p h n", h=nh),
                                            over_cols(ats[:, f, 12:12 + nh], HD), ALU.mult), name, 2)

            for pos in range(2 * KT):
                ada(STREAM[pos][1], STREAM[pos][2], pos)
            stage("mod0")
            stage("mod1")
            for n in range(2):
                wait_taken(dve, f"mod{n}", 0)
            for part in range(4):
                for k in range(4 * part, 4 * part + 4):
                    wait_taken(dve, "xT", k // 2)
                    ins = dve.tensor_scalar(xT[:, k, :], xT[:, k, :], modc[:, 1, k:k + 1], modc[:, 0, k:k + 1], ALU.mult, ALU.add)
                ins.then_inc(v_hmod, 1)
            for part in range(4):
                dve.wait_ge(a_hi, part + 1)
                ks = slice(4 * part, 4 * part + 4)
                lower(hlo[:, ks, :], xT[:, ks, :], hhi[:, ks, :]).then_inc(v_lo, 1)

            split_at(0)
            for g in range(W_GROUPS):
                if g + 1 < W_GROUPS:
                    split_at(g + 1)
                for name in with_moves(g):
                    stage(name)

            for i, kg in enumerate(WOUT_ORDER):
                dve.wait_ge(mix_hi, i + 1)
                ks = slice(4 * kg, 4 * kg + 4)
                lower(hlo[:, ks, :], mixT[:, ks, :], hhi[:, ks, :]).then_inc(mix_lo, 1)

            h1 = 2 * W_GROUPS
            n1 = 16 * (POS1 // RING + 1)
            with dve.Fori(0, 2) as it:
                for i in range(2 * GROUPS):
                    split(i % RING, NB, it * (4 * GROUPS) + (h1 + 2 * i), it * 32 + (n1 + 16 * (i // RING)))

            def gate_rows(j, n_in):
                dve.wait_ge(wpost_in, n_in)
                g = grow[:, j * NB:(j + 1) * NB]
                return dve.tensor_tensor(g, mx_of[j][:, :], g, ALU.mult)
            mx_of = {}
            for j in range(4):
                mx_of[j] = wait_full(dve, "gate_a", j)
                taken(gate_rows(j, 16), "gate_a", j)
            for j in range(4):
                wait_taken(dve, "gate_a", j)
            dve.wait_ge(a_yr, 1)
            dve.wait_ge(xr_in, 16)
            for t in range(TT):
                step(dve.scalar_tensor_tensor(out=y[:, t, :], in0=y[:, t, :], scalar=st[:, 48 + t:49 + t], in1=grow[:, :],
                                              op0=ALU.mult, op1=ALU.mult))
                dve.tensor_tensor(x1[:, t, :], x1[:, t, :], y[:, t, :], ALU.add).then_inc(v_x1, 1)
            for t in range(TT):
                dve.wait_ge(a_x1r, t + 1)
                dve.tensor_scalar(y[:, t, :], x1[:, t, :], st[:, 52 + t:53 + t], None, ALU.mult).then_inc(v_x1n, 1)
            for j in range(8):
                dve.wait_ge(h2_hi, j + 1)
                ks = slice(2 * j, 2 * j + 2)
                lower(hlo[:, ks, :], hful[:, j % 2], hhi[:, ks, :]).then_inc(h2_lo, 1)

            h2 = h1 + 8 * GROUPS
            n2 = n1 + 64
            dve.wait_ge(y_zero, 1)
            with dve.Fori(0, QUARTERS) as q:
                def down(c):
                    ci = NCH + 4 + c
                    dve.wait_ge(halves_done, q * (16 * GROUPS) + (h2 + 2 * GROUPS * (c + 1)))
                    d = y[:, :, (c - 4) * NB:(c - 3) * NB]
                    dve.tensor_tensor(d, d, gps[ci % 2][:, :, :], ALU.add).then_inc(gemm_free[ci % 2], 1)
                for c in range(8):
                    for g in range(GROUPS):
                        i = c * GROUPS + g
                        split(i % RING, NB, q * (16 * GROUPS) + (h2 + 2 * i), q * 128 + (n2 + 16 * (i // RING)))
                        if g == 0 and 1 <= c <= 4:
                            ci = NCH + 4 + c - 1
                            dve.wait_ge(gemm_free[ci % 2], q * 4 + (ci // 2 + 1))
                            r = rst[:, (c - 1) % 2]
                            dve.tensor_tensor(r, r, r, ALU.mult).then_inc(v_sq, 1)
                        if g == 0 and c >= 5:
                            down(c - 1)
                        if g == 2 and 1 <= c <= 4:
                            for i2 in range(2):
                                f = 2 * (c - 1) + i2
                                dve.wait_ge(act_hi, q * 8 + (f + 1))
                                ks = slice(2 * f, 2 * f + 2)
                                b = mlp_fill(f)[0]
                                lower(alo[:, ks, :], mx[b][:, :].rearrange("p (k n) -> p k n", k=2), ahi[:, ks, :])\
                                    .then_inc(bank_free[b], 1)
                down(7)

            for j in range(4):
                b, n = mlp_fill(8 * QUARTERS + j)
                dve.wait_ge(bank_full[b], n + 1)
                mx_of[j] = mx[b]
                step(gate_rows(j, 32))
            for t in range(TT):
                dve.wait_ge(a_yss, t + 1)
                step(dve.scalar_tensor_tensor(out=y[:, t, :], in0=y[:, t, :], scalar=st[:, 56 + t:57 + t], in1=grow[:, :],
                                              op0=ALU.mult, op1=ALU.mult))
                dve.tensor_tensor(y[:, t, :], x1[:, t, :], y[:, t, :], ALU.add).then_inc(v_out, 1)


_INS = ['x', 'c', 'positions', 'ada_w', 'ada_b', 'norm_pre_mix', 'norm_post_mix', 'norm_pre_mlp', 'norm_post_mlp',
        'w_in', 'w_out', 'gdn_conv_w', 'gdn_a_log', 'gdn_dt_bias', 'gdn_norm_w', 'ssm_conv_w', 'ssm_conv_b',
        'ssm_a_log', 'ssm_dt_bias', 'ssm_d', 'ssm_norm_w', 'attn_sinks', 'sc_conv_w', 'w_up', 'w_down']


def shape_constants():
    import numpy as np
    i = np.arange(P)
    r, c = i[:, None], i[None, :]
    same = (r // 64) == (c // 64)
    m = np.zeros((NCONST, P, P), np.float32)
    m[IDENT] = r == c
    m[UINC] = r <= c
    m[UINCB] = (r <= c) & same
    m[SGT] = r > c
    m[SGTB] = (r > c) & same
    m[CH0] = r < 64
    m[CH1] = r >= 64
    for lv in range(6):
        s = 2 ** lv
        m[LV0 + lv] = ((r // (2 * s)) == (c // (2 * s))) & ((r // s) % 2 == 1) & ((c // s) % 2 == 0)
    m[ONES] = 1
    m[AMP] = np.where(c > r, 0, -1e30)
    m[AMC] = np.where(c <= r, 0, -1e30)
    e = np.arange(0, HD, 2, dtype=np.float32) / np.float32(HD)
    return np.ascontiguousarray(m.transpose(1, 0, 2).reshape(P, NCONST * P)), np.power(np.float32(10000.0), -e).astype(np.float32)


def kernel(**inputs):
    import numpy as _np
    import concourse.bacc as _bacc
    from concourse import mybir as _mybir
    from concourse.bass_utils import run_bass_kernel_spmd as _run

    nc = _bacc.Bacc("TRN2", target_bir_lowering=False, num_devices=1)
    arrays = {name: _np.ascontiguousarray(inputs[name]) for name in _INS}
    arrays["consts"], arrays["inv_freq"] = shape_constants()
    aps = {}
    for name, value in arrays.items():
        aps[name] = nc.dram_tensor(name, value.shape, _mybir.dt.from_np(value.dtype), kind="ExternalInput").ap()
    aps["out"] = nc.dram_tensor("out", (1, SEQ, D), F32, kind="ExternalOutput").ap()
    build(nc, aps)
    r = _run(nc, [arrays], core_ids=[0])
    return r.results[0]["out"]
```

```python
from contextlib import ExitStack

import concourse.bass as bass
from concourse import mybir

F32 = mybir.dt.float32
F32R = mybir.dt.float32r
I32 = mybir.dt.int32
ALU = mybir.AluOpType
ACT = mybir.ActivationFunctionType
AX = mybir.AxisListType.X

P = 128
SEQ = 256
TT = SEQ // P
D = 2048
KT = D // P
GW = D // 4
H = 4
SH = 8
QH = 8
HD = 64
HIDDEN = 4 * D
QUARTERS = HIDDEN // D
IN_WIDTH = 5904
NB = 512
EPS = 1e-6
GK = 4
GROUPS = KT // GK
RING = 4
ADA_COLS = 2048

(IDENT, UINC, UINCB, SGT, SGTB, CH0, CH1, LV0, LV1, LV2, LV3, LV4, LV5, ONES, AMP, AMC) = range(16)
NCONST = 16
SUM_MASKS = (UINC, UINCB, SGT, SGTB, CH0, CH1)
CS_SSM, CS_GDN, REST_SSM, REST_GDN, TOT0, TOT1 = range(6)

P_DTB, P_ALOG, P_SD, P_SINK, P_FREQ, P_COLS = 0, 12, 24, 32, 40, 72

VA_C, VA_PRE_MIX, VA_PRE_MLP, VA_CONVB, VA_SC, VA_SSMN, VA_GDNN, VA_ROWS = 0, 16, 32, 48, 56, 68, 72, 73
VB_GDN, VB_SSM, VB_ROWS = 0, 48, 80

ROWS = [("c", 0, VA_C, KT), ("norm_pre_mix", 0, VA_PRE_MIX, KT), ("norm_pre_mlp", 0, VA_PRE_MLP, KT),
        ("ssm_conv_b", 0, VA_CONVB, 8), ("sc_conv_w", 0, VA_SC, 12), ("ssm_norm_w", 0, VA_SSMN, 4),
        ("gdn_norm_w", 0, VA_GDNN, 1), ("gdn_conv_w", 1, VB_GDN, 48), ("ssm_conv_w", 1, VB_SSM, 32)]
NVROWS = len(ROWS)
PRM = [("gdn_dt_bias", P_DTB, 4), ("ssm_dt_bias", P_DTB + 4, 8), ("gdn_a_log", P_ALOG, 4),
       ("ssm_a_log", P_ALOG + 4, 8), ("ssm_d", P_SD, 8), ("attn_sinks", P_SINK, 8), ("inv_freq", P_FREQ, 32)]
CHUNKS = [
    ("s1", 2048, 260), ("a1", 3592, 388), ("gq", 0, 512), ("gk", 512, 512), ("gv", 1024, 512),
    ("gz", 1536, 512), ("xbc0", 2568, 512), ("xbc1", 3080, 512), ("s2", 2308, 260), ("a2", 3980, 388),
    ("cc", 4880, 512), ("ch", 5392, 512), ("cb", 4368, 512),
]
CHUNK = {name: i for i, (name, _, _) in enumerate(CHUNKS)}
NCH = len(CHUNKS)
T_B, T_A, T_SZ, T_DT, T_AQ, T_AK, T_AV, T_GZ, T_COLS = 0, 4, 8, 520, 528, 1040, 1168, 1296, 1808
TM_AT = {"s1": 0, "s2": 260, "a1": 520, "a2": 908, "gz": T_GZ}
CONV = {"gq": (0, 0, 0), "gk": (1, 4, 4), "gv": (0, 8, 8), "xbc0": (1, 12, 0), "xbc1": (0, 16, 4)}
CONV_ORDER = ["gq", "gk", "gv", "xbc0", "xbc1"]
STAGED = ["gq", "gk", "gv", "xbc0", "xbc1", "cc", "cb"]
STG_OF = {"gq": 0, "gk": 1, "gv": 0, "xbc0": 1, "xbc1": 0, "cc": 1, "cb": 0}

SEGS = [0, 1, 3, 2, 4, 5]

W_GROUPS = NCH * GROUPS
SLOTS = 2 * W_GROUPS


TWO_PI = 6.283185307179586
PI2_A, PI2_B = 6.28125, 0.0019340515136718750
PI2_C = TWO_PI - PI2_A - PI2_B
PI_LOW = 3.1415925


def att_part(f):
    if f < 2:
        return 0, list(range(4 * f, 4 * f + 4)), [0]
    return 1, list(range(2 * (f - 2), 2 * (f - 2) + 2)), [0, 1]


def stream_plan():
    items = [("ada", a, k) for a in range(2) for k in range(KT)]
    rest = [("ada", a, k) for a in (2, 3) for k in range(KT)]
    for g in range(W_GROUPS):
        items.append(("w", g // GROUPS, g % GROUPS))
        if g < 20 or g % 2 == 0:
            if rest:
                items.append(rest.pop(0))
    assert not rest
    while len(items) % RING:
        items.append(("none", 0, 0))
    return items


STREAM = stream_plan()
POS_OF = {item: pos for pos, item in enumerate(STREAM)}
POS1 = len(STREAM)
assert POS1 % RING == 0


def schedule():
    s = {h: [] for h in range(SLOTS)}

    def at(h, *names):
        s[h].extend(names)
    at(16, "softplus")
    at(18, "sums")
    at(19, "decay0")
    at(20, "decay1")
    at(24, "conv_gq")
    at(26, "silu_gq")
    at(27, "tm_q")
    at(32, "conv_gk")
    at(34, "silu_gk")
    at(35, "tm_k")
    at(36, "mod2")
    at(37, "l2stat")
    at(38, "l2scale")
    at(40, "conv_gv")
    at(41, "kqT")
    at(42, "silu_gv", "kk")
    at(43, "qk")
    at(44, "tm_v")
    at(45, "kbg", "lv0")
    for lv in range(1, 6):
        at(44 + 2 * lv, f"invY{lv}")
        at(45 + 2 * lv, f"invX{lv}")
    at(50, "qdT", "silu_gz")
    at(56, "uw")
    at(57, "gdn_v0", "gdn_s0")
    at(58, "gdn_v1", "conv_xbc0")
    at(59, "gdn_s1", "gdn_o0")
    at(60, "gdn_v2")
    at(61, "gdn_s2", "silu_xbc0")
    at(62, "gdn_v3")
    at(63, "gdn_o1")
    at(64, "gdn_gate", "conv_xbc1")
    at(66, "gdn_out", "silu_xbc1")
    at(68, "ssm_tm")
    at(69, "ssm_cb")
    at(70, "ssm_e0", "ssm_s")
    at(71, "ssm_e1", "ssm_o")
    at(72, "ssm_y0", "ssm_e2", "silu_sz")
    at(73, "ssm_y1", "ssm_e3")
    at(74, "ssm_y2")
    at(75, "ssm_y3")
    at(76, "ssm_gate")
    at(78, "ssm_out")
    at(80, "rope")
    at(84, "att_T")
    at(86, "att_s0")
    at(87, "att_s1")
    for f in range(6):
        at(88 + 2 * f, f"att_t{f}")
        at(89 + 2 * f, f"att_v{f}")
        if f + 2 < 6:
            at(89 + 2 * f, f"att_s{f + 2}")
    at(96, "conv_cc")
    at(101, "att_out")
    at(103, "mul_cb")
    return [s[h] for h in range(SLOTS)]


SCHEDULE = schedule()


def with_moves(h):
    n = 2 * GROUPS
    return ([f"evac{h // n}"] if h % n == n - 1 else []) + SCHEDULE[h]

FILLS = {
    "conv_gq": 2, "conv_gk": 2, "conv_gv": 2, "conv_xbc0": 2, "conv_xbc1": 2, "conv_cc": 2, "mul_cb": 2,
    "mod0": 1, "mod1": 1, "mod2": 1, "mod4": 1, "sums": 1, "decay0": 2, "decay1": 2,
    "tm_q": 2, "tm_k": 2, "tm_v": 2, "kqT": 4, "kk": 2, "qk": 2, "lv0": 2,
    "invY1": 2, "invY2": 2, "invY3": 2, "invY4": 2, "invY5": 2,
    "invX1": 4, "invX2": 4, "invX3": 4, "invX4": 4, "invX5": 2,
    "qdT": 2, "uw": 4, "gdn_v0": 0, "gdn_v1": 2, "gdn_v2": 2, "gdn_v3": 2,
    "gdn_s0": 1, "gdn_s1": 1, "gdn_s2": 1, "gdn_o0": 1, "gdn_o1": 1, "gdn_out": 2,
    "ssm_tm": 3, "ssm_cb": 1, "ssm_s": 1, "ssm_o": 1, **{f"ssm_e{i}": 1 for i in range(4)},
    **{f"ssm_y{i}": 1 for i in range(4)}, "ssm_out": 2, "att_T": 4,
    **{f"att_{part}{f}": 1 for part in "stv" for f in range(6)}, "att_out": 2, "vecT": 1, "xT": 8, "gate_a": 4, "h2T": 8,
}
ORDER = ["vecT", "xT", "mod0", "mod1"] + [n for slot in SCHEDULE for n in slot] + ["gate_a", "mod4", "h2T"]


def fill_plan():
    at, n = {}, 0
    for name in ORDER:
        for i in range(FILLS.get(name, 0)):
            at[name, i] = (n % 4, n // 4)
            n += 1
    return at, n


FILL_AT, NFILLS = fill_plan()


MLP_ITEMS = []
for c_ in range(8):
    for g_ in range(GROUPS):
        MLP_ITEMS.append(("w", c_ * GROUPS + g_))
        if c_ < 4 and g_ == 1:
            MLP_ITEMS.append(("ada", c_))
assert len(MLP_ITEMS) % RING == 0
MLP_POS = {item: i for i, item in enumerate(MLP_ITEMS)}


def mlp_back(i):
    kind, n = MLP_ITEMS[(i - RING) % len(MLP_ITEMS)]
    return kind, n, int(i < RING)


def mlp_fill(f):
    return (NFILLS + f) % 4, (NFILLS + f) // 4


def fill_of(name, i):
    return FILL_AT[name, i]


def build(nc, a):
    with ExitStack() as ctx:
        cursor = [nc.sbuf_base + (-nc.sbuf_base) % 64]

        def place(name, shape, dt, offset):
            return nc.alloc_sbuf_tensor_at(name, shape, dt, offset=offset)

        def sb(name, shape, dt=F32):
            size = 4
            for n in shape[1:]:
                size *= n
            t = place(name, shape, dt, cursor[0])
            cursor[0] += size + (-size) % 64
            return t

        def sem(name):
            return ctx.enter_context(nc.semaphore(name))

        cst = sb("cst", [P, NCONST, P])
        vcol = sb("vcol", [P, 2, P])
        prm = sb("prm", [P, P_COLS])
        epsc = sb("epsc", [P, 2])
        cact = sb("cact", [P, KT])
        modc = sb("modc", [P, 4, KT])
        st = sb("st", [P, 64])
        yss = sb("yss", [P, TT, 4])
        trig = sb("trig", [P, 2, TT, 32])
        raw = sb("raw", [P, RING, GK * NB])
        whi = sb("whi", [P, 2, 2, NB], F32R)
        wlo = sb("wlo", [P, 2, 2, NB], F32R)
        hhi = sb("hhi", [P, KT, SEQ], F32R)
        hlo = sb("hlo", [P, KT, SEQ], F32R)
        acc = sb("acc", [P, 2, ADA_COLS])
        base = cursor[0]

        def zone(start):
            at = [start]

            def take(name, shape, dt=F32):
                size = 4
                for n in shape[1:]:
                    size *= n
                t = place(name, shape, dt, at[0])
                at[0] += size + (-size) % 64
                assert at[0] <= nc.sbuf_usable_end, (name, at[0])
                return t
            take.at = at
            return take
        z0 = zone(base)
        x0 = z0("x0", [P, TT, D])
        xn0 = z0("xn0", [P, TT, D])
        xT = z0("xT", [P, KT, SEQ])
        vrow = z0("vrow", [P, 2, P])
        posi = z0("posi", [P, TT], I32)
        posf = z0("posf", [P, TT])
        ang = z0("ang", [P, 4, TT, 32])
        angi = z0("angi", [P, TT, 32], I32)
        junk0 = z0("junk0", [P, D])

        z1 = zone(base)
        mixT = z1("mixT", [P, KT, SEQ])
        stg = z1("stg", [P, 2, TT, NB])
        ptm = z1("ptm", [P, TT, T_COLS])
        cvo = z1("cvo", [P, 20, SEQ])
        dec = z1("dec", [P, 10, TT, 12])
        sums = z1("sums", [P, len(SUM_MASKS), TT, 12])
        shared = z1.at[0]
        tm = z1("tm", [P, 3, TT, H, P])
        Dm = z1("Dm", [P, TT, H, P])
        Dt = z1("Dt", [P, TT, H, P])
        Cm = z1("Cm", [P, TT, H, P])
        Xm = z1("Xm", [P, TT, H, P])
        Xt = z1("Xt", [P, TT, H, P])
        Ym = z1("Ym", [P, TT, H, P])
        Sm = z1("Sm", [P, H, P])
        qnT = cvo[:, 0:4, :].rearrange("p j (t n) -> p (j t n)", t=TT).rearrange("p (t h n) -> p t h n", t=TT, h=H)
        knT = cvo[:, 4:8, :].rearrange("p j (t n) -> p (j t n)", t=TT).rearrange("p (t h n) -> p t h n", t=TT, h=H)
        kbg = cvo[:, 8:12, :].rearrange("p j (t n) -> p (j t n)", t=TT).rearrange("p (t h n) -> p t h n", t=TT, h=H)
        qdT = qnT
        U, WT, O, VZ = Xm, Dm, Ym, Cm

        z2 = zone(shared)
        xs = z2("xs", [P, TT, GW])
        xdt = z2("xdt", [P, TT, SH, HD])
        xdd = z2("xdd", [P, SH, HD])
        btm = z2("btm", [P, 2, P])
        CBm = z2("CBm", [P, 4, P])
        M1s = z2("M1s", [P, 2, 4, P])
        Es = z2("Es", [P, 2, 4, P])
        stt_ = z2("stt_", [P, 2, SEQ])
        yb = z2("yb", [P, TT, GW])
        ytmp = z2("ytmp", [P, TT, GW])
        assert z2.at[0] - shared <= z1.at[0] - shared
        z3 = zone(shared)
        rq = z3("rq", [P, TT, 10, HD])
        rtmp = z3("rtmp", [P, 2, TT, 10, 32])
        kz = z3("kz", [P, TT, 2, 2, P])
        qT2 = z3("qT2", [P, TT, 4, P])
        kzT = z3("kzT", [P, 4, SEQ])
        sc = z3("sc", [P, 2, NB])
        PT = z3("PT", [P, 2, 4, P])
        ats = z3("ats", [P, 6, 16])
        yc = z3("yc", [P, TT, GW])

        z4 = zone(base)
        x1 = z4("x1", [P, TT, D])
        y = z4("y", [P, TT, D])
        grow = z4("grow", [P, D])
        hful = z4("hful", [P, 2, 2, SEQ])
        rst = z4("rst", [P, 2, TT, NB])
        ahi = z4("ahi", [P, KT, SEQ], F32R)
        alo = z4("alo", [P, KT, SEQ], F32R)

        gps = [ctx.enter_context(nc.psum_tensor(f"gps{i}", [P, TT, NB], F32)) for i in range(2)]
        mx = [ctx.enter_context(nc.psum_tensor(f"mx{i}", [P, NB], F32)) for i in range(4)]

        raw_in = [sem(f"raw_in{i}") for i in range(RING)]
        slot_claimed = sem("slot_claimed")
        ada_used = sem("ada_used")
        hi_ready = sem("hi_ready")
        lo_ready = sem("lo_ready")
        halves_done = sem("halves_done")
        gemm_free = [sem(f"gemm_free{i}") for i in range(2)]
        bank_full = [sem(f"bank_full{i}") for i in range(4)]
        bank_free = [sem(f"bank_free{i}") for i in range(4)]
        cst_in, vrow_in, prm_in, x_in, pos_in = (sem(n) for n in ("cst_in", "vrow_in", "prm_in", "x_in", "pos_in"))
        rows_zero = sem("rows_zero")
        acc_zero = sem("acc_zero")
        acc_seed = [sem(f"acc_seed{i}") for i in range(2)]
        acc_full = sem("acc_full")
        vec_step = sem("vec_step")
        act_step = sem("act_step")
        pool_step = sem("pool_step")
        v_eps = sem("v_eps")
        a_ss, a_rstd, v_xn, a_cact = (sem(n) for n in ("a_ss", "a_rstd", "v_xn", "a_cact"))
        a_hi, v_hmod, v_lo = sem("a_hi"), sem("v_hmod"), sem("v_lo")
        a_silu = sem("a_silu")
        v_taps = sem("v_taps")
        a_tap = sem("a_tap")
        v_dec, a_dec = sem("v_dec"), sem("a_dec")
        p_m1 = sem("p_m1")
        p_dmask = sem("p_dmask")
        v_ss, a_rn, v_qkn, p_kbg, p_qd, v_rn = (sem(n) for n in ("v_ss", "a_rn", "v_qkn", "p_kbg", "p_qd", "v_rn"))
        p_C, v_X, p_vz, v_vz = (sem(n) for n in ("p_C", "v_X", "p_vz", "v_vz"))
        v_oss, a_orn, v_og, a_gz = (sem(n) for n in ("v_oss", "a_orn", "v_og", "a_gz"))
        v_xdt, p_ms1, v_es, v_yss, a_yrn, v_yg, a_sz = (
            sem(n) for n in ("v_xdt", "p_ms1", "v_es", "v_yss", "a_yrn", "v_yg", "a_sz"))
        p_rope, v_sc, a_p, v_yc, v_aneg, a_es = (sem(n) for n in ("p_rope", "v_sc", "a_p", "v_yc", "v_aneg", "a_es"))
        v_ang, a_trig = sem("v_ang"), sem("a_trig")
        mix_hi, mix_lo = sem("mix_hi"), sem("mix_lo")
        xr_in, wpost_in = sem("xr_in"), sem("wpost_in")
        a_ysq, v_ysum = sem("a_ysq"), sem("v_ysum")
        a_yss, a_yr, v_x1, a_x1r, v_x1n, a_h2, h2_hi, h2_lo = (
            sem(n) for n in ("a_yss", "a_yr", "v_x1", "a_x1r", "v_x1n", "a_h2", "h2_hi", "h2_lo"))
        y_zero = sem("y_zero")
        a_relu, v_sq, act_hi = sem("a_relu"), sem("v_sq"), sem("act_hi")
        v_out, out_done = sem("v_out"), sem("out_done")

        block = ctx.enter_context(nc.Block())

        def tap_col(c, tap, j):
            row = (VB_GDN + tap * 12 if c[0] == "g" else VB_SSM + tap * 8) + CONV[c][2] + j
            return vcol[:, 1, row:row + 1]

        def c_(i):
            return cst[:, i, :]

        def over_heads(ap, n=H):
            return ap.unsqueeze(1).broadcast_to([P, n, ap.shape[1]])

        def over_cols(ap, n):
            return ap.unsqueeze(2).broadcast_to([P, ap.shape[1], n])

        def wait_chunk_taken(eng, ci):
            eng.wait_ge(gemm_free[ci % 2], ci // 2 + 1)

        def wait_full(eng, name, i):
            b, n = fill_of(name, i)
            eng.wait_ge(bank_full[b], n + 1)
            return mx[b]

        def wait_taken(eng, name, i):
            b, n = fill_of(name, i)
            eng.wait_ge(bank_free[b], n + 1)

        def taken(ins, name, i):
            ins.then_inc(bank_free[fill_of(name, i)[0]], 1)

        def slab(b, n=4):
            return b[:, :].rearrange("p (h n) -> p h n", h=n)

        ada_v = a["ada_w"][0].rearrange("(k p) n -> k p n", p=P)
        adab_v = a["ada_b"]
        win_v = a["w_in"][0].rearrange("(g k p) n -> g p k n", k=GK, p=P)
        wout_v = a["w_out"][0].rearrange("(g k p) n -> g p k n", k=GK, p=P)
        wup_v = a["w_up"][0].rearrange("(g k p) n -> g p k n", k=GK, p=P)
        wdn_v = a["w_down"][0].rearrange("(q g k p) n -> q g p k n", q=QUARTERS, k=GK, p=P)
        x_v = a["x"][0].rearrange("(t p) n -> p t n", p=P)
        out_v = a["out"][0].rearrange("(t p) n -> p t n", p=P)
        WOUT_ORDER = (3, 0, 1, 2)

        @block.sync
        def _(sp):
            sp.dma_start(x0[:, :, :], x_v).then_inc(x_in, 16)
            sp.dma_start(cst[:, :, :], a["consts"].rearrange("p (c n) -> p c n", n=P)).then_inc(cst_in, 16)

            def slot(i):
                return raw[:, i, :].rearrange("p (k n) -> p k n", k=GK)

            for pos, (kind, i, j) in enumerate(STREAM):
                if kind == "ada" and j == 0:
                    sp.wait_ge(acc_zero, i + 1)
                    s0 = SEGS[i] * ADA_COLS
                    sp.dma_start(acc[0:1, i % 2, :], adab_v[:, s0:s0 + ADA_COLS]).then_inc(acc_seed[i % 2], 16)
                if pos >= RING:
                    last = STREAM[pos - RING]
                    if kind == "none" or last[0] == "none":
                        continue
                    if last[0] == "ada":
                        sp.wait_ge(ada_used, last[1] * KT + last[2] + 1)
                    else:
                        sp.wait_ge(lo_ready, 2 * (last[1] * GROUPS + last[2]) + 2)
                if kind == "ada":
                    s0 = SEGS[i] * ADA_COLS
                    sp.dma_start(raw[:, pos % RING, :], ada_v[j, :, s0:s0 + ADA_COLS]).then_inc(raw_in[pos % RING], 16)
                else:
                    _, c0, w = CHUNKS[i]
                    sp.dma_start(slot(pos % RING)[:, :, 0:w], win_v[j, :, :, c0:c0 + w]).then_inc(raw_in[pos % RING], 16)
            h1 = 2 * W_GROUPS
            sp.wait_ge(ada_used, 4 * KT)
            sp.wait_ge(lo_ready, h1)

            def seed(n):
                sp.wait_ge(acc_zero, n + 1)
                s0 = SEGS[n] * ADA_COLS
                sp.dma_start(acc[0:1, n % 2, :], adab_v[:, s0:s0 + ADA_COLS]).then_inc(acc_seed[n % 2], 16)

            def slot_free(i, h, ada_before, turn, per_turn):
                if h is not None:
                    split_before = sp.snap(turn * per_turn + h)
                    sp.wait_ge(lo_ready, split_before)
                    sp.sem_inc(slot_claimed, 1)
                if ada_before is not None:
                    used_before = sp.snap(turn * ada_before[1] + ada_before[0])
                    sp.wait_ge(ada_used, used_before)
                    sp.sem_inc(slot_claimed, 1)

            seed(4)
            s4, s5 = SEGS[4] * ADA_COLS, SEGS[5] * ADA_COLS
            with sp.Fori(0, 2) as it:
                for n in range(2 * GROUPS):
                    c, g = divmod(n, GROUPS)
                    slot_free(2 * n, h1 + 2 * (n - 1), None, it, 4 * GROUPS)
                    sp.dma_start(slot((2 * n) % RING), wout_v[WOUT_ORDER[g], :, :, bass.ds(it * (2 * NB) + c * NB, NB)])\
                        .then_inc(raw_in[(2 * n) % RING], 16)
                    slot_free(2 * n + 1, None, (4 * KT + n - 1, 2 * GROUPS), it, 0)
                    sp.dma_start(raw[:, (2 * n + 1) % RING, :],
                                 ada_v[bass.ds(it * (2 * GROUPS) + n, 1), :, s4:s4 + ADA_COLS].rearrange("o p n -> p (o n)"))\
                        .then_inc(raw_in[(2 * n + 1) % RING], 16)
            h2 = h1 + 8 * GROUPS
            seed(5)
            sp.wait_ge(lo_ready, h2)
            sp.wait_ge(ada_used, 5 * KT)
            with sp.Fori(0, QUARTERS) as q:
                for i, (kind, n) in enumerate(MLP_ITEMS):
                    back_kind, back, turns_back = mlp_back(i)
                    if back_kind == "w":
                        slot_free(i, h2 + 2 * (back + 1) - turns_back * 16 * GROUPS, None, q, 16 * GROUPS)
                    else:
                        slot_free(i, None, (5 * KT + back + 1 - turns_back * 4, 4), q, 0)
                    if kind == "w":
                        c, g = divmod(n, GROUPS)
                        if c < 4:
                            src = wup_v[g, :, :, bass.ds(q * D + c * NB, NB)]
                        else:
                            src = wdn_v[bass.ds(q, 1), g, :, :, (c - 4) * NB:(c - 3) * NB]\
                                .rearrange("o p k n -> p (o k) n")
                        sp.dma_start(slot(i % RING), src).then_inc(raw_in[i % RING], 16)
                    else:
                        sp.dma_start(raw[:, i % RING, :],
                                     ada_v[bass.ds(q * 4 + n, 1), :, s5:s5 + ADA_COLS].rearrange("o p n -> p (o n)"))\
                            .then_inc(raw_in[i % RING], 16)
            for m in range(TT):
                sp.wait_ge(v_out, m + 1)
                sp.dma_start(out_v[:, m, :], y[:, m, :]).then_inc(out_done, 16)
            sp.wait_ge(out_done, 16 * TT)

        @block.tensor
        def _(pe):
            def fill(name, i, *extra):
                b, n = fill_of(name, i)
                if n:
                    pe.wait_ge(bank_free[b], n)
                return mx[b]

            def full(ins, name, i):
                ins.then_inc(bank_full[fill_of(name, i)[0]], 1)

            def half(psum, lhs_hi, lhs_lo, kg, g, hh, w, h):
                pe.wait_ge(lo_ready, h + 1)
                for kk in range(2):
                    k = kg * GK + hh * 2 + kk
                    for m in range(TT):
                        o = psum[:, m, 0:w]
                        xh = lhs_hi[:, k, m * P:(m + 1) * P]
                        xl = lhs_lo[:, k, m * P:(m + 1) * P]
                        first = g == 0 and hh == 0 and kk == 0
                        final = g == GROUPS - 1 and hh == 1 and kk == 1
                        pe.matmul(o, xh, whi[:, hh, kk, 0:w], start=first, stop=False)
                        pe.matmul(o, xh, wlo[:, hh, kk, 0:w], start=False, stop=False)
                        mm = pe.matmul(o, xl, whi[:, hh, kk, 0:w], start=False, stop=final)
                mm.then_inc(halves_done, 1)

            def stage(name):
                if name.startswith("conv_") or name == "mul_cb":
                    c = name.split("_")[1]
                    if c == "cc":
                        wait_chunk_taken(pe, CHUNK["ch"])
                        s = stg[:, 1]
                    else:
                        wait_chunk_taken(pe, CHUNK[c])
                        s = stg[:, STG_OF[c]]
                    for i in range(2):
                        b = fill(name, i)
                        for j in range(2):
                            for t in range(TT):
                                mm = pe.transpose(b[:, j * SEQ + t * P:j * SEQ + (t + 1) * P],
                                                  s[:, t, (2 * i + j) * P:(2 * i + j + 1) * P], c_(IDENT))
                        full(mm, name, i)
                elif name.startswith("mod"):
                    n = int(name[3])
                    pe.wait_ge(acc_full, n + 1)
                    b = fill(name, 0)
                    for k in range(KT):
                        mm = pe.matmul(b[:, k:k + 1], acc[:, n % 2, k * P:(k + 1) * P], cst[:, ONES, 0:1], start=True, stop=True)
                    full(mm, name, 0)
                elif name == "sums":
                    pe.wait_ge(v_dec, 3)
                    b = fill(name, 0)
                    for i, m in enumerate(SUM_MASKS):
                        mm = pe.matmul(b[:, i * 24:(i + 1) * 24], c_(m), dec[:, 9, :, :].rearrange("p t n -> p (t n)"),
                                       start=True, stop=True)
                    full(mm, name, 0)
                elif name.startswith("decay"):
                    t = int(name[5])
                    pe.wait_ge(p_m1, t + 1)
                    b = fill(name, 0)
                    mm = pe.matmul(b[:, :], c_(UINC), Cm[:, t].rearrange("p h n -> p (h n)"), start=True, stop=True)
                    full(mm, name, 0)
                    b = fill(name, 1)
                    for h in range(H):
                        mm = pe.matmul(b[:, h * P:(h + 1) * P], Cm[:, t, h, :], c_(UINC), start=True, stop=True)
                    full(mm, name, 1)
                elif name.startswith("tm_"):
                    w = "qkv".index(name[3])
                    pe.wait_ge(a_silu, w + 1)
                    for t in range(TT):
                        b = fill(name, t)
                        for h in range(H):
                            mm = pe.transpose(b[:, h * P:(h + 1) * P], cvo[:, w * 4 + h, t * P:(t + 1) * P], c_(IDENT))
                        full(mm, name, t)
                elif name == "kqT":
                    pe.wait_ge(v_qkn, 2)
                    for w in range(2):
                        for t in range(TT):
                            b = fill(name, w * 2 + t)
                            for h in range(H):
                                mm = pe.transpose(b[:, h * P:(h + 1) * P], tm[:, 1 - w, t, h, :], c_(IDENT))
                            full(mm, name, w * 2 + t)
                elif name in ("kk", "qk"):
                    for t in range(TT):
                        wait_taken(pe, "kqT", t)
                        wait_taken(pe, "kqT", 2 + t)
                        b = fill(name, t)
                        for h in range(H):
                            r = knT if name == "kk" else qnT
                            mm = pe.matmul(b[:, h * P:(h + 1) * P], knT[:, t, h, :], r[:, t, h, :], start=True, stop=True)
                        full(mm, name, t)
                elif name == "lv0":
                    for t in range(TT):
                        pe.wait_ge(p_C, t + 1)
                        b = fill(name, t)
                        for h in range(H):
                            mm = pe.matmul(b[:, h * P:(h + 1) * P], Cm[:, t, h, :], c_(IDENT), start=True, stop=True)
                        full(mm, name, t)
                elif name.startswith("invY"):
                    lv = int(name[4])
                    for t in range(TT):
                        pe.wait_ge(p_C, 2 * lv + t + 1)
                        pe.wait_ge(v_X, 2 * (lv - 1) + t + 1)
                        b = fill(name, t)
                        for h in range(H):
                            mm = pe.matmul(b[:, h * P:(h + 1) * P], Cm[:, t, h, :], Xt[:, t, h, :], start=True, stop=True)
                        full(mm, name, t)
                elif name.startswith("invX"):
                    lv = int(name[4])
                    for t in range(TT):
                        wait_taken(pe, f"invY{lv}", t)
                        b = fill(name, t)
                        for h in range(H):
                            mm = pe.matmul(b[:, h * P:(h + 1) * P], Xm[:, t, h, :], Ym[:, t, h, :], start=True, stop=True)
                        full(mm, name, t)
                    if lv < 5:
                        for t in range(TT):
                            b = fill(name, 2 + t)
                            for h in range(H):
                                mm = pe.matmul(b[:, h * P:(h + 1) * P], Ym[:, t, h, :], Xm[:, t, h, :], start=True, stop=True)
                            full(mm, name, 2 + t)
                elif name == "qdT":
                    pe.wait_ge(p_qd, 1)
                    for t in range(TT):
                        b = fill(name, t)
                        for h in range(H):
                            mm = pe.transpose(b[:, h * P:(h + 1) * P], tm[:, 0, t, h, :], c_(IDENT))
                        full(mm, name, t)
                elif name == "uw":
                    pe.wait_ge(p_kbg, 1)
                    for t in range(TT):
                        pe.wait_ge(v_X, 2 * 5 + t + 1)
                        wait_taken(pe, "tm_v", t)
                        b = fill(name, 2 * t)
                        for h in range(H):
                            mm = pe.matmul(b[:, h * P:(h + 1) * P], Xt[:, t, h, :], tm[:, 2, t, h, :], start=True, stop=True)
                        full(mm, name, 2 * t)
                        b = fill(name, 2 * t + 1)
                        for h in range(H):
                            mm = pe.matmul(b[:, h * P:(h + 1) * P], kbg[:, t, h, :], Xt[:, t, h, :], start=True, stop=True)
                        full(mm, name, 2 * t + 1)
                elif name.startswith("gdn_v"):
                    c = int(name[5])
                    if c:
                        t = c // 2
                        wait_taken(pe, f"gdn_s{c - 1}", 0)
                        wait_taken(pe, "uw", 2 * t + 1)
                        wait_taken(pe, "qdT", t)
                        for i, lhs in enumerate((WT, qdT)):
                            b = fill(name, i)
                            for h in range(H):
                                mm = pe.matmul(b[:, h * P:(h + 1) * P], lhs[:, t, h, :], Sm[:, h, :], start=True, stop=True)
                            full(mm, name, i)
                elif name.startswith("gdn_s"):
                    c = int(name[5])
                    pe.wait_ge(v_vz, c + 1)
                    b = fill(name, 0)
                    for h in range(H):
                        mm = pe.matmul(b[:, h * P:(h + 1) * P], tm[:, 1, c // 2, h, :], VZ[:, c % 2, h, :], start=True, stop=True)
                    full(mm, name, 0)
                elif name in ("gdn_o0", "gdn_o1"):
                    t = int(name[5])
                    pe.wait_ge(v_vz, 2 * t + 2)
                    b = fill(name, 0)
                    for h in range(H):
                        for cc in range(2):
                            mm = pe.matmul(b[:, h * P:(h + 1) * P], Dt[:, t, h, :], VZ[:, cc, h, :], start=(cc == 0), stop=(cc == 1))
                    full(mm, name, 0)
                elif name == "gdn_out":
                    pe.wait_ge(v_og, 1)
                    for t in range(TT):
                        b = fill(name, t)
                        for h in range(H):
                            mm = pe.transpose(b[:, h * P:(h + 1) * P], O[:, t, h, :], c_(IDENT))
                        full(mm, name, t)
                elif name == "ssm_tm":
                    pe.wait_ge(a_silu, 5)
                    for t in range(TT):
                        b = fill(name, t)
                        for j in range(4):
                            mm = pe.transpose(b[:, j * P:(j + 1) * P], cvo[:, 12 + j, t * P:(t + 1) * P], c_(IDENT))
                        full(mm, name, t)
                    b = fill(name, 2)
                    for g in range(2):
                        mm = pe.transpose(b[:, g * P:(g + 1) * P], cvo[:, 16 + g, 0:P], c_(IDENT))
                    full(mm, name, 2)
                elif name == "ssm_cb":
                    b = fill(name, 0)
                    for t in range(TT):
                        for g in range(2):
                            mm = pe.matmul(b[:, (t * 2 + g) * P:(t * 2 + g + 1) * P], cvo[:, 16 + g, t * P:(t + 1) * P],
                                           cvo[:, 18 + g, t * P:(t + 1) * P], start=True, stop=True)
                    full(mm, name, 0)
                elif name == "ssm_s":
                    pe.wait_ge(v_xdt, 1)
                    wait_taken(pe, "ssm_tm", 2)
                    b = fill(name, 0)
                    for g in range(2):
                        mm = pe.matmul(b[:, g * SEQ:(g + 1) * SEQ], btm[:, g, :],
                                       xdd[:, 4 * g:4 * g + 4, :].rearrange("p h n -> p (h n)"), start=True, stop=True)
                    full(mm, name, 0)
                elif name == "ssm_o":
                    wait_taken(pe, "ssm_s", 0)
                    b = fill(name, 0)
                    for g in range(2):
                        mm = pe.matmul(b[:, g * SEQ:(g + 1) * SEQ], cvo[:, 18 + g, P:SEQ], stt_[:, g, :], start=True, stop=True)
                    full(mm, name, 0)
                elif name.startswith("ssm_e"):
                    i = int(name[5])
                    t, g = i // 2, i % 2
                    pe.wait_ge(p_ms1, i + 1)
                    b = fill(name, 0)
                    for h in range(4):
                        mm = pe.matmul(b[:, h * P:(h + 1) * P], M1s[:, i % 2, h, :], c_(UINC), start=True, stop=True)
                    full(mm, name, 0)
                elif name.startswith("ssm_y"):
                    i = int(name[5])
                    t, g = i // 2, i % 2
                    pe.wait_ge(v_es, i + 1)
                    b = fill(name, 0)
                    for h in range(4):
                        mm = pe.matmul(b[:, h * HD:(h + 1) * HD], Es[:, i % 2, h, :], xdt[:, t, g * 4 + h, :], start=True, stop=True)
                    full(mm, name, 0)
                elif name == "ssm_out":
                    pe.wait_ge(v_yg, 1)
                    for t in range(TT):
                        b = fill(name, t)
                        for j in range(4):
                            mm = pe.transpose(b[:, j * P:(j + 1) * P], yb[:, t, j * P:(j + 1) * P], c_(IDENT))
                        full(mm, name, t)
                elif name == "att_T":
                    pe.wait_ge(p_rope, 1)
                    for t in range(TT):
                        b = fill(name, t)
                        for j in range(4):
                            mm = pe.transpose(b[:, j * P:(j + 1) * P], rq[:, t, 2 * j:2 * j + 2, :].rearrange("p h n -> p (h n)"), c_(IDENT))
                        full(mm, name, t)
                    for t in range(TT):
                        b = fill(name, 2 + t)
                        for gz in range(4):
                            mm = pe.transpose(b[:, gz * P:(gz + 1) * P], kz[:, t, gz // 2, gz % 2, :], c_(IDENT))
                        full(mm, name, 2 + t)
                elif name.startswith("att_s"):
                    f = int(name[5])
                    n, heads, blocks = att_part(f)
                    if f == 0:
                        for i in range(4):
                            wait_taken(pe, "att_T", i)
                    w = len(blocks) * P
                    b = fill(name, 0)
                    for i, h in enumerate(heads):
                        g, z = h // 4, h % 2
                        mm = pe.matmul(b[:, i * w:(i + 1) * w], qT2[:, n, h // 2, :], kzT[:, g * 2 + z, blocks[0] * P:blocks[0] * P + w],
                                       start=True, stop=True)
                    full(mm, name, 0)
                elif name.startswith("att_t"):
                    f = int(name[5])
                    pe.wait_ge(a_p, f + 1)
                    b = fill(name, 0)
                    for i in range(4):
                        mm = pe.transpose(b[:, i * P:(i + 1) * P], sc[:, f % 2, i * P:(i + 1) * P], c_(IDENT))
                    full(mm, name, 0)
                elif name.startswith("att_v"):
                    f = int(name[5])
                    n, heads, blocks = att_part(f)
                    wait_taken(pe, f"att_t{f}", 0)
                    b = fill(name, 0)
                    for i, h in enumerate(heads):
                        for j, kb in enumerate(blocks):
                            mm = pe.matmul(b[:, i * HD:(i + 1) * HD], PT[:, f % 2, i * len(blocks) + j, :],
                                           ptm[:, kb, T_AV + (h // 4) * HD:T_AV + (h // 4 + 1) * HD],
                                           start=(j == 0), stop=(j == len(blocks) - 1))
                    full(mm, name, 0)
                elif name == "att_out":
                    wait_taken(pe, "att_v5", 0)
                    for t in range(TT):
                        b = fill(name, t)
                        for j in range(4):
                            mm = pe.transpose(b[:, j * P:(j + 1) * P], yc[:, t, j * P:(j + 1) * P], c_(IDENT))
                        full(mm, name, t)

            pe.wait_ge(cst_in, 16)
            pe.wait_ge(rows_zero, 1)
            pe.wait_ge(vrow_in, 16 * NVROWS)
            b = fill("vecT", 0)
            for i in range(2):
                mm = pe.transpose(b[:, i * P:(i + 1) * P], vrow[:, i, :], c_(IDENT))
            full(mm, "vecT", 0)
            pe.wait_ge(v_xn, TT)
            for j in range(8):
                b = fill("xT", j)
                for kk in range(2):
                    for t in range(TT):
                        k = 2 * j + kk
                        mm = pe.transpose(b[:, kk * SEQ + t * P:kk * SEQ + (t + 1) * P], xn0[:, t, k * P:(k + 1) * P], c_(IDENT))
                full(mm, "xT", j)
            stage("mod0")
            stage("mod1")

            for h in range(SLOTS):
                g, hh = divmod(h, 2)
                ci, gi = divmod(g, GROUPS)
                if gi == 0 and hh == 0 and ci >= 2:
                    pe.wait_ge(gemm_free[ci % 2], ci // 2)
                if ci == 0 and hh == 0:
                    pe.wait_ge(v_lo, gi + 1)
                half(gps[ci % 2], hhi, hlo, gi, gi, hh, CHUNKS[ci][2], h)
                for name in SCHEDULE[h]:
                    stage(name)

            pe.wait_ge(acc_full, 4)
            for j in range(4):
                b = fill("gate_a", j)
                mm = pe.matmul(b[:, :], c_(ONES), acc[:, 1, j * NB:(j + 1) * NB], start=True, stop=True)
                full(mm, "gate_a", j)

            h1 = 2 * W_GROUPS
            with pe.Fori(0, 2) as it:
                for c in range(2):
                    ci = NCH + c
                    pe.wait_ge(gemm_free[ci % 2], it + ci // 2)
                    for g in range(GROUPS):
                        if c == 0:
                            pe.wait_ge(mix_lo, g + 1)
                        for hh in range(2):
                            half(gps[ci % 2], hhi, hlo, WOUT_ORDER[g], g, hh, NB, it * (4 * GROUPS) + (h1 + (c * GROUPS + g) * 2 + hh))

            stage("mod4")
            for j in range(8):
                if j % 4 == 0:
                    pe.wait_ge(v_x1n, TT)
                b = fill("h2T", j)
                for kk in range(2):
                    for t in range(TT):
                        k = 2 * j + kk
                        mm = pe.transpose(b[:, kk * SEQ + t * P:kk * SEQ + (t + 1) * P], y[:, t, k * P:(k + 1) * P], c_(IDENT))
                full(mm, "h2T", j)

            h2 = h1 + 8 * GROUPS
            with pe.Fori(0, QUARTERS) as q:
                def turn(c):
                    pe.wait_ge(v_sq, q * 4 + (c + 1))
                    for i in range(2):
                        f = 2 * c + i
                        bank, n = mlp_fill(f)
                        b = mx[bank]
                        pe.wait_ge(bank_free[bank], q * 2 + n)
                        for j in range(2):
                            for t in range(TT):
                                mm = pe.transpose(b[:, j * SEQ + t * P:j * SEQ + (t + 1) * P],
                                                  rst[:, c % 2, t, (2 * i + j) * P:(2 * i + j + 1) * P], c_(IDENT))
                        mm.then_inc(bank_full[bank], 1)
                for c in range(8):
                    ci = NCH + 4 + c
                    pe.wait_ge(gemm_free[ci % 2], q * 4 + ci // 2)
                    for g in range(GROUPS):
                        if c == 0:
                            pe.wait_ge(h2_lo, 2 * g + 2)
                        if c == 4 and g in (0, 3):
                            b, n = mlp_fill(5 if g == 0 else 7)
                            pe.wait_ge(bank_free[b], q * 2 + (n + 1))
                        for hh in range(2):
                            half(gps[ci % 2], hhi if c < 4 else ahi, hlo if c < 4 else alo, g, g, hh, NB,
                                 q * (16 * GROUPS) + (h2 + (c * GROUPS + g) * 2 + hh))
                        if g == 1 and 1 <= c <= 4:
                            turn(c - 1)

            pe.wait_ge(acc_full, 6)
            for j in range(4):
                b, n = mlp_fill(8 * QUARTERS + j)
                pe.wait_ge(bank_free[b], n)
                pe.matmul(mx[b][:, :], c_(ONES), acc[:, 1, j * NB:(j + 1) * NB], start=True, stop=True)\
                    .then_inc(bank_full[b], 1)

        @block.gpsimd
        def _(pool):
            pool.memset(vrow[:, :, :], 0.0).then_inc(rows_zero, 1)
            pool.memset(epsc[:, 0:1], EPS).then_inc(v_eps, 1)
            pool.memset(acc[:, 0, :], 0.0).then_inc(acc_zero, 1)
            pool.memset(acc[:, 1, :], 0.0).then_inc(acc_zero, 1)

            def level(t, lv):
                pool.tensor_tensor(Cm[:, t], Dm[:, t], over_heads(c_(LV0 + lv)), ALU.mult).then_inc(p_C, 1)

            def m1s(i):
                t, g = i // 2, i % 2
                pool.tensor_tensor(M1s[:, i % 2], over_heads(c_(SGT)), over_cols(dec[:, 9, t, 4 + 4 * g:8 + 4 * g], P),
                                   ALU.mult).then_inc(p_ms1, 1)

            def stage(name):
                if name.startswith("mod"):
                    n = int(name[3])
                    wait_full(pool, name, 0)
                    pool.memset(acc[:, n % 2, :], 0.0).then_inc(acc_zero, 1)
                elif name == "sums":
                    pool.wait_ge(v_dec, 3)
                    for t in range(TT):
                        pool.tensor_tensor(Cm[:, t], over_heads(c_(SGT)), over_cols(dec[:, 9, t, 0:H], P), ALU.mult)\
                            .then_inc(p_m1, 1)
                elif name.startswith("decay"):
                    t = int(name[5])
                    wait_taken(pool, name, 0)
                    pool.tensor_tensor(Dm[:, t], Dm[:, t], over_heads(c_(SGTB)), ALU.mult).then_inc(p_dmask, 1)
                    wait_taken(pool, name, 1)
                    pool.tensor_tensor(Dt[:, t], Dt[:, t], over_heads(c_(UINCB)), ALU.mult).then_inc(p_dmask, 1)
                elif name == "kbg":
                    pool.wait_ge(v_qkn, 2)
                    pool.wait_ge(v_rn, 1)
                    for t in range(TT):
                        if t == 0:
                            wait_taken(pool, "tm_v", 0)
                            wait_taken(pool, "tm_v", 1)
                        ins = pool.tensor_tensor(kbg[:, t], tm[:, 1, t], over_cols(dec[:, 8, t, 4:8], P), ALU.mult)
                    ins.then_inc(p_kbg, 1)
                    for t in range(TT):
                        wait_full(pool, "kqT", 2 + t)
                        pool.tensor_tensor(tm[:, 0, t], tm[:, 0, t], over_cols(sums[:, CS_GDN, t, 0:H], P), ALU.mult)\
                            .then_inc(p_qd, 1)
                    pool.wait_ge(p_kbg, 1)
                    for t in range(TT):
                        pool.tensor_tensor(tm[:, 1, t], tm[:, 1, t], over_cols(sums[:, REST_GDN, t, 0:H], P), ALU.mult)\
                            .then_inc(p_qd, 1)
                elif name == "kk":
                    for t in range(TT):
                        wait_taken(pool, "kk", t)
                        level(t, 0)
                elif name == "lv0":
                    for t in range(TT):
                        wait_full(pool, "lv0", t)
                        level(t, 1)
                elif name.startswith("invY"):
                    lv = int(name[4])
                    for t in range(TT):
                        wait_full(pool, name, t)
                        if lv < 5:
                            level(t, lv + 1)
                elif name == "invX5":
                    for t in range(TT):
                        wait_full(pool, name, t)
                    pool.memset(VZ[:, :, :, :], 0.0).then_inc(p_vz, 1)
                    pool.memset(O[0:64, 0], 0.0).then_inc(p_vz, 1)
                elif name == "ssm_tm":
                    wait_full(pool, "gdn_out", 1)
                    m1s(0)
                    m1s(1)
                elif name in ("ssm_e0", "ssm_e1"):
                    wait_full(pool, name, 0)
                    m1s(int(name[5]) + 2)
                elif name == "rope":
                    wait_full(pool, "ssm_out", 1)
                    pool.wait_ge(a_trig, 1)
                    wait_chunk_taken(pool, CHUNK["a2"])
                    pool.memset(kz[:, :, :, :, :], 0.0).then_inc(pool_step, 1)
                    qk = ptm[:, :, T_AQ:T_AV].rearrange("p t (h s n) -> p t h s n", h=10, s=2)
                    out = rq[:, :, :, :].rearrange("p t h (s n) -> p t h s n", s=2)
                    n = 1
                    for t in range(TT):
                        cos = trig[:, 0, t, :].unsqueeze(1).broadcast_to([P, 10, 32])
                        sin = trig[:, 1, t, :].unsqueeze(1).broadcast_to([P, 10, 32])
                        for s, (first, second, op) in enumerate(((cos, sin, ALU.subtract), (sin, cos, ALU.add))):
                            pool.tensor_tensor(rtmp[:, 0, t], qk[:, t, :, 0], first, ALU.mult).then_inc(pool_step, 1)
                            pool.tensor_tensor(rtmp[:, 1, t], qk[:, t, :, 1], second, ALU.mult).then_inc(pool_step, 1)
                            n += 2
                            pool.wait_ge(pool_step, n)
                            pool.tensor_tensor(out[:, t, :, s], rtmp[:, 0, t], rtmp[:, 1, t], op).then_inc(pool_step, 1)
                            n += 1
                            pool.wait_ge(pool_step, n)
                    for z in range(2):
                        for t in range(TT):
                            ins = pool.tensor_copy(kz[:, t, :, z, z * HD:(z + 1) * HD], rq[:, t, 8:10, :])
                    ins.then_inc(p_rope, 1)

            stage("mod0")
            stage("mod1")
            for slot in SCHEDULE:
                for name in slot:
                    stage(name)
            wait_full(pool, "gate_a", 3)
            pool.memset(acc[:, 1, :], 0.0).then_inc(acc_zero, 1)
            wait_full(pool, "h2T", 7)
            pool.memset(y[:, :, :], 0.0).then_inc(y_zero, 1)

        @block.scalar
        def _(act):
            steps = [0]

            def step(ins):
                ins.then_inc(act_step, 1)
                steps[0] += 1
                act.wait_ge(act_step, steps[0])

            for name, stack, row, n in ROWS:
                src = a[name] if name in ("c",) else a[name][0]
                if len(src.shape) == 1:
                    src = src.rearrange("(r n) -> r n", n=P)
                else:
                    src = src.rearrange("k (r n) -> (k r) n", n=P)
                if row == VA_C and stack == 0:
                    act.wait_ge(rows_zero, 1)
                act.dma_start(vrow[row:row + n, stack, :], src).then_inc(vrow_in, 16)
            for name, col, n in PRM:
                src = a[name] if name == "inv_freq" else a[name][0]
                act.dma_start(prm[:, col:col + n], src.partition_broadcast(P)).then_inc(prm_in, 16)
            act.dma_start(posi[:, :], a["positions"][0].rearrange("(t p) -> p t", p=P),
                          allow_slow_non_contiguous=True).then_inc(pos_in, 16)

            junk = rst[:, :, :, :].rearrange("p b t n -> p (b t n)")

            def rstd(ap, n, done):
                step(act.activation(ap, ap, ACT.Ln, bias=epsc[:, 0:1], scale=1.0 / n))
                act.activation(ap, ap, ACT.Exp, scale=-0.5).then_inc(done, 1)

            act.wait_ge(x_in, 16)
            act.wait_ge(v_eps, 1)
            for t in range(TT):
                step(act.activation(junk0[:, :], x0[:, t, :], ACT.Square, accum_out=st[:, t:t + 1]))
            rstd(st[:, 0:2], D, a_rstd)
            act.wait_ge(prm_in, 16 * len(PRM))
            act.activation(prm[:, P_ALOG:P_ALOG + 12], prm[:, P_ALOG:P_ALOG + 12], ACT.Exp).then_inc(a_rstd, 1)
            wait_full(act, "vecT", 0)
            taken(act.activation(vcol[:, :, :], mx[fill_of("vecT", 0)[0]][:, 0:2 * P].rearrange("p (v n) -> p v n", v=2), ACT.Copy), "vecT", 0)
            wait_taken(act, "vecT", 0)
            act.activation(cact[:, :], vcol[:, 0, VA_C:VA_C + KT], ACT.Silu).then_inc(a_cact, 1)
            act.wait_ge(v_ang, 1)
            act.activation(trig[:, 0], ang[:, 1], ACT.Sin)
            act.activation(trig[:, 1], ang[:, 3], ACT.Sin).then_inc(a_trig, 1)
            for j in range(8):
                b = wait_full(act, "xT", j)
                taken(act.activation(xT[:, 2 * j:2 * j + 2, :], b[:, :].rearrange("p (k n) -> p k n", k=2), ACT.Copy), "xT", j)
            for part in range(4):
                act.wait_ge(v_hmod, part + 1)
                act.activation(hhi[:, 4 * part:4 * part + 4, :], xT[:, 4 * part:4 * part + 4, :], ACT.Copy).then_inc(a_hi, 1)

            def split(slot, w, hh, h, n_in, first=False):
                if hh == 0:
                    act.wait_ge(raw_in[slot], n_in)
                if not first:
                    act.wait_ge(halves_done, h - 1)
                src = raw[:, slot, :].rearrange("p (k n) -> p k n", k=GK)[:, 2 * hh:2 * hh + 2, 0:w]
                act.activation(whi[:, hh, :, 0:w], src, ACT.Copy).then_inc(hi_ready, 1)

            def split_at(h):
                ci, gi = divmod(h // 2, GROUPS)
                pos = POS_OF["w", ci, gi]
                split(pos % RING, CHUNKS[ci][2], h % 2, h, 16 * (pos // RING + 1), h < 2)

            staged = {}
            for i, c in enumerate(STAGED):
                before = [s for s in STAGED[:i] if STG_OF[s] == STG_OF[c]]
                staged[c] = before[-1] if before else None

            def evacuate(ci):
                name, _, w = CHUNKS[ci]
                if name == "ch":
                    return
                act.wait_ge(halves_done, 2 * GROUPS * (ci + 1))
                if name in STG_OF:
                    if staged[name]:
                        wait_full(act, ("mul_" if staged[name] == "cb" else "conv_") + staged[name], 1)
                    dst = stg[:, STG_OF[name], :, :]
                else:
                    dst = ptm[:, :, TM_AT[name]:TM_AT[name] + w]
                act.activation(dst, gps[ci % 2][:, :, 0:w], ACT.Copy).then_inc(gemm_free[ci % 2], 1)

            def copy_out(dst, name, i, func=ACT.Copy, **kw):
                b = wait_full(act, name, i)
                shape = dst.shape
                src = b[:, :] if len(shape) == 2 else b[:, 0:shape[1] * shape[2]].rearrange("p (h n) -> p h n", h=shape[1])
                taken(act.activation(dst, src, func, **kw), name, i)

            def stage(name):
                if name.startswith("evac"):
                    evacuate(int(name[4:]))
                elif name.startswith("conv_"):
                    c = name[5:]
                    for i in range(2):
                        b = wait_full(act, name, i)
                        for jj in range(2):
                            j = 2 * i + jj
                            if c == "cc":
                                w = vcol[:, 0, VA_SC + 2 * 4 + j:VA_SC + 2 * 4 + j + 1]
                                dst = mixT[:, 12 + j, :]
                            else:
                                tile0 = CONV[c][1]
                                w = tap_col(c, 3, j)
                                dst = cvo[:, tile0 + j, :]
                            ins = act.activation(dst, b[:, jj * SEQ:(jj + 1) * SEQ], ACT.Copy, scale=w)
                        ins.then_inc(a_tap, 1)
                elif name.startswith("silu_"):
                    c = name[5:]
                    if c == "gz":
                        wait_chunk_taken(act, CHUNK["gz"])
                        act.activation(ptm[:, :, T_GZ:T_GZ + GW], ptm[:, :, T_GZ:T_GZ + GW], ACT.Silu).then_inc(a_gz, 1)
                    elif c == "sz":
                        wait_chunk_taken(act, CHUNK["s2"])
                        act.activation(ptm[:, :, T_SZ:T_SZ + GW], ptm[:, :, T_SZ:T_SZ + GW], ACT.Silu).then_inc(a_sz, 1)
                    else:
                        tile0 = CONV[c][1]
                        wait_taken(act, "conv_" + c, 1)
                        if c[0] == "g":
                            act.activation(cvo[:, tile0:tile0 + 4, :], cvo[:, tile0:tile0 + 4, :], ACT.Silu).then_inc(a_silu, 1)
                        else:
                            for j in range(4):
                                t_ = tile0 + j
                                ins = act.activation(cvo[:, t_, :], cvo[:, t_, :], ACT.Silu,
                                                     bias=vcol[:, 0, VA_CONVB + t_ - 12:VA_CONVB + t_ - 11])
                            ins.then_inc(a_silu, 1)
                elif name == "softplus":
                    act.wait_ge(v_dec, 1)
                    act.activation(dec[:, 8, :, 8:12], ptm[:, :, T_B:T_B + 4], ACT.Exp, scale=-1.0)
                    act.activation(dec[:, 2], dec[:, 1], ACT.Exp, scale=-1.0).then_inc(a_dec, 1)
                    act.wait_ge(v_dec, 2)
                    act.activation(dec[:, 6], dec[:, 3], ACT.Ln).then_inc(a_dec, 1)
                elif name == "sums":
                    b = wait_full(act, name, 0)
                    taken(act.activation(sums[:, :, :, :].rearrange("p s t n -> p (s t n)"), b[:, 0:len(SUM_MASKS) * 24], ACT.Exp), name, 0)
                elif name.startswith("decay"):
                    t = int(name[5])
                    copy_out(Dm[:, t], name, 0, ACT.Exp)
                    copy_out(Dt[:, t], name, 1, ACT.Exp)
                elif name in ("tm_q", "tm_k"):
                    for t in range(TT):
                        copy_out(tm[:, "qk".index(name[3]), t], name, t)
                elif name == "l2stat":
                    act.wait_ge(v_ss, 2)
                    step(act.activation(st[:, 20:36], st[:, 4:20], ACT.Ln, bias=epsc[:, 0:1]))
                    act.activation(st[:, 20:36], st[:, 20:36], ACT.Exp, scale=-0.5).then_inc(a_rn, 1)
                elif name == "kqT":
                    for t in range(TT):
                        copy_out(knT[:, t], name, t)
                    for t in range(TT):
                        copy_out(qnT[:, t], name, 2 + t)
                elif name.startswith("invY"):
                    for t in range(TT):
                        copy_out(Ym[:, t], name, t)
                elif name == "qdT":
                    for t in range(TT):
                        copy_out(qdT[:, t], name, t)
                elif name == "uw":
                    for t in range(TT):
                        copy_out(U[:, t], name, 2 * t)
                        copy_out(WT[:, t], name, 2 * t + 1)
                elif name in ("gdn_v1", "gdn_v2", "gdn_v3"):
                    c = int(name[5])
                    r0 = (c % 2) * 64
                    b = wait_full(act, name, 1)
                    taken(act.activation(O[r0:r0 + 64, c // 2], slab(b)[r0:r0 + 64], ACT.Copy), name, 1)
                elif name == "gdn_gate":
                    act.wait_ge(v_oss, 1)
                    rstd(st[:, 36:44], P, a_orn)
                elif name == "gdn_out":
                    for t in range(TT):
                        copy_out(mixT[:, 0:4, t * P:(t + 1) * P], name, t, scale=vcol[:, 0, VA_GDNN:VA_GDNN + 1])
                elif name == "ssm_tm":
                    for t in range(TT):
                        b = wait_full(act, name, t)
                        taken(act.activation(xs[:, t, :], b[:, :], ACT.Copy), name, t)
                    copy_out(btm[:, :, :], name, 2)
                elif name == "ssm_s":
                    copy_out(stt_[:, :, :], name, 0)
                elif name.startswith("ssm_e"):
                    copy_out(Es[:, int(name[5]) % 2], name, 0, ACT.Exp)
                elif name == "ssm_gate":
                    act.wait_ge(v_yss, 1)
                    rstd(st[:, 44:48], SEQ, a_yrn)
                elif name == "att_T":
                    for t in range(TT):
                        copy_out(qT2[:, t], name, t)
                    for t in range(TT):
                        copy_out(kzT[:, :, t * P:(t + 1) * P], name, 2 + t)
                elif name.startswith("att_s"):
                    f = int(name[5])
                    n, heads, blocks = att_part(f)
                    w = len(blocks) * P
                    act.wait_ge(v_aneg, f + 1)
                    act.activation(ats[:, f, 8:8 + len(heads)], ats[:, f, 8:8 + len(heads)], ACT.Exp)
                    for i in range(len(heads)):
                        s = sc[:, f % 2, i * w:(i + 1) * w]
                        ins = act.activation(s, s, ACT.Exp, bias=ats[:, f, 4 + i:5 + i], accum_out=ats[:, f, 12 + i:13 + i])
                    ins.then_inc(a_p, 1)
                elif name.startswith("att_t"):
                    copy_out(PT[:, int(name[5]) % 2], name, 0)
                elif name == "att_out":
                    for t in range(TT):
                        copy_out(mixT[:, 8:12, t * P:(t + 1) * P], name, t)

            split_at(0)
            split_at(1)
            for h in range(SLOTS):
                if h + 2 < SLOTS:
                    split_at(h + 2)
                for name in with_moves(h):
                    stage(name)

            act.wait_ge(halves_done, 2 * W_GROUPS)
            for i, kg in enumerate(WOUT_ORDER):
                if kg == 3:
                    wait_taken(act, "mul_cb", 1)
                if kg == 1:
                    wait_taken(act, "ssm_out", 1)
                if kg == 0:
                    wait_taken(act, "gdn_out", 1)
                if kg == 2:
                    wait_taken(act, "att_out", 1)
                act.activation(hhi[:, 4 * kg:4 * kg + 4, :], mixT[:, 4 * kg:4 * kg + 4, :], ACT.Copy).then_inc(mix_hi, 1)
            act.wait_ge(mix_lo, 4)
            act.dma_start(x1[:, :, :], x_v).then_inc(xr_in, 16)
            act.dma_start(grow[:, :], a["norm_post_mix"][0].partition_broadcast(P)).then_inc(wpost_in, 16)

            h1 = 2 * W_GROUPS
            n1 = 16 * (POS1 // RING + 1)
            with act.Fori(0, 2) as it:
                for n in range(2 * GROUPS):
                    for hh in range(2):
                        split((2 * n) % RING, NB, hh, it * (4 * GROUPS) + (h1 + 2 * n + hh), it * 64 + (n1 + 16 * (2 * n // RING)))
                    if n % GROUPS == GROUPS - 1:
                        c = n // GROUPS
                        act.wait_ge(halves_done, it * (4 * GROUPS) + (h1 + 2 * GROUPS * (c + 1)))
                        for t in range(TT):
                            act.activation(rst[:, c, t, :], gps[(NCH + c) % 2][:, t, :], ACT.Square,
                                           accum_out=yss[:, t, bass.ds(it * 2 + c, 1)]).then_inc(a_ysq, 1)

            act.wait_ge(v_ysum, 1)
            rstd(st[:, 48:50], D, a_yr)
            for t in range(TT):
                act.wait_ge(v_x1, t + 1)
                step(act.activation(junk, x1[:, t, :], ACT.Square, accum_out=st[:, 52 + t:53 + t]))
                rstd(st[:, 52 + t:53 + t], D, a_x1r)
            act.dma_start(grow[:, :], a["norm_post_mlp"][0].partition_broadcast(P)).then_inc(wpost_in, 16)
            wait_taken(act, "mod2", 0)
            wait_taken(act, "mod4", 0)
            for j in range(8):
                b = wait_full(act, "h2T", j)
                if j >= 2:
                    act.wait_ge(h2_lo, j - 1)
                for kk in range(2):
                    k = 2 * j + kk
                    ins = act.activation(hful[:, j % 2, kk, :], b[:, kk * SEQ:(kk + 1) * SEQ], ACT.Identity,
                                         bias=modc[:, 2, k:k + 1], scale=modc[:, 3, k:k + 1])
                taken(ins, "h2T", j)
                wait_taken(act, "h2T", j)
                act.activation(hhi[:, 2 * j:2 * j + 2, :], hful[:, j % 2], ACT.Copy).then_inc(h2_hi, 1)

            h2 = h1 + 8 * GROUPS
            n2 = n1 + 128
            with act.Fori(0, QUARTERS) as q:
                def relu(c):
                    ci = NCH + 4 + c
                    act.wait_ge(halves_done, q * (16 * GROUPS) + (h2 + 2 * GROUPS * (c + 1)))
                    f = 2 * ((c + 2) % 4) + 1
                    b, n = mlp_fill(f)
                    act.wait_ge(bank_full[b], q * 2 + (n + 1 - (2 if c < 2 else 0)))
                    act.activation(rst[:, c % 2], gps[ci % 2][:, :, :], ACT.Relu).then_inc(gemm_free[ci % 2], 1)
                for c in range(8):
                    for g in range(GROUPS):
                        i = c * GROUPS + g
                        pos = MLP_POS["w", i]
                        for hh in range(2):
                            split(pos % RING, NB, hh, q * (16 * GROUPS) + (h2 + 2 * i + hh),
                                  q * (4 * len(MLP_ITEMS)) + (n2 + 16 * (pos // RING)))
                        if g == 0 and 1 <= c <= 4:
                            relu(c - 1)
                        if g == 2 and 1 <= c <= 4:
                            for i2 in range(2):
                                f = 2 * (c - 1) + i2
                                b, n = mlp_fill(f)
                                act.wait_ge(bank_full[b], q * 2 + (n + 1))
                                act.activation(ahi[:, 2 * f:2 * f + 2, :], mx[b][:, :].rearrange("p (k n) -> p k n", k=2),
                                               ACT.Copy).then_inc(act_hi, 1)
            wait_chunk_taken(act, NCH + 4 + 8 * QUARTERS - 2)
            wait_chunk_taken(act, NCH + 4 + 8 * QUARTERS - 1)
            for t in range(TT):
                step(act.activation(junk, y[:, t, :], ACT.Square, accum_out=st[:, 56 + t:57 + t]))
                rstd(st[:, 56 + t:57 + t], D, a_yss)

        @block.vector
        def _(dve):
            steps = [0]

            def step(ins):
                ins.then_inc(vec_step, 1)
                steps[0] += 1
                dve.wait_ge(vec_step, steps[0])

            dve.wait_ge(pos_in, 16)
            dve.wait_ge(prm_in, 16 * len(PRM))
            step(dve.tensor_copy(posf[:, :], posi[:, :]))
            for t in range(TT):
                ins = dve.tensor_scalar(ang[:, 0, t, :], prm[:, P_FREQ:P_FREQ + 32], posf[:, t:t + 1], None, ALU.mult)
            step(ins)
            for quarter, dst in ((0.25, 1), (0.0, 3)):
                step(dve.tensor_scalar(ang[:, 2], ang[:, 0], 1.0 / TWO_PI, quarter, ALU.mult, ALU.add))
                step(dve.tensor_copy(angi[:, :, :], ang[:, 2]))
                step(dve.tensor_copy(ang[:, 2], angi[:, :, :]))
                step(dve.scalar_tensor_tensor(out=ang[:, dst], in0=ang[:, 2], scalar=-PI2_A, in1=ang[:, 0], op0=ALU.mult, op1=ALU.add))
                step(dve.scalar_tensor_tensor(out=ang[:, dst], in0=ang[:, 2], scalar=-PI2_B, in1=ang[:, dst], op0=ALU.mult, op1=ALU.add))
                step(dve.scalar_tensor_tensor(out=ang[:, dst], in0=ang[:, 2], scalar=-PI2_C, in1=ang[:, dst], op0=ALU.mult, op1=ALU.add))
                step(dve.tensor_scalar(ang[:, dst], ang[:, dst], quarter * TWO_PI, PI_LOW, ALU.add, ALU.min))
                ins = dve.tensor_scalar(ang[:, dst], ang[:, dst], -PI_LOW, None, ALU.max)
                if dst == 3:
                    ins.then_inc(v_ang, 1)
                else:
                    step(ins)
            dve.wait_ge(a_rstd, 1)
            for t in range(TT):
                dve.tensor_scalar(xn0[:, t, :], x0[:, t, :], st[:, 2 * 0 + t:t + 1], None, ALU.mult).then_inc(v_xn, 1)

            def ada(a_, k, pos):
                if a_ == 0 and k == 0:
                    dve.wait_ge(a_cact, 1)
                if k == 0:
                    dve.wait_ge(acc_seed[a_ % 2], 16 * (a_ // 2 + 1))
                else:
                    dve.wait_ge(ada_used, a_ * KT + k)
                dve.wait_ge(raw_in[pos % RING], 16 * (pos // RING + 1))
                dve.scalar_tensor_tensor(out=acc[:, a_ % 2, :], in0=raw[:, pos % RING, :], scalar=cact[:, k:k + 1],
                                         in1=acc[:, a_ % 2, :], op0=ALU.mult, op1=ALU.add).then_inc(ada_used, 1)
                if k == KT - 1:
                    dve.wait_ge(ada_used, a_ * KT + KT)
                    dve.sem_inc(acc_full, 1)

            def split(slot, w, hh, h, n_in):
                if hh == 0:
                    dve.wait_ge(raw_in[slot], n_in)
                dve.wait_ge(hi_ready, h + 1)
                src = raw[:, slot, :].rearrange("p (k n) -> p k n", k=GK)[:, 2 * hh:2 * hh + 2, 0:w]
                dve.tensor_tensor(wlo[:, hh, :, 0:w], src, whi[:, hh, :, 0:w].bitcast(F32), ALU.subtract)\
                    .then_inc(lo_ready, 1)

            def split_at(h):
                ci, gi = divmod(h // 2, GROUPS)
                pos = POS_OF["w", ci, gi]
                split(pos % RING, CHUNKS[ci][2], h % 2, h, 16 * (pos // RING + 1))
                if h % 2 and pos + 1 < POS1 and STREAM[pos + 1][0] == "ada":
                    ada(STREAM[pos + 1][1], STREAM[pos + 1][2], pos + 1)

            def lower(dst_lo, src, src_hi):
                return dve.tensor_tensor(dst_lo, src, src_hi.bitcast(F32), ALU.subtract)

            def taps(name, i, dst, w_of, n_taps):
                b = wait_full(dve, name, i)
                for back in range(1, n_taps):
                    for jj in range(2):
                        d = dst(2 * i + jj)[:, back:SEQ]
                        ins = dve.scalar_tensor_tensor(out=d, in0=b[:, jj * SEQ:(jj + 1) * SEQ - back],
                                                       scalar=w_of(n_taps - 1 - back, 2 * i + jj), in1=d, op0=ALU.mult, op1=ALU.add)
                        if back == n_taps - 1 and jj == 1:
                            taken(ins, name, i)
                        elif jj == 1:
                            step(ins)

            def stage(name):
                if name == "evac" + str(CHUNK["ch"]):
                    ci = CHUNK["ch"]
                    dve.wait_ge(halves_done, 2 * GROUPS * (ci + 1))
                    wait_chunk_taken(dve, CHUNK["cc"])
                    s = stg[:, STG_OF["cc"]]
                    dve.tensor_tensor(s, gps[ci % 2][:, :, :], s, ALU.mult).then_inc(gemm_free[ci % 2], 1)
                elif name.startswith("mod"):
                    n = int(name[3])
                    b = wait_full(dve, name, 0)
                    if n in (0, 2):
                        taken(dve.tensor_copy(modc[:, n, :], b[:, 0:KT]), name, 0)
                    else:
                        row = VA_PRE_MIX if n == 1 else VA_PRE_MLP
                        taken(dve.scalar_tensor_tensor(out=modc[:, 1 if n == 1 else 3, :], in0=b[:, 0:KT], scalar=1.0,
                                                       in1=vcol[:, 0, row:row + KT], op0=ALU.add, op1=ALU.mult), name, 0)
                elif name.startswith("conv_"):
                    c = name[5:]
                    for i in range(2):
                        dve.wait_ge(a_tap, 2 * (CONV_ORDER + ["cc"]).index(c) + i + 1)
                        if c == "cc":
                            taps(name, i, lambda j: mixT[:, 12 + j, :],
                                 lambda tap, j: vcol[:, 0, VA_SC + tap * 4 + j:VA_SC + tap * 4 + j + 1], 3)
                        else:
                            tile0 = CONV[c][1]
                            taps(name, i, lambda j: cvo[:, tile0 + j, :], lambda tap, j: tap_col(c, tap, j), 4)
                elif name == "mul_cb":
                    for i in range(2):
                        b = wait_full(dve, name, i)
                        wait_taken(dve, "conv_cc", i)
                        d = mixT[:, 12 + 2 * i:14 + 2 * i, :]
                        taken(dve.tensor_tensor(d, b[:, :].rearrange("p (k n) -> p k n", k=2), d, ALU.mult), name, i)
                elif name == "softplus":
                    wait_chunk_taken(dve, CHUNK["s1"])
                    wait_chunk_taken(dve, CHUNK["a1"])
                    dve.wait_ge(a_rstd, 2)
                    z, ax, e, u, num, den, ln, sp = (dec[:, i] for i in range(8))
                    for col, n, at in ((T_A, 4, 0), (T_DT, 8, 4)):
                        ins = dve.tensor_tensor(z[:, :, at:at + n], ptm[:, :, col:col + n],
                                                prm[:, P_DTB + at:P_DTB + at + n].unsqueeze(1).broadcast_to([P, TT, n]), ALU.add)
                    step(ins)
                    dve.scalar_tensor_tensor(out=ax, in0=z, scalar=-1.0, in1=z, op0=ALU.mult, op1=ALU.max).then_inc(v_dec, 1)
                    dve.wait_ge(a_dec, 1)
                    dve.tensor_scalar(dec[:, 8, :, 8:12], dec[:, 8, :, 8:12], 1.0, None, ALU.add)
                    dve.tensor_scalar(u, e, 1.0, None, ALU.add).then_inc(v_dec, 1)
                    dve.wait_ge(v_dec, 2)
                    step(dve.tensor_scalar(den, u, -1.0, None, ALU.add))
                    step(dve.tensor_scalar(num, den, 0.0, None, ALU.is_equal))
                    step(dve.tensor_tensor(den, den, num, ALU.add))
                    step(dve.reciprocal(den, den))
                    dve.wait_ge(a_dec, 2)
                    step(dve.tensor_tensor(num, num, ln, ALU.add))
                    step(dve.tensor_tensor(num, num, e, ALU.mult))
                    step(dve.tensor_tensor(num, num, den, ALU.mult))
                    dve.reciprocal(dec[:, 8, :, 0:4], dec[:, 8, :, 8:12])
                    step(dve.scalar_tensor_tensor(out=sp, in0=z, scalar=0.0, in1=num, op0=ALU.max, op1=ALU.add))
                    dve.scalar_tensor_tensor(out=dec[:, 9], in0=sp, scalar=-1.0,
                                             in1=prm[:, P_ALOG:P_ALOG + 12].unsqueeze(1).broadcast_to([P, TT, 12]),
                                             op0=ALU.mult, op1=ALU.mult).then_inc(v_dec, 1)
                elif name == "sums":
                    wait_taken(dve, "sums", 0)
                    dve.wait_ge(v_dec, 3)
                    dve.tensor_tensor(dec[:, 8, :, 4:8], dec[:, 8, :, 0:4], sums[:, CS_GDN, :, 0:H], ALU.mult).then_inc(v_rn, 1)
                elif name in ("tm_q", "tm_k"):
                    w = "qk".index(name[3])
                    for t in range(TT):
                        wait_taken(dve, name, t)
                        step(dve.tensor_tensor(Ym[:, t], tm[:, w, t], tm[:, w, t], ALU.mult))
                        ins = dve.tensor_reduce(st[:, 4 + 8 * w + 4 * t:8 + 8 * w + 4 * t], Ym[:, t], AX, ALU.add)
                    ins.then_inc(v_ss, 1)
                elif name == "tm_v":
                    for t in range(TT):
                        b = wait_full(dve, name, t)
                        taken(dve.tensor_tensor(tm[:, 2, t], slab(b), over_cols(dec[:, 8, t, 0:4], P), ALU.mult), name, t)
                elif name == "l2scale":
                    dve.wait_ge(a_rn, 1)
                    for w in (0, 1):
                        n = tm[:, w].rearrange("p t h n -> p (t h) n")
                        r = over_cols(st[:, 20 + 8 * w:28 + 8 * w], P)
                        if w == 0:
                            step(dve.tensor_scalar(st[:, 20:28], st[:, 20:28], float(P) ** -0.5, None, ALU.mult))
                        dve.tensor_tensor(n, n, r, ALU.mult).then_inc(v_qkn, 1)
                elif name == "kk":
                    for t in range(TT):
                        dve.wait_ge(p_dmask, 2 * t + 1)
                        b = wait_full(dve, name, t)
                        for h in range(H):
                            ins = dve.scalar_tensor_tensor(out=Dm[:, t, h], in0=b[:, h * P:(h + 1) * P], scalar=dec[:, 8, t, h:h + 1],
                                                           in1=Dm[:, t, h], op0=ALU.mult, op1=ALU.mult)
                        taken(ins, name, t)
                elif name == "qk":
                    for t in range(TT):
                        dve.wait_ge(p_dmask, 2 * t + 2)
                        b = wait_full(dve, name, t)
                        taken(dve.tensor_tensor(Dt[:, t], slab(b), Dt[:, t], ALU.mult), name, t)
                elif name == "lv0":
                    for t in range(TT):
                        dve.wait_ge(p_C, t + 1)
                        b = wait_full(dve, name, t)
                        step(dve.scalar_tensor_tensor(out=Xt[:, t], in0=slab(b), scalar=-1.0, in1=over_heads(c_(IDENT)),
                                                      op0=ALU.mult, op1=ALU.add))
                        step(dve.tensor_tensor(Xm[:, t], Dm[:, t], over_heads(c_(LV0)), ALU.mult))
                        step(dve.scalar_tensor_tensor(out=Xm[:, t], in0=Xm[:, t], scalar=-1.0, in1=over_heads(c_(IDENT)),
                                                      op0=ALU.mult, op1=ALU.add))
                        dve.sem_inc(bank_free[fill_of(name, t)[0]], 1)
                        dve.sem_inc(v_X, 1)
                elif name.startswith("invX"):
                    lv = int(name[4])
                    for t in range(TT):
                        b = wait_full(dve, name, t)
                        ins = dve.tensor_tensor(Xt[:, t], Xt[:, t], slab(b), ALU.subtract)
                        taken(ins, name, t)
                        if lv < 5:
                            b = wait_full(dve, name, 2 + t)
                            taken(dve.tensor_tensor(Xm[:, t], Xm[:, t], slab(b), ALU.subtract), name, 2 + t)
                            wait_taken(dve, name, 2 + t)
                        wait_taken(dve, name, t)
                        dve.sem_inc(v_X, 1)
                elif name.startswith("gdn_v"):
                    c = int(name[5])
                    t, r0 = c // 2, (c % 2) * 64
                    wait_taken(dve, "uw", 2 * t)
                    if c == 0:
                        dve.wait_ge(p_vz, 2)
                        dve.tensor_copy(VZ[0:64, 0], U[0:64, 0]).then_inc(v_vz, 1)
                    else:
                        if c == 2:
                            wait_full(dve, "gdn_o0", 0)
                        b = wait_full(dve, name, 0)
                        step(dve.tensor_tensor(VZ[r0:r0 + 64, c % 2], U[r0:r0 + 64, t], slab(b)[r0:r0 + 64], ALU.subtract))
                        dve.sem_inc(bank_free[fill_of(name, 0)[0]], 1)
                        dve.sem_inc(v_vz, 1)
                elif name.startswith("gdn_s"):
                    c = int(name[5])
                    b = wait_full(dve, name, 0)
                    if c == 0:
                        taken(dve.tensor_copy(Sm[:, :, :], slab(b)), name, 0)
                    else:
                        wait_taken(dve, f"gdn_s{c - 1}", 0)
                        for h in range(H):
                            ins = dve.scalar_tensor_tensor(out=Sm[:, h], in0=Sm[:, h], scalar=sums[:, TOT0 + c % 2, c // 2, h:h + 1],
                                                           in1=b[:, h * P:(h + 1) * P], op0=ALU.mult, op1=ALU.add)
                        taken(ins, name, 0)
                elif name in ("gdn_o0", "gdn_o1"):
                    t = int(name[5])
                    b = wait_full(dve, name, 0)
                    dve.wait_ge(p_vz, 2)
                    wait_taken(dve, f"gdn_v{2 * t + 1}", 1)
                    if t:
                        wait_taken(dve, "gdn_v2", 1)
                    taken(dve.tensor_tensor(O[:, t], O[:, t], slab(b), ALU.add), name, 0)
                elif name == "gdn_gate":
                    wait_taken(dve, "gdn_o0", 0)
                    wait_taken(dve, "gdn_o1", 0)
                    step(dve.tensor_tensor(Xt[:, :, :, :], O[:, :, :, :], O[:, :, :, :], ALU.mult))
                    dve.tensor_reduce(st[:, 36:44], Xt[:, :, :, :].rearrange("p t h n -> p (t h) n"), AX, ALU.add).then_inc(v_oss, 1)
                    dve.wait_ge(a_orn, 1)
                    o = O[:, :, :, :].rearrange("p t h n -> p (t h) n")
                    step(dve.tensor_tensor(o, o, over_cols(st[:, 36:44], P), ALU.mult))
                    dve.wait_ge(a_gz, 1)
                    o = O[:, :, :, :].rearrange("p t h n -> p t (h n)")
                    dve.tensor_tensor(o, o, ptm[:, :, T_GZ:T_GZ + GW], ALU.mult).then_inc(v_og, 1)
                elif name == "ssm_tm":
                    for t in range(TT):
                        wait_taken(dve, name, t)
                    x3 = xs[:, :, :].rearrange("p t (h n) -> p t h n", h=SH)
                    for t in range(TT):
                        dve.tensor_tensor(yb[:, t, :].rearrange("p (h n) -> p h n", h=SH), x3[:, t],
                                          over_cols(prm[:, P_SD:P_SD + 8], HD), ALU.mult)
                    for t in range(TT):
                        ins = dve.tensor_tensor(xdt[:, t], x3[:, t], over_cols(dec[:, 7, t, 4:12], HD), ALU.mult)
                    step(ins)
                    dve.tensor_tensor(xdd[:, :, :], xdt[:, 0], over_cols(sums[:, REST_SSM, 0, 4:12], HD), ALU.mult).then_inc(v_xdt, 1)
                elif name == "ssm_cb":
                    b = wait_full(dve, name, 0)
                    taken(dve.tensor_tensor(CBm[:, :, :], slab(b), over_heads(c_(UINC)), ALU.mult), name, 0)
                elif name == "ssm_o":
                    b = wait_full(dve, name, 0)
                    step(dve.tensor_tensor(ytmp[:, 0, :].rearrange("p (h n) -> p h n", h=SH), b[:, :].rearrange("p (h n) -> p h n", h=SH),
                                           over_cols(sums[:, CS_SSM, 1, 4:12], HD), ALU.mult))
                    taken(dve.tensor_tensor(yb[:, 1, :], yb[:, 1, :], ytmp[:, 0, :], ALU.add), name, 0)
                elif name.startswith("ssm_e"):
                    i = int(name[5])
                    t, g = i // 2, i % 2
                    wait_taken(dve, "ssm_cb", 0)
                    wait_taken(dve, name, 0)
                    dve.tensor_tensor(Es[:, i % 2], Es[:, i % 2], over_heads(CBm[:, 2 * t + g, :]), ALU.mult).then_inc(v_es, 1)
                elif name.startswith("ssm_y"):
                    i = int(name[5])
                    t, g = i // 2, i % 2
                    b = wait_full(dve, name, 0)
                    wait_taken(dve, "ssm_o", 0)
                    d = yb[:, t, g * SEQ:(g + 1) * SEQ]
                    taken(dve.tensor_tensor(d, d, b[:, 0:SEQ], ALU.add), name, 0)
                elif name == "ssm_gate":
                    for i in range(4):
                        wait_taken(dve, f"ssm_y{i}", 0)
                    dve.wait_ge(a_sz, 1)
                    step(dve.tensor_tensor(yb[:, :, :], yb[:, :, :], ptm[:, :, T_SZ:T_SZ + GW], ALU.mult))
                    step(dve.tensor_tensor(ytmp[:, :, :], yb[:, :, :], yb[:, :, :], ALU.mult))
                    dve.tensor_reduce(st[:, 44:48], ytmp[:, :, :].rearrange("p t (g n) -> p (t g) n", g=2), AX, ALU.add).then_inc(v_yss, 1)
                    dve.wait_ge(a_yrn, 1)
                    o = yb[:, :, :].rearrange("p t (g n) -> p (t g) n", g=2)
                    dve.tensor_tensor(o, o, over_cols(st[:, 44:48], SEQ), ALU.mult).then_inc(v_yg, 1)
                elif name == "ssm_out":
                    for t in range(TT):
                        b = wait_full(dve, name, t)
                        taken(dve.tensor_tensor(mixT[:, 4:8, t * P:(t + 1) * P], slab(b), over_cols(vcol[:, 0, VA_SSMN:VA_SSMN + 4], P),
                                                ALU.mult), name, t)
                elif name.startswith("att_s"):
                    f = int(name[5])
                    n, heads, blocks = att_part(f)
                    nh, w = len(heads), len(blocks) * P
                    b = wait_full(dve, name, 0)
                    mask = cst[:, AMC, :] if len(blocks) == 1 else cst[:, AMP:AMC + 1, :].rearrange("p a n -> p (a n)")
                    s = sc[:, f % 2, :].rearrange("p (h n) -> p h n", h=nh)
                    step(dve.scalar_tensor_tensor(out=s, in0=slab(b, nh), scalar=float(HD) ** -0.5, in1=over_heads(mask, nh),
                                                  op0=ALU.mult, op1=ALU.add))
                    dve.sem_inc(bank_free[fill_of(name, 0)[0]], 1)
                    step(dve.tensor_reduce(ats[:, f, 0:nh], s, AX, ALU.max))
                    sink = prm[:, P_SINK + heads[0]:P_SINK + heads[0] + nh]
                    step(dve.tensor_tensor(ats[:, f, 0:nh], ats[:, f, 0:nh], sink, ALU.max))
                    step(dve.tensor_scalar(ats[:, f, 4:4 + nh], ats[:, f, 0:nh], -1.0, None, ALU.mult))
                    dve.tensor_tensor(ats[:, f, 8:8 + nh], ats[:, f, 4:4 + nh], sink, ALU.add).then_inc(v_aneg, 1)
                elif name.startswith("att_t"):
                    f = int(name[5])
                    nh = len(att_part(f)[1])
                    dve.wait_ge(a_p, f + 1)
                    step(dve.tensor_tensor(ats[:, f, 12:12 + nh], ats[:, f, 12:12 + nh], ats[:, f, 8:8 + nh], ALU.add))
                    step(dve.reciprocal(ats[:, f, 12:12 + nh], ats[:, f, 12:12 + nh]))
                elif name.startswith("att_v"):
                    f = int(name[5])
                    n, heads, blocks = att_part(f)
                    nh = len(heads)
                    b = wait_full(dve, name, 0)
                    taken(dve.tensor_tensor(yc[:, n, heads[0] * HD:(heads[0] + nh) * HD].rearrange("p (h n) -> p h n", h=nh),
                                            b[:, 0:nh * HD].rearrange("p (h n) -> p h n", h=nh),
                                            over_cols(ats[:, f, 12:12 + nh], HD), ALU.mult), name, 0)

            for pos in range(2 * KT):
                ada(STREAM[pos][1], STREAM[pos][2], pos)
            stage("mod0")
            stage("mod1")
            for n in range(2):
                wait_taken(dve, f"mod{n}", 0)
            for part in range(4):
                for k in range(4 * part, 4 * part + 4):
                    wait_taken(dve, "xT", k // 2)
                    ins = dve.tensor_scalar(xT[:, k, :], xT[:, k, :], modc[:, 1, k:k + 1], modc[:, 0, k:k + 1], ALU.mult, ALU.add)
                ins.then_inc(v_hmod, 1)
            for part in range(4):
                dve.wait_ge(a_hi, part + 1)
                ks = slice(4 * part, 4 * part + 4)
                lower(hlo[:, ks, :], xT[:, ks, :], hhi[:, ks, :]).then_inc(v_lo, 1)

            split_at(0)
            split_at(1)
            for h in range(SLOTS):
                if h + 2 < SLOTS:
                    split_at(h + 2)
                for name in with_moves(h):
                    stage(name)

            for i, kg in enumerate(WOUT_ORDER):
                dve.wait_ge(mix_hi, i + 1)
                ks = slice(4 * kg, 4 * kg + 4)
                lower(hlo[:, ks, :], mixT[:, ks, :], hhi[:, ks, :]).then_inc(mix_lo, 1)

            def gate_rows(j, bank, n_in):
                dve.wait_ge(wpost_in, n_in)
                g = grow[:, j * NB:(j + 1) * NB]
                return dve.tensor_tensor(g, bank[:, :], g, ALU.mult)
            for j in range(4):
                b = wait_full(dve, "gate_a", j)
                taken(gate_rows(j, b, 16), "gate_a", j)
            for j in range(4):
                wait_taken(dve, "gate_a", j)

            h1 = 2 * W_GROUPS
            n1 = 16 * (POS1 // RING + 1)

            def ada_turn(n_acc, pos, n_in, k, used):
                dve.wait_ge(ada_used, used)
                dve.wait_ge(raw_in[pos % RING], n_in)
                dve.scalar_tensor_tensor(out=acc[:, n_acc % 2, :], in0=raw[:, pos % RING, :], scalar=cact[:, bass.ds(k, 1)],
                                         in1=acc[:, n_acc % 2, :], op0=ALU.mult, op1=ALU.add).then_inc(ada_used, 1)

            dve.wait_ge(acc_seed[0], 16 * 3)
            with dve.Fori(0, 2) as it:
                for n in range(2 * GROUPS):
                    for hh in range(2):
                        split((2 * n) % RING, NB, hh, it * (4 * GROUPS) + (h1 + 2 * n + hh), it * 64 + (n1 + 16 * (2 * n // RING)))
                    ada_turn(4, 2 * n + 1, it * 64 + (n1 + 16 * ((2 * n + 1) // RING)), it * (2 * GROUPS) + n,
                             it * (2 * GROUPS) + (4 * KT + n))
                    if n % GROUPS == GROUPS - 1:
                        c = n // GROUPS
                        dve.wait_ge(halves_done, it * (4 * GROUPS) + (h1 + 2 * GROUPS * (c + 1)))
                        dve.wait_ge(a_ysq, it * 4 + 2 * (c + 1))
                        cols = bass.ds(it * (2 * NB) + c * NB, NB)
                        for t in range(TT):
                            ins = dve.tensor_tensor(y[:, t, cols], gps[(NCH + c) % 2][:, t, :], grow[:, cols], ALU.mult)
                        ins.then_inc(gemm_free[(NCH + c) % 2], 1)
            dve.tensor_reduce(st[:, 48:50], yss[:, :, :], AX, ALU.add).then_inc(v_ysum, 1)
            dve.wait_ge(ada_used, 5 * KT)
            dve.sem_inc(acc_full, 1)

            wait_chunk_taken(dve, NCH + 2)
            wait_chunk_taken(dve, NCH + 3)
            dve.wait_ge(a_yr, 1)
            dve.wait_ge(xr_in, 16)
            for t in range(TT):
                dve.scalar_tensor_tensor(out=x1[:, t, :], in0=y[:, t, :], scalar=st[:, 48 + t:49 + t], in1=x1[:, t, :],
                                         op0=ALU.mult, op1=ALU.add).then_inc(v_x1, 1)
            stage("mod4")
            for t in range(TT):
                dve.wait_ge(a_x1r, t + 1)
                dve.tensor_scalar(y[:, t, :], x1[:, t, :], st[:, 52 + t:53 + t], None, ALU.mult).then_inc(v_x1n, 1)
            for j in range(8):
                dve.wait_ge(h2_hi, j + 1)
                ks = slice(2 * j, 2 * j + 2)
                lower(hlo[:, ks, :], hful[:, j % 2], hhi[:, ks, :]).then_inc(h2_lo, 1)

            h2 = h1 + 8 * GROUPS
            n2 = n1 + 128
            dve.wait_ge(y_zero, 1)
            dve.wait_ge(acc_seed[1], 16 * 3)
            with dve.Fori(0, QUARTERS) as q:
                def down(c):
                    ci = NCH + 4 + c
                    dve.wait_ge(halves_done, q * (16 * GROUPS) + (h2 + 2 * GROUPS * (c + 1)))
                    d = y[:, :, (c - 4) * NB:(c - 3) * NB]
                    dve.tensor_tensor(d, d, gps[ci % 2][:, :, :], ALU.add).then_inc(gemm_free[ci % 2], 1)
                for c in range(8):
                    for g in range(GROUPS):
                        i = c * GROUPS + g
                        pos = MLP_POS["w", i]
                        per_turn = 4 * len(MLP_ITEMS)
                        for hh in range(2):
                            split(pos % RING, NB, hh, q * (16 * GROUPS) + (h2 + 2 * i + hh), q * per_turn + (n2 + 16 * (pos // RING)))
                        if g == 1 and c < 4:
                            pos = MLP_POS["ada", c]
                            ada_turn(5, pos, q * per_turn + (n2 + 16 * (pos // RING)), q * 4 + c, q * 4 + (5 * KT + c))
                        if g == 0 and 1 <= c <= 4:
                            ci = NCH + 4 + c - 1
                            dve.wait_ge(gemm_free[ci % 2], q * 4 + (ci // 2 + 1))
                            r = rst[:, (c - 1) % 2]
                            dve.tensor_tensor(r, r, r, ALU.mult).then_inc(v_sq, 1)
                        if g == 0 and c >= 5:
                            down(c - 1)
                        if g == 2 and 1 <= c <= 4:
                            for i2 in range(2):
                                f = 2 * (c - 1) + i2
                                dve.wait_ge(act_hi, q * 8 + (f + 1))
                                ks = slice(2 * f, 2 * f + 2)
                                b = mlp_fill(f)[0]
                                lower(alo[:, ks, :], mx[b][:, :].rearrange("p (k n) -> p k n", k=2), ahi[:, ks, :])\
                                    .then_inc(bank_free[b], 1)
                down(7)
            dve.wait_ge(ada_used, 6 * KT)
            dve.sem_inc(acc_full, 1)

            for j in range(4):
                b, n = mlp_fill(8 * QUARTERS + j)
                dve.wait_ge(bank_full[b], n + 1)
                step(gate_rows(j, mx[b], 32))
            for t in range(TT):
                dve.wait_ge(a_yss, t + 1)
                step(dve.scalar_tensor_tensor(out=y[:, t, :], in0=y[:, t, :], scalar=st[:, 56 + t:57 + t], in1=grow[:, :],
                                              op0=ALU.mult, op1=ALU.mult))
                dve.tensor_tensor(y[:, t, :], x1[:, t, :], y[:, t, :], ALU.add).then_inc(v_out, 1)


_INS = ['x', 'c', 'positions', 'ada_w', 'ada_b', 'norm_pre_mix', 'norm_post_mix', 'norm_pre_mlp', 'norm_post_mlp',
        'w_in', 'w_out', 'gdn_conv_w', 'gdn_a_log', 'gdn_dt_bias', 'gdn_norm_w', 'ssm_conv_w', 'ssm_conv_b',
        'ssm_a_log', 'ssm_dt_bias', 'ssm_d', 'ssm_norm_w', 'attn_sinks', 'sc_conv_w', 'w_up', 'w_down']


def shape_constants():
    import numpy as np
    i = np.arange(P)
    r, c = i[:, None], i[None, :]
    same = (r // 64) == (c // 64)
    m = np.zeros((NCONST, P, P), np.float32)
    m[IDENT] = r == c
    m[UINC] = r <= c
    m[UINCB] = (r <= c) & same
    m[SGT] = r > c
    m[SGTB] = (r > c) & same
    m[CH0] = r < 64
    m[CH1] = r >= 64
    for lv in range(6):
        s = 2 ** lv
        m[LV0 + lv] = ((r // (2 * s)) == (c // (2 * s))) & ((r // s) % 2 == 1) & ((c // s) % 2 == 0)
    m[ONES] = 1
    m[AMP] = np.where(c > r, 0, -1e30)
    m[AMC] = np.where(c <= r, 0, -1e30)
    e = np.arange(0, HD, 2, dtype=np.float32) / np.float32(HD)
    return np.ascontiguousarray(m.transpose(1, 0, 2).reshape(P, NCONST * P)), np.power(np.float32(10000.0), -e).astype(np.float32)


def kernel(**inputs):
    import numpy as _np
    import concourse.bacc as _bacc
    from concourse import mybir as _mybir
    from concourse.bass_utils import run_bass_kernel_spmd as _run

    nc = _bacc.Bacc("TRN2", target_bir_lowering=False, num_devices=1)
    arrays = {name: _np.ascontiguousarray(inputs[name]) for name in _INS}
    arrays["consts"], arrays["inv_freq"] = shape_constants()
    aps = {}
    for name, value in arrays.items():
        aps[name] = nc.dram_tensor(name, value.shape, _mybir.dt.from_np(value.dtype), kind="ExternalInput").ap()
    aps["out"] = nc.dram_tensor("out", (1, SEQ, D), F32, kind="ExternalOutput").ap()
    build(nc, aps)
    r = _run(nc, [arrays], core_ids=[0])
    return r.results[0]["out"]
```

```python
from contextlib import ExitStack

import concourse.bass as bass
from concourse import mybir

F32 = mybir.dt.float32
F32R = mybir.dt.float32r
I32 = mybir.dt.int32
ALU = mybir.AluOpType
ACT = mybir.ActivationFunctionType
AX = mybir.AxisListType.X

P = 128
SEQ = 256
TT = SEQ // P
D = 2048
KT = D // P
GW = D // 4
H = 4
SH = 8
QH = 8
HD = 64
HIDDEN = 4 * D
QUARTERS = HIDDEN // D
IN_WIDTH = 5904
NB = 512
EPS = 1e-6
GK = 4
GROUPS = KT // GK
RING = 4
AHEAD = 4
PARTS = 6
ADA_COLS = 2048

(IDENT, UINC, UINCB, SGT, SGTB, CH0, CH1, LV0, LV1, LV2, LV3, LV4, LV5, ONES, AMP, AMC) = range(16)
NCONST = 16
SUM_MASKS = (UINC, UINCB, SGT, SGTB, CH0, CH1)
CS_SSM, CS_GDN, REST_SSM, REST_GDN, TOT0, TOT1 = range(6)

P_DTB, P_ALOG, P_SD, P_SINK, P_FREQ, P_COLS = 0, 12, 24, 32, 40, 72

VA_C, VA_PRE_MIX, VA_PRE_MLP, VA_CONVB, VA_SC, VA_SSMN, VA_GDNN, VA_ROWS = 0, 16, 32, 48, 56, 68, 72, 73
VB_GDN, VB_SSM, VB_ROWS = 0, 48, 80

ROWS = [("c", 0, VA_C, KT), ("norm_pre_mix", 0, VA_PRE_MIX, KT), ("norm_pre_mlp", 0, VA_PRE_MLP, KT),
        ("ssm_conv_b", 0, VA_CONVB, 8), ("sc_conv_w", 0, VA_SC, 12), ("ssm_norm_w", 0, VA_SSMN, 4),
        ("gdn_norm_w", 0, VA_GDNN, 1), ("gdn_conv_w", 1, VB_GDN, 48), ("ssm_conv_w", 1, VB_SSM, 32)]
NVROWS = len(ROWS)
PRM = [("gdn_dt_bias", P_DTB, 4), ("ssm_dt_bias", P_DTB + 4, 8), ("gdn_a_log", P_ALOG, 4),
       ("ssm_a_log", P_ALOG + 4, 8), ("ssm_d", P_SD, 8), ("attn_sinks", P_SINK, 8), ("inv_freq", P_FREQ, 32)]
CHUNKS = [
    ("gz", 1536, 512), ("gk", 512, 512), ("gq", 0, 512), ("s1", 2048, 260), ("a1", 3592, 388),
    ("gv", 1024, 512), ("xbc0", 2568, 512), ("xbc1", 3080, 512), ("s2", 2308, 260), ("a2", 3980, 388),
    ("cc", 4880, 512), ("ch", 5392, 512), ("cb", 4368, 512),
]
CHUNK = {name: i for i, (name, _, _) in enumerate(CHUNKS)}
NCH = len(CHUNKS)
SPLIT_AFTER = ["gdn_out", "ssm_out", "att_out", "mul_cb"]
FIRST = 3
T_B, T_A, T_SZ, T_DT, T_AQ, T_AK, T_AV, T_GZ, T_COLS = 0, 4, 8, 520, 528, 1040, 1168, 1296, 1808
TM_AT = {"s1": 0, "s2": 260, "a1": 520, "a2": 908, "gz": T_GZ}
CONV = {"gk": (4, 4), "gq": (0, 0), "gv": (8, 8), "xbc0": (12, 0), "xbc1": (16, 4)}
CONV_ORDER = ["gk", "gq", "gv", "xbc0", "xbc1"]
STAGED = ["gk", "gq", "gv", "xbc0", "xbc1", "cc", "cb"]
STG_OF = {"gk": 0, "gq": 1, "gv": 0, "xbc0": 1, "xbc1": 0, "cc": 1, "cb": 0}

SEGS = [0, 1, 3, 2, 4, 5]

W_GROUPS = NCH * GROUPS
SLOTS = 2 * W_GROUPS
HALVES = [(c, g, hh) for g in range(GROUPS) for c in range(FIRST) for hh in range(2)] + \
         [(c, g, hh) for c in range(FIRST, NCH) for g in range(GROUPS) for hh in range(2)]
H_OF = {half: h for h, half in enumerate(HALVES)}


TWO_PI = 6.283185307179586
PI2_A, PI2_B = 6.28125, 0.0019340515136718750
PI2_C = TWO_PI - PI2_A - PI2_B
PI_LOW = 3.1415925


def att_part(f):
    if f < 2:
        return 0, list(range(4 * f, 4 * f + 4)), [0]
    return 1, list(range(2 * (f - 2), 2 * (f - 2) + 2)), [0, 1]


def stream_plan():
    items = [("part", 0, j) for j in range(2 * GROUPS)]
    for q in range(GROUPS):
        for c in range(FIRST):
            items.append(("w", c, q))
            if q + 1 < GROUPS:
                items += [("part", q + 1, j) for j in range(2 * c, 2 * c + (4 if c == FIRST - 1 else 2))]
    rest = [("ada", a, k) for a in (2, 3) for k in range(KT)] + [("ada", 4, k) for k in range(KT // 4)]
    for g in range(FIRST * GROUPS, W_GROUPS):
        items.append(("w", g // GROUPS, g % GROUPS))
        if rest:
            items.append(rest.pop(0))
    rest += [("ada", 4, k) for k in range(KT // 4, KT)]
    for n in range(4 * GROUPS):
        items.append(("out", n // GROUPS, n % GROUPS))
        if n < 12:
            items.append(rest.pop(0))
    assert not rest
    return items


STREAM = stream_plan()
RINGED = [item for item in STREAM if item[0] != "part"]
POS_OF = {item: pos for pos, item in enumerate(RINGED)}
N_RINGED = len(RINGED)
assert N_RINGED % RING == 0 and all(item[0] == "out" for item in RINGED[-RING:])


def part_steps(q, j):
    return (q * GROUPS + j // 2) * 2 * GK + 2 * GK - 1 + j % 2


def pair_of(ci):
    return (ci, 0) if ci < FIRST else ((ci - 1) % 2, (ci - 1) // 2)


def schedule():
    s = {h: [] for h in range(SLOTS)}

    def at(h, *names):
        s[h].extend(names)
    at(24, "conv_gk")
    at(26, "silu_gk")
    at(27, "tm_k", "conv_gq")
    at(29, "silu_gq", "tm_q")
    at(33, "l2stat", "l2scale")
    at(36, "kqT")
    at(39, "softplus", "softplus_u")
    at(42, "softplus_log")
    at(45, "sums", "decay0")
    at(46, "decay1")
    at(48, "kk", "qk", "lv0", "conv_gv", "invY1")
    at(50, "invX1")
    at(51, "silu_gv", "invY2")
    at(52, "invX2")
    at(53, "tm_v", "invY3")
    at(54, "invX3", "kbg", "silu_gz", "qdT", "invY4", "invX4", "angles", "invY5", "invX5", "uw", "gdn_v0")
    at(55, "gdn_s0")
    at(57, "gdn_v1", "conv_xbc0")
    at(58, "gdn_s1")
    at(59, "gdn_o0")
    at(61, "mod2", "gdn_v2", "gdn_s2", "silu_xbc0")
    at(62, "gdn_v3")
    at(63, "gdn_o1")
    at(64, "gdn_gate", "conv_xbc1")
    at(65, "gdn_out")
    at(66, "silu_xbc1")
    at(67, "ssm_tm")
    at(68, "ssm_cb")
    at(70, "ssm_e0", "ssm_s")
    at(71, "ssm_e1", "ssm_o")
    at(72, "ssm_y0", "ssm_e2", "silu_sz")
    at(74, "ssm_y1", "ssm_e3")
    at(75, "ssm_y2")
    at(76, "ssm_y3")
    at(78, "ssm_gate")
    at(81, "ssm_out", "rope")
    at(85, "att_T", "att_s0", "att_s1")
    at(86, "att_t0")
    at(87, "att_v0", "split0", "att_s2")
    at(88, "att_t1")
    at(90, "att_v1", "att_s3")
    at(93, "att_t2", "split1")
    at(96, "att_v2", "att_s4", "att_t3")
    at(99, "att_v3", "att_s5", "att_t4", "conv_cc")
    at(101, "att_v4", "att_t5")
    at(102, "att_v5")
    at(103, "att_out", "split2", "mul_cb", "split3")
    return [s[h] for h in range(SLOTS)]


SCHEDULE = schedule()


def with_moves(h):
    ci, g, hh = HALVES[h]
    return ([f"evac{ci}"] if g == GROUPS - 1 and hh == 1 else []) + SCHEDULE[h]

FILLS = {
    "conv_gq": 2, "conv_gk": 2, "conv_gv": 2, "conv_xbc0": 2, "conv_xbc1": 2, "conv_cc": 2, "mul_cb": 2,
    **{f"part{q}": 1 for q in range(GROUPS)}, "mod2": 1, "mod4": 1, "sums": 1, "decay0": 2, "decay1": 2,
    "tm_q": 2, "tm_k": 2, "tm_v": 2, "kqT": 4, "kk": 2, "qk": 2, "lv0": 2,
    "invY1": 2, "invY2": 2, "invY3": 2, "invY4": 2, "invY5": 2,
    "invX1": 4, "invX2": 4, "invX3": 4, "invX4": 4, "invX5": 2,
    "qdT": 2, "uw": 4, "gdn_v0": 0, "gdn_v1": 2, "gdn_v2": 2, "gdn_v3": 2,
    "gdn_s0": 1, "gdn_s1": 1, "gdn_s2": 1, "gdn_o0": 1, "gdn_o1": 1, "gdn_out": 2,
    "ssm_tm": 3, "ssm_cb": 1, "ssm_s": 1, "ssm_o": 1, **{f"ssm_e{i}": 1 for i in range(4)},
    **{f"ssm_y{i}": 1 for i in range(4)}, "ssm_out": 2, "att_T": 4,
    **{f"att_{part}{f}": 1 for part in "stv" for f in range(6)}, "att_out": 2, "r2": 1, "vecT": 1, "xT": 8, "gate_a": 4, "h2Ta": 3, "h2Tb": 5,
}
START = ["vecT", "xT"] + [f"part{q}" for q in range(GROUPS)]
ORDER = [n for slot in SCHEDULE for n in slot] + ["gate_a", "mod4", "h2Ta", "r2", "h2Tb"]


def fill_plan():
    at, n = {}, 0
    for name in START:
        for i in range(FILLS[name]):
            at[name, i] = (n % 2, n // 2)
            n += 1
    before = [-(-n // 2), n // 2, 0, 0]
    n = 0
    for name in ORDER:
        for i in range(FILLS.get(name, 0)):
            at[name, i] = (n % 4, n // 4 + before[n % 4])
            n += 1
    return at, n, before


FILL_AT, NFILLS, FILLS_BEFORE = fill_plan()


MLP_ITEMS = []
for c_ in range(8):
    for g_ in range(GROUPS):
        MLP_ITEMS.append(("w", c_ * GROUPS + g_))
        if 1 <= c_ <= 4 and g_ == 1:
            MLP_ITEMS.append(("ada", c_ - 1))
assert len(MLP_ITEMS) % RING == 0
MLP_POS = {item: i for i, item in enumerate(MLP_ITEMS)}


def mlp_back(i):
    kind, n = MLP_ITEMS[(i - RING) % len(MLP_ITEMS)]
    return kind, n, int(i < RING)


def h2T(j):
    return ("h2Ta", j) if j < 3 else ("h2Tb", j - 3)


def mlp_fill(f):
    b = (NFILLS + f) % 4
    return b, (NFILLS + f) // 4 + FILLS_BEFORE[b]


def fill_of(name, i):
    return FILL_AT[name, i]


def build(nc, a):
    with ExitStack() as ctx:
        cursor = [nc.sbuf_base + (-nc.sbuf_base) % 64]

        def place(name, shape, dt, offset):
            return nc.alloc_sbuf_tensor_at(name, shape, dt, offset=offset)

        def sb(name, shape, dt=F32):
            size = 4
            for n in shape[1:]:
                size *= n
            t = place(name, shape, dt, cursor[0])
            cursor[0] += size + (-size) % 64
            return t

        def sem(name):
            return ctx.enter_context(nc.semaphore(name))

        cst = sb("cst", [P, NCONST, P])
        vcol = sb("vcol", [P, 2, P])
        prm = sb("prm", [P, P_COLS])
        epsc = sb("epsc", [P, 2])
        cact = sb("cact", [P, KT])
        modc = sb("modc", [P, 4, KT])
        st = sb("st", [P, 64])
        yss = sb("yss", [P, TT, 4])
        trig = sb("trig", [P, 2, TT, 32])
        posi = sb("posi", [P, TT], I32)
        posf = sb("posf", [P, TT])
        ang = sb("ang", [P, 4, TT, 32])
        angi = sb("angi", [P, TT, 32], I32)
        raw = sb("raw", [P, RING, GK * NB])
        whi = sb("whi", [P, AHEAD, 2, NB], F32R)
        wlo = sb("wlo", [P, AHEAD, 2, NB], F32R)
        hhi = sb("hhi", [P, KT, SEQ], F32R)
        hlo = sb("hlo", [P, KT, SEQ], F32R)
        acc = sb("acc", [P, 2, ADA_COLS])
        base = cursor[0]

        def zone(start):
            at = [start]

            def take(name, shape, dt=F32):
                size = 4
                for n in shape[1:]:
                    size *= n
                t = place(name, shape, dt, at[0])
                at[0] += size + (-size) % 64
                assert at[0] <= nc.sbuf_usable_end, (name, at[0])
                return t
            take.at = at
            return take
        z0 = zone(base)
        x0 = z0("x0", [P, TT, D])
        part = z0("part", [P, PARTS, GK * NB])
        xT = z0("xT", [P, KT, SEQ])
        vrow = z0("vrow", [P, 2, P])

        z1 = zone(base)
        mixT = z1("mixT", [P, KT, SEQ])
        stg = z1("stg", [P, 2, TT, NB])
        ptm = z1("ptm", [P, TT, T_COLS])
        cvo = z1("cvo", [P, 20, SEQ])
        dec = z1("dec", [P, 10, TT, 12])
        sums = z1("sums", [P, len(SUM_MASKS), TT, 12])
        shared = z1.at[0]
        tm = z1("tm", [P, 3, TT, H, P])
        Dm = z1("Dm", [P, TT, H, P])
        Dt = z1("Dt", [P, TT, H, P])
        Cm = z1("Cm", [P, TT, H, P])
        Xm = z1("Xm", [P, TT, H, P])
        Xt = z1("Xt", [P, TT, H, P])
        Ym = z1("Ym", [P, TT, H, P])
        Sm = z1("Sm", [P, H, P])
        qnT = cvo[:, 0:4, :].rearrange("p j (t n) -> p (j t n)", t=TT).rearrange("p (t h n) -> p t h n", t=TT, h=H)
        knT = cvo[:, 4:8, :].rearrange("p j (t n) -> p (j t n)", t=TT).rearrange("p (t h n) -> p t h n", t=TT, h=H)
        kbg = cvo[:, 8:12, :].rearrange("p j (t n) -> p (j t n)", t=TT).rearrange("p (t h n) -> p t h n", t=TT, h=H)
        qdT = qnT
        U, WT, O, VZ = Xm, Dm, Ym, Cm

        z2 = zone(shared)
        xs = z2("xs", [P, TT, GW])
        xdt = z2("xdt", [P, TT, SH, HD])
        xdd = z2("xdd", [P, SH, HD])
        btm = z2("btm", [P, 2, P])
        CBm = z2("CBm", [P, 4, P])
        M1s = z2("M1s", [P, 2, 4, P])
        Es = z2("Es", [P, 2, 4, P])
        stt_ = z2("stt_", [P, 2, SEQ])
        yb = z2("yb", [P, TT, GW])
        ytmp = z2("ytmp", [P, TT, GW])
        assert z2.at[0] - shared <= z1.at[0] - shared
        z3 = zone(shared)
        rq = z3("rq", [P, TT, 10, HD])
        rtmp = z3("rtmp", [P, 2, TT, 10, 32])
        kz = z3("kz", [P, TT, 2, 2, P])
        qT2 = z3("qT2", [P, TT, 4, P])
        kzT = z3("kzT", [P, 4, SEQ])
        sc = z3("sc", [P, 2, NB])
        PT = z3("PT", [P, 2, 4, P])
        ats = z3("ats", [P, 6, 16])
        yc = z3("yc", [P, TT, GW])

        z4 = zone(base)
        x1 = z4("x1", [P, TT, D])
        y = z4("y", [P, TT, D])
        grow = z4("grow", [P, D])
        ahi = z4("ahi", [P, KT, SEQ], F32R)
        alo = z4("alo", [P, KT, SEQ], F32R)
        hful = z4("hful", [P, 2, 2, SEQ])
        rst = z4("rst", [P, 2, TT, NB])
        rdiag = z4("rdiag", [P, TT, P])
        rrow = z4("rrow", [P, SEQ])

        gps = [ctx.enter_context(nc.psum_tensor(f"gps{i}", [P, TT, NB], F32)) for i in range(2)]
        mx = [ctx.enter_context(nc.psum_tensor(f"mx{i}", [P, NB], F32)) for i in range(4)]

        raw_in = [sem(f"raw_in{i}") for i in range(RING)]
        part_in = [sem(f"part_in{i}") for i in range(PARTS)]
        slot_claimed = sem("slot_claimed")
        ada_part_step = sem("ada_part_step")
        ada_used = sem("ada_used")
        hi_ready = sem("hi_ready")
        lo_ready = sem("lo_ready")
        halves_done = sem("halves_done")
        gemm_free = [sem(f"gemm_free{i}") for i in range(3)]
        bank_full = [sem(f"bank_full{i}") for i in range(4)]
        bank_free = [sem(f"bank_free{i}") for i in range(4)]
        cst_in, vrow_in, prm_in, x_in, pos_in = (sem(n) for n in ("cst_in", "vrow_in", "prm_in", "x_in", "pos_in"))
        rows_zero = sem("rows_zero")
        acc_zero = sem("acc_zero")
        acc_seed = [sem(f"acc_seed{i}") for i in range(2)]
        acc_full = sem("acc_full")
        vec_step = sem("vec_step")
        act_step = sem("act_step")
        pool_step = sem("pool_step")
        gdn_squared = sem("gdn_squared")
        ssm_gated_raw = sem("ssm_gated_raw")
        ssm_squared = sem("ssm_squared")
        eps_set = sem("eps_set")
        x_root_ready = sem("x_root_ready")
        x_normed = sem("x_normed")
        silu_c_ready = sem("silu_c_ready")
        h_ready = sem("h_ready")
        h_hi_ready = sem("h_hi_ready")
        h_lo_ready = sem("h_lo_ready")
        last_tap_ready = sem("last_tap_ready")
        silu_done = sem("silu_done")
        log_decay_step = sem("log_decay_step")
        softplus_exp_step = sem("softplus_exp_step")
        gdn_decay_spread = sem("gdn_decay_spread")
        decay_masked = sem("decay_masked")
        kbg_factor_ready = sem("kbg_factor_ready")
        l2_sums_ready = sem("l2_sums_ready")
        l2_root_ready = sem("l2_root_ready")
        qk_normed = sem("qk_normed")
        kbg_ready = sem("kbg_ready")
        qk_decayed = sem("qk_decayed")
        level_ready = sem("level_ready")
        inverse_ready = sem("inverse_ready")
        vz_zeroed = sem("vz_zeroed")
        v_new_ready = sem("v_new_ready")
        gdn_squares_ready = sem("gdn_squares_ready")
        gdn_root_ready = sem("gdn_root_ready")
        gz_silu_ready = sem("gz_silu_ready")
        gdn_gated = sem("gdn_gated")
        xdt_ready = sem("xdt_ready")
        ssm_decay_spread = sem("ssm_decay_spread")
        ssm_weights_ready = sem("ssm_weights_ready")
        ssm_squares_ready = sem("ssm_squares_ready")
        ssm_root_ready = sem("ssm_root_ready")
        sz_silu_ready = sem("sz_silu_ready")
        ssm_gated = sem("ssm_gated")
        angles_ready = sem("angles_ready")
        trig_ready = sem("trig_ready")
        rope_done = sem("rope_done")
        sink_ready = sem("sink_ready")
        probs_ready = sem("probs_ready")
        mix_hi = sem("mix_hi")
        mix_lo = sem("mix_lo")
        x_again_in = sem("x_again_in")
        norm_row_in = sem("norm_row_in")
        y_squared = sem("y_squared")
        y_sums_ready = sem("y_sums_ready")
        y_root_ready = sem("y_root_ready")
        x1_ready = sem("x1_ready")
        x1_squared = sem("x1_squared")
        x1_sums_ready = sem("x1_sums_ready")
        x1_root_ready = sem("x1_root_ready")
        rdiag_ready = sem("rdiag_ready")
        x1T_scaled = sem("x1T_scaled")
        h2_hi = sem("h2_hi")
        h2_lo = sem("h2_lo")
        y_zero = sem("y_zero")
        relu_squared = sem("relu_squared")
        act_hi_ready = sem("act_hi_ready")
        y_chunk_ready = sem("y_chunk_ready")
        out_ready = sem("out_ready")
        out_done = sem("out_done")

        block = ctx.enter_context(nc.Block())

        def tap_col(c, tap, j):
            row = (VB_GDN + tap * 12 if c[0] == "g" else VB_SSM + tap * 8) + CONV[c][1] + j
            return vcol[:, 1, row:row + 1]

        def c_(i):
            return cst[:, i, :]

        def over_heads(ap, n=H):
            return ap.unsqueeze(1).broadcast_to([P, n, ap.shape[1]])

        def over_cols(ap, n):
            return ap.unsqueeze(2).broadcast_to([P, ap.shape[1], n])

        def wait_chunk_taken(eng, ci):
            pair, before = pair_of(ci)
            eng.wait_ge(gemm_free[pair], before + 1)

        def sums_of(ci, w):
            if ci == 2:
                return [mx[2][:, 0:w], mx[3][:, 0:w]]
            b = gps[pair_of(ci)[0]]
            return [b[:, t, 0:w] for t in range(TT)]

        def wait_full(eng, name, i):
            b, n = fill_of(name, i)
            eng.wait_ge(bank_full[b], n + 1)
            return mx[b]

        def wait_taken(eng, name, i):
            b, n = fill_of(name, i)
            eng.wait_ge(bank_free[b], n + 1)

        def taken(ins, name, i):
            ins.then_inc(bank_free[fill_of(name, i)[0]], 1)

        def slab(b, n=4):
            return b[:, :].rearrange("p (h n) -> p h n", h=n)

        ada_v = a["ada_w"][0].rearrange("(k p) n -> k p n", p=P)
        adag_v = a["ada_w"][0].rearrange("(g k p) n -> g p k n", k=GK, p=P)
        adab_v = a["ada_b"]
        win_v = a["w_in"][0].rearrange("(g k p) n -> g p k n", k=GK, p=P)
        wout_v = a["w_out"][0].rearrange("(g k p) n -> g p k n", k=GK, p=P)
        wup_v = a["w_up"][0].rearrange("(g k p) n -> g p k n", k=GK, p=P)
        wdn_v = a["w_down"][0].rearrange("(q g k p) n -> q g p k n", q=QUARTERS, k=GK, p=P)
        x_v = a["x"][0].rearrange("(t p) n -> p t n", p=P)
        out_v = a["out"][0].rearrange("(t p) n -> p t n", p=P)

        @block.sync
        def _(sp):
            sp.dma_start(cst[:, :, :], a["consts"].rearrange("p (c n) -> p c n", n=P)).then_inc(cst_in, 16)

            def slot(i):
                return raw[:, i, :].rearrange("p (k n) -> p k n", k=GK)

            def seed(n):
                sp.wait_ge(acc_zero, n + 1)
                s0 = SEGS[n] * ADA_COLS
                sp.dma_start(acc[0:1, n % 2, :], adab_v[:, s0:s0 + ADA_COLS]).then_inc(acc_seed[n % 2], 16)

            seed(0)
            seed(1)
            for item in STREAM:
                kind, i, j = item
                if kind == "part":
                    n = i * 2 * GROUPS + j
                    if n == 2:
                        sp.dma_start(x0[:, :, :], x_v).then_inc(x_in, 16)
                    if n >= PARTS:
                        sp.wait_ge(ada_part_step, part_steps(*divmod(n - PARTS, 2 * GROUPS)))
                    c0 = SEGS[j % 2] * ADA_COLS + i * NB
                    sp.dma_start(part[:, n % PARTS, :].rearrange("p (k n) -> p k n", k=GK),
                                 adag_v[j // 2, :, :, c0:c0 + NB]).then_inc(part_in[n % PARTS], 16)
                    continue
                pos = POS_OF[item]
                if kind == "ada" and j == 0:
                    seed(i)
                if pos >= RING:
                    last, n, m = RINGED[pos - RING]
                    if last == "ada":
                        sp.wait_ge(ada_used, (n - 2) * KT + m + 1)
                    elif last == "w":
                        sp.wait_ge(lo_ready, H_OF[n, m, 1] + 1)
                    else:
                        sp.wait_ge(lo_ready, SLOTS + 2 * (n * GROUPS + m + 1))
                if kind == "ada":
                    s0 = SEGS[i] * ADA_COLS
                    sp.dma_start(raw[:, pos % RING, :], ada_v[j, :, s0:s0 + ADA_COLS]).then_inc(raw_in[pos % RING], 16)
                elif kind == "out":
                    sp.dma_start(slot(pos % RING), wout_v[j, :, :, i * NB:(i + 1) * NB]).then_inc(raw_in[pos % RING], 16)
                else:
                    _, c0, w = CHUNKS[i]
                    sp.dma_start(slot(pos % RING)[:, :, 0:w], win_v[j, :, :, c0:c0 + w]).then_inc(raw_in[pos % RING], 16)

            h2 = SLOTS + 8 * GROUPS
            s5 = SEGS[5] * ADA_COLS
            seed(5)
            with sp.Fori(0, QUARTERS) as q:
                for i, (kind, n) in enumerate(MLP_ITEMS):
                    back_kind, back, turns_back = mlp_back(i)
                    if back_kind == "w":
                        split_before = sp.snap(q * (16 * GROUPS) + (h2 + 2 * (back + 1) - turns_back * 16 * GROUPS))
                        sp.wait_ge(lo_ready, split_before)
                    else:
                        used_before = sp.snap(q * 4 + (3 * KT + back + 1 - turns_back * 4))
                        sp.wait_ge(ada_used, used_before)
                    sp.sem_inc(slot_claimed, 1)
                    if kind == "w":
                        c, g = divmod(n, GROUPS)
                        if c < 4:
                            src = wup_v[g, :, :, bass.ds(q * D + c * NB, NB)]
                        else:
                            src = wdn_v[bass.ds(q, 1), g, :, :, (c - 4) * NB:(c - 3) * NB]\
                                .rearrange("o p k n -> p (o k) n")
                        sp.dma_start(slot(i % RING), src).then_inc(raw_in[i % RING], 16)
                    else:
                        sp.dma_start(raw[:, i % RING, :],
                                     ada_v[bass.ds(q * 4 + n, 1), :, s5:s5 + ADA_COLS].rearrange("o p n -> p (o n)"))\
                            .then_inc(raw_in[i % RING], 16)
            for n in range(2 * TT):
                m, cols = n // 2, slice(n % 2 * (D // 2), (n % 2 + 1) * (D // 2))
                sp.wait_ge(out_ready, n + 1)
                sp.dma_start(out_v[:, m, cols], y[:, m, cols]).then_inc(out_done, 16)
            sp.wait_ge(out_done, 16 * 2 * TT)

        @block.tensor
        def _(pe):
            def fill(name, i):
                b, n = fill_of(name, i)
                if name in START and n == 0:
                    return mx[b]
                if n:
                    pe.wait_ge(bank_free[b], n)
                else:
                    wait_chunk_taken(pe, 2)
                return mx[b]

            def full(ins, name, i):
                ins.then_inc(bank_full[fill_of(name, i)[0]], 1)

            def half(psum, lhs_hi, lhs_lo, g, hh, w, buf, h):
                pe.wait_ge(lo_ready, h + 1)
                for kk in range(2):
                    k = g * GK + hh * 2 + kk
                    for m in range(TT):
                        o = psum[m]
                        xh = lhs_hi[:, k, m * P:(m + 1) * P]
                        xl = lhs_lo[:, k, m * P:(m + 1) * P]
                        first = g == 0 and hh == 0 and kk == 0
                        final = g == GROUPS - 1 and hh == 1 and kk == 1
                        pe.matmul(o, xh, whi[:, buf, kk, 0:w], start=first, stop=False)
                        pe.matmul(o, xh, wlo[:, buf, kk, 0:w], start=False, stop=False)
                        mm = pe.matmul(o, xl, whi[:, buf, kk, 0:w], start=False, stop=final)
                mm.then_inc(halves_done, 1)

            def stage(name):
                if name.startswith("conv_") or name == "mul_cb":
                    c = name.split("_")[1]
                    if c == "cc":
                        wait_chunk_taken(pe, CHUNK["ch"])
                        s = stg[:, 1]
                    else:
                        wait_chunk_taken(pe, CHUNK[c])
                        s = stg[:, STG_OF[c]]
                    for i in range(2):
                        b = fill(name, i)
                        for j in range(2):
                            for t in range(TT):
                                mm = pe.transpose(b[:, j * SEQ + t * P:j * SEQ + (t + 1) * P],
                                                  s[:, t, (2 * i + j) * P:(2 * i + j + 1) * P], c_(IDENT))
                        full(mm, name, i)
                elif name.startswith("mod"):
                    n = int(name[3])
                    pe.wait_ge(acc_full, n - 1)
                    b = fill(name, 0)
                    for k in range(KT):
                        mm = pe.matmul(b[:, k:k + 1], acc[:, n % 2, k * P:(k + 1) * P], cst[:, ONES, 0:1], start=True, stop=True)
                    full(mm, name, 0)
                elif name.startswith("part"):
                    q = int(name[4])
                    pe.wait_ge(ada_part_step, part_steps(q, 2 * GROUPS - 1))
                    b = fill(name, 0)
                    for i in range(2):
                        for k in range(GK):
                            mm = pe.matmul(b[:, i * GK + k:i * GK + k + 1], acc[:, i, (q * GK + k) * P:(q * GK + k + 1) * P],
                                           cst[:, ONES, 0:1], start=True, stop=True)
                    full(mm, name, 0)
                elif name == "sums":
                    pe.wait_ge(log_decay_step, 3)
                    b = fill(name, 0)
                    for i, m in enumerate(SUM_MASKS):
                        mm = pe.matmul(b[:, i * 24:(i + 1) * 24], c_(m), dec[:, 9, :, :].rearrange("p t n -> p (t n)"),
                                       start=True, stop=True)
                    full(mm, name, 0)
                elif name.startswith("decay"):
                    t = int(name[5])
                    pe.wait_ge(gdn_decay_spread, t + 1)
                    b = fill(name, 0)
                    mm = pe.matmul(b[:, :], c_(UINC), Cm[:, t].rearrange("p h n -> p (h n)"), start=True, stop=True)
                    full(mm, name, 0)
                    b = fill(name, 1)
                    for h in range(H):
                        mm = pe.matmul(b[:, h * P:(h + 1) * P], Cm[:, t, h, :], c_(UINC), start=True, stop=True)
                    full(mm, name, 1)
                elif name.startswith("tm_"):
                    w = "qkv".index(name[3])
                    pe.wait_ge(silu_done, CONV_ORDER.index("g" + name[3]) + 1)
                    for t in range(TT):
                        b = fill(name, t)
                        for h in range(H):
                            mm = pe.transpose(b[:, h * P:(h + 1) * P], cvo[:, w * 4 + h, t * P:(t + 1) * P], c_(IDENT))
                        full(mm, name, t)
                elif name == "kqT":
                    pe.wait_ge(qk_normed, 2)
                    for w in range(2):
                        for t in range(TT):
                            b = fill(name, w * 2 + t)
                            for h in range(H):
                                mm = pe.transpose(b[:, h * P:(h + 1) * P], tm[:, 1 - w, t, h, :], c_(IDENT))
                            full(mm, name, w * 2 + t)
                elif name in ("kk", "qk"):
                    for t in range(TT):
                        wait_taken(pe, "kqT", t)
                        wait_taken(pe, "kqT", 2 + t)
                        b = fill(name, t)
                        for h in range(H):
                            r = knT if name == "kk" else qnT
                            mm = pe.matmul(b[:, h * P:(h + 1) * P], knT[:, t, h, :], r[:, t, h, :], start=True, stop=True)
                        full(mm, name, t)
                elif name == "lv0":
                    for t in range(TT):
                        pe.wait_ge(level_ready, t + 1)
                        b = fill(name, t)
                        for h in range(H):
                            mm = pe.transpose(b[:, h * P:(h + 1) * P], Cm[:, t, h, :], c_(IDENT))
                        full(mm, name, t)
                elif name.startswith("invY"):
                    lv = int(name[4])
                    for t in range(TT):
                        pe.wait_ge(level_ready, 2 * lv + t + 1)
                        pe.wait_ge(inverse_ready, 2 * (lv - 1) + t + 1)
                        b = fill(name, t)
                        for h in range(H):
                            mm = pe.matmul(b[:, h * P:(h + 1) * P], Cm[:, t, h, :], Xt[:, t, h, :], start=True, stop=True)
                        full(mm, name, t)
                elif name.startswith("invX"):
                    lv = int(name[4])
                    for t in range(TT):
                        wait_taken(pe, f"invY{lv}", t)
                        b = fill(name, t)
                        for h in range(H):
                            mm = pe.matmul(b[:, h * P:(h + 1) * P], Xm[:, t, h, :], Ym[:, t, h, :], start=True, stop=True)
                        full(mm, name, t)
                    if lv < 5:
                        for t in range(TT):
                            b = fill(name, 2 + t)
                            for h in range(H):
                                mm = pe.matmul(b[:, h * P:(h + 1) * P], Ym[:, t, h, :], Xm[:, t, h, :], start=True, stop=True)
                            full(mm, name, 2 + t)
                elif name == "qdT":
                    for t in range(TT):
                        pe.wait_ge(qk_decayed, t + 1)
                        b = fill(name, t)
                        for h in range(H):
                            mm = pe.transpose(b[:, h * P:(h + 1) * P], tm[:, 0, t, h, :], c_(IDENT))
                        full(mm, name, t)
                elif name == "uw":
                    pe.wait_ge(kbg_ready, 1)
                    for t in range(TT):
                        pe.wait_ge(inverse_ready, 2 * 5 + t + 1)
                        wait_taken(pe, "tm_v", t)
                        b = fill(name, 2 * t)
                        for h in range(H):
                            mm = pe.matmul(b[:, h * P:(h + 1) * P], Xt[:, t, h, :], tm[:, 2, t, h, :], start=True, stop=True)
                        full(mm, name, 2 * t)
                        b = fill(name, 2 * t + 1)
                        for h in range(H):
                            mm = pe.matmul(b[:, h * P:(h + 1) * P], kbg[:, t, h, :], Xt[:, t, h, :], start=True, stop=True)
                        full(mm, name, 2 * t + 1)
                elif name.startswith("gdn_v"):
                    c = int(name[5])
                    if c:
                        t = c // 2
                        wait_taken(pe, f"gdn_s{c - 1}", 0)
                        wait_taken(pe, "uw", 2 * t + 1)
                        wait_taken(pe, "qdT", t)
                        for i, lhs in enumerate((WT, qdT)):
                            b = fill(name, i)
                            for h in range(H):
                                mm = pe.matmul(b[:, h * P:(h + 1) * P], lhs[:, t, h, :], Sm[:, h, :], start=True, stop=True)
                            full(mm, name, i)
                elif name.startswith("gdn_s"):
                    c = int(name[5])
                    pe.wait_ge(v_new_ready, c + 1)
                    pe.wait_ge(qk_decayed, TT + c // 2 + 1)
                    b = fill(name, 0)
                    for h in range(H):
                        mm = pe.matmul(b[:, h * P:(h + 1) * P], tm[:, 1, c // 2, h, :], VZ[:, c % 2, h, :], start=True, stop=True)
                    full(mm, name, 0)
                elif name in ("gdn_o0", "gdn_o1"):
                    t = int(name[5])
                    pe.wait_ge(v_new_ready, 2 * t + 2)
                    b = fill(name, 0)
                    for h in range(H):
                        for cc in range(2):
                            mm = pe.matmul(b[:, h * P:(h + 1) * P], Dt[:, t, h, :], VZ[:, cc, h, :], start=(cc == 0), stop=(cc == 1))
                    full(mm, name, 0)
                elif name == "gdn_out":
                    pe.wait_ge(gdn_gated, 1)
                    for t in range(TT):
                        b = fill(name, t)
                        for h in range(H):
                            mm = pe.transpose(b[:, h * P:(h + 1) * P], O[:, t, h, :], c_(IDENT))
                        full(mm, name, t)
                elif name == "ssm_tm":
                    pe.wait_ge(silu_done, 5)
                    for t in range(TT):
                        b = fill(name, t)
                        for j in range(4):
                            mm = pe.transpose(b[:, j * P:(j + 1) * P], cvo[:, 12 + j, t * P:(t + 1) * P], c_(IDENT))
                        full(mm, name, t)
                    b = fill(name, 2)
                    for g in range(2):
                        mm = pe.transpose(b[:, g * P:(g + 1) * P], cvo[:, 16 + g, 0:P], c_(IDENT))
                    full(mm, name, 2)
                elif name == "ssm_cb":
                    b = fill(name, 0)
                    for t in range(TT):
                        for g in range(2):
                            mm = pe.matmul(b[:, (t * 2 + g) * P:(t * 2 + g + 1) * P], cvo[:, 16 + g, t * P:(t + 1) * P],
                                           cvo[:, 18 + g, t * P:(t + 1) * P], start=True, stop=True)
                    full(mm, name, 0)
                elif name == "ssm_s":
                    pe.wait_ge(xdt_ready, 1)
                    wait_taken(pe, "ssm_tm", 2)
                    b = fill(name, 0)
                    for g in range(2):
                        mm = pe.matmul(b[:, g * SEQ:(g + 1) * SEQ], btm[:, g, :],
                                       xdd[:, 4 * g:4 * g + 4, :].rearrange("p h n -> p (h n)"), start=True, stop=True)
                    full(mm, name, 0)
                elif name == "ssm_o":
                    wait_taken(pe, "ssm_s", 0)
                    b = fill(name, 0)
                    for g in range(2):
                        mm = pe.matmul(b[:, g * SEQ:(g + 1) * SEQ], cvo[:, 18 + g, P:SEQ], stt_[:, g, :], start=True, stop=True)
                    full(mm, name, 0)
                elif name.startswith("ssm_e"):
                    i = int(name[5])
                    t, g = i // 2, i % 2
                    pe.wait_ge(ssm_decay_spread, i + 1)
                    b = fill(name, 0)
                    for h in range(4):
                        mm = pe.matmul(b[:, h * P:(h + 1) * P], M1s[:, i % 2, h, :], c_(UINC), start=True, stop=True)
                    full(mm, name, 0)
                elif name.startswith("ssm_y"):
                    i = int(name[5])
                    t, g = i // 2, i % 2
                    pe.wait_ge(ssm_weights_ready, i + 1)
                    b = fill(name, 0)
                    for h in range(4):
                        mm = pe.matmul(b[:, h * HD:(h + 1) * HD], Es[:, i % 2, h, :], xdt[:, t, g * 4 + h, :], start=True, stop=True)
                    full(mm, name, 0)
                elif name == "ssm_out":
                    pe.wait_ge(ssm_gated, 1)
                    for t in range(TT):
                        b = fill(name, t)
                        for j in range(4):
                            mm = pe.transpose(b[:, j * P:(j + 1) * P], yb[:, t, j * P:(j + 1) * P], c_(IDENT))
                        full(mm, name, t)
                elif name == "att_T":
                    pe.wait_ge(rope_done, 1)
                    for t in range(TT):
                        b = fill(name, t)
                        for j in range(4):
                            mm = pe.transpose(b[:, j * P:(j + 1) * P], rq[:, t, 2 * j:2 * j + 2, :].rearrange("p h n -> p (h n)"), c_(IDENT))
                        full(mm, name, t)
                    for t in range(TT):
                        b = fill(name, 2 + t)
                        for gz in range(4):
                            mm = pe.transpose(b[:, gz * P:(gz + 1) * P], kz[:, t, gz // 2, gz % 2, :], c_(IDENT))
                        full(mm, name, 2 + t)
                elif name.startswith("att_s"):
                    f = int(name[5])
                    n, heads, blocks = att_part(f)
                    if f == 0:
                        for i in range(4):
                            wait_taken(pe, "att_T", i)
                    w = len(blocks) * P
                    b = fill(name, 0)
                    for i, h in enumerate(heads):
                        g, z = h // 4, h % 2
                        mm = pe.matmul(b[:, i * w:(i + 1) * w], qT2[:, n, h // 2, :], kzT[:, g * 2 + z, blocks[0] * P:blocks[0] * P + w],
                                       start=True, stop=True)
                    full(mm, name, 0)
                elif name.startswith("att_t"):
                    f = int(name[5])
                    pe.wait_ge(probs_ready, f + 1)
                    b = fill(name, 0)
                    for i in range(4):
                        mm = pe.transpose(b[:, i * P:(i + 1) * P], sc[:, f % 2, i * P:(i + 1) * P], c_(IDENT))
                    full(mm, name, 0)
                elif name.startswith("att_v"):
                    f = int(name[5])
                    n, heads, blocks = att_part(f)
                    wait_taken(pe, f"att_t{f}", 0)
                    b = fill(name, 0)
                    for i, h in enumerate(heads):
                        for j, kb in enumerate(blocks):
                            mm = pe.matmul(b[:, i * HD:(i + 1) * HD], PT[:, f % 2, i * len(blocks) + j, :],
                                           ptm[:, kb, T_AV + (h // 4) * HD:T_AV + (h // 4 + 1) * HD],
                                           start=(j == 0), stop=(j == len(blocks) - 1))
                    full(mm, name, 0)
                elif name == "att_out":
                    wait_taken(pe, "att_v5", 0)
                    for t in range(TT):
                        b = fill(name, t)
                        for j in range(4):
                            mm = pe.transpose(b[:, j * P:(j + 1) * P], yc[:, t, j * P:(j + 1) * P], c_(IDENT))
                        full(mm, name, t)

            pe.wait_ge(cst_in, 16)
            pe.wait_ge(rows_zero, 1)
            pe.wait_ge(vrow_in, 16 * NVROWS)
            b = fill("vecT", 0)
            for i in range(2):
                mm = pe.transpose(b[:, i * P:(i + 1) * P], vrow[:, i, :], c_(IDENT))
            full(mm, "vecT", 0)
            pe.wait_ge(x_normed, TT)
            for j in range(8):
                b = fill("xT", j)
                for kk in range(2):
                    for t in range(TT):
                        k = 2 * j + kk
                        mm = pe.transpose(b[:, kk * SEQ + t * P:kk * SEQ + (t + 1) * P], x0[:, t, k * P:(k + 1) * P], c_(IDENT))
                full(mm, "xT", j)

            for h, (ci, gi, hh) in enumerate(HALVES):
                if gi == 0 and hh == 0 and ci >= FIRST:
                    pair, before = pair_of(ci)
                    pe.wait_ge(gemm_free[pair], before)
                if h == 0 or (ci, hh) == (2, 0) and gi + 1 < GROUPS:
                    stage(f"part{0 if h == 0 else gi + 1}")
                if ci == 0 and hh == 0:
                    pe.wait_ge(h_lo_ready, gi + 1)
                w = CHUNKS[ci][2]
                half(sums_of(ci, w), hhi, hlo, gi, hh, w, h % AHEAD, h)
                for name in SCHEDULE[h]:
                    stage(name)

            pe.wait_ge(acc_full, 2)
            for j in range(4):
                b = fill("gate_a", j)
                mm = pe.matmul(b[:, :], c_(ONES), acc[:, 1, j * NB:(j + 1) * NB], start=True, stop=True)
                full(mm, "gate_a", j)

            h1 = SLOTS
            with pe.Fori(0, 2) as it:
                for c in range(2):
                    pair, before = pair_of(NCH + c)
                    pe.wait_ge(gemm_free[pair], it + before)
                    for g in range(GROUPS):
                        if c == 0:
                            pe.wait_ge(mix_lo, g + 1)
                        for hh in range(2):
                            half(sums_of(NCH + c, NB), ahi, alo, g, hh, NB, (h1 + (c * GROUPS + g) * 2 + hh) % AHEAD, it * (4 * GROUPS) + (h1 + (c * GROUPS + g) * 2 + hh))

            stage("mod4")
            for j in range(8):
                if j == 3:
                    pe.wait_ge(rdiag_ready, 1)
                    b = fill("r2", 0)
                    mm = pe.matmul(b[:, 0:SEQ], c_(ONES), rdiag[:, :, :].rearrange("p t n -> p (t n)"), start=True, stop=True)
                    full(mm, "r2", 0)
                pe.wait_ge(x1_ready, TT * (1 + j // 4))
                b = fill(*h2T(j))
                for kk in range(2):
                    for t in range(TT):
                        k = 2 * j + kk
                        mm = pe.transpose(b[:, kk * SEQ + t * P:kk * SEQ + (t + 1) * P], x1[:, t, k * P:(k + 1) * P], c_(IDENT))
                full(mm, *h2T(j))

            h2 = h1 + 8 * GROUPS

            def mlp_turn(q, last):
                def turn(c):
                    pe.wait_ge(relu_squared, q * 4 + (c + 1))
                    for i in range(2):
                        f = 2 * c + i
                        bank, n = mlp_fill(f)
                        b = mx[bank]
                        pe.wait_ge(bank_free[bank], q * 2 + n)
                        for j in range(2):
                            for t in range(TT):
                                mm = pe.transpose(b[:, j * SEQ + t * P:j * SEQ + (t + 1) * P],
                                                  rst[:, c % 2, t, (2 * i + j) * P:(2 * i + j + 1) * P], c_(IDENT))
                        mm.then_inc(bank_full[bank], 1)
                for c in range(8):
                    pair, before = pair_of(NCH + 4 + c)
                    pe.wait_ge(gemm_free[pair], q * 4 + before)
                    for g in range(GROUPS):
                        if c == 0:
                            pe.wait_ge(h2_lo, 2 * g + 2)
                        if c == 4 and g in (0, 3):
                            b, n = mlp_fill(5 if g == 0 else 7)
                            pe.wait_ge(bank_free[b], q * 2 + (n + 1))
                        for hh in range(2):
                            half(sums_of(NCH + 4 + c, NB), hhi if c < 4 else ahi, hlo if c < 4 else alo, g, hh, NB,
                                 (h2 + (c * GROUPS + g) * 2 + hh) % AHEAD,
                                 q * (16 * GROUPS) + (h2 + (c * GROUPS + g) * 2 + hh))
                        if g == 1 and 1 <= c <= 4:
                            turn(c - 1)
                        if last and c == 5 and g == 1:
                            pe.wait_ge(acc_full, 4)
                            for j in range(4):
                                b, n = mlp_fill(8 * QUARTERS + j)
                                pe.wait_ge(bank_free[b], n)
                                pe.matmul(mx[b][:, :], c_(ONES), acc[:, 1, j * NB:(j + 1) * NB], start=True, stop=True)\
                                    .then_inc(bank_full[b], 1)

            with pe.Fori(0, QUARTERS - 1) as q:
                mlp_turn(q, False)
            mlp_turn(QUARTERS - 1, True)

        @block.gpsimd
        def _(pool):
            pool.memset(vrow[:, :, :], 0.0).then_inc(rows_zero, 1)
            pool.memset(epsc[:, 0:1], EPS).then_inc(eps_set, 1)
            pool.memset(acc[:, 0, :], 0.0).then_inc(acc_zero, 1)
            pool.memset(acc[:, 1, :], 0.0).then_inc(acc_zero, 1)

            def level(t, lv):
                pool.tensor_tensor(Cm[:, t], Dm[:, t], over_heads(c_(LV0 + lv)), ALU.mult).then_inc(level_ready, 1)

            def m1s(i):
                t, g = i // 2, i % 2
                pool.tensor_tensor(M1s[:, i % 2], over_heads(c_(SGT)), over_cols(dec[:, 9, t, 4 + 4 * g:8 + 4 * g], P),
                                   ALU.mult).then_inc(ssm_decay_spread, 1)

            def stage(name):
                if name == "part3":
                    wait_full(pool, name, 0)
                    for n in range(2):
                        pool.memset(acc[:, n, :], 0.0).then_inc(acc_zero, 1)
                elif name.startswith("mod"):
                    n = int(name[3])
                    wait_full(pool, name, 0)
                    pool.memset(acc[:, n % 2, :], 0.0).then_inc(acc_zero, 1)
                elif name == "sums":
                    pool.wait_ge(log_decay_step, 3)
                    for t in range(TT):
                        pool.tensor_tensor(Cm[:, t], over_heads(c_(SGT)), over_cols(dec[:, 9, t, 0:H], P), ALU.mult)\
                            .then_inc(gdn_decay_spread, 1)
                elif name.startswith("decay"):
                    t = int(name[5])
                    wait_taken(pool, name, 0)
                    pool.tensor_tensor(Dm[:, t], Dm[:, t], over_heads(c_(SGTB)), ALU.mult).then_inc(decay_masked, 1)
                    wait_taken(pool, name, 1)
                    pool.tensor_tensor(Dt[:, t], Dt[:, t], over_heads(c_(UINCB)), ALU.mult).then_inc(decay_masked, 1)
                elif name == "kbg":
                    pool.wait_ge(qk_normed, 2)
                    pool.wait_ge(kbg_factor_ready, 1)
                    for t in range(TT):
                        if t == 0:
                            wait_taken(pool, "tm_v", 0)
                            wait_taken(pool, "tm_v", 1)
                        ins = pool.tensor_tensor(kbg[:, t], tm[:, 1, t], over_cols(dec[:, 8, t, 4:8], P), ALU.mult)
                    ins.then_inc(kbg_ready, 1)
                    for t in range(TT):
                        wait_full(pool, "kqT", 2 + t)
                        pool.tensor_tensor(tm[:, 0, t], tm[:, 0, t], over_cols(sums[:, CS_GDN, t, 0:H], P), ALU.mult)\
                            .then_inc(qk_decayed, 1)
                    pool.wait_ge(kbg_ready, 1)
                    for t in range(TT):
                        pool.tensor_tensor(tm[:, 1, t], tm[:, 1, t], over_cols(sums[:, REST_GDN, t, 0:H], P), ALU.mult)\
                            .then_inc(qk_decayed, 1)
                elif name == "kk":
                    for t in range(TT):
                        wait_taken(pool, "kk", t)
                        level(t, 0)
                elif name == "lv0":
                    for t in range(TT):
                        wait_full(pool, "lv0", t)
                        level(t, 1)
                elif name.startswith("invY"):
                    lv = int(name[4])
                    for t in range(TT):
                        wait_full(pool, name, t)
                        if lv < 5:
                            level(t, lv + 1)
                elif name == "invX5":
                    for t in range(TT):
                        wait_full(pool, name, t)
                    pool.memset(VZ[:, :, :, :], 0.0).then_inc(vz_zeroed, 1)
                    pool.memset(O[0:64, 0], 0.0).then_inc(vz_zeroed, 1)
                elif name == "ssm_tm":
                    wait_full(pool, "gdn_out", 1)
                    m1s(0)
                    m1s(1)
                elif name in ("ssm_e0", "ssm_e1"):
                    wait_full(pool, name, 0)
                    m1s(int(name[5]) + 2)
                elif name == "rope":
                    wait_full(pool, "ssm_out", 1)
                    pool.wait_ge(trig_ready, 1)
                    wait_chunk_taken(pool, CHUNK["a2"])
                    pool.memset(kz[:, :, :, :, :], 0.0).then_inc(pool_step, 1)
                    qk = ptm[:, :, T_AQ:T_AV].rearrange("p t (h s n) -> p t h s n", h=10, s=2)
                    out = rq[:, :, :, :].rearrange("p t h (s n) -> p t h s n", s=2)
                    n = 1
                    for t in range(TT):
                        cos = trig[:, 0, t, :].unsqueeze(1).broadcast_to([P, 10, 32])
                        sin = trig[:, 1, t, :].unsqueeze(1).broadcast_to([P, 10, 32])
                        for s, (first, second, op) in enumerate(((cos, sin, ALU.subtract), (sin, cos, ALU.add))):
                            pool.tensor_tensor(rtmp[:, 0, t], qk[:, t, :, 0], first, ALU.mult).then_inc(pool_step, 1)
                            pool.tensor_tensor(rtmp[:, 1, t], qk[:, t, :, 1], second, ALU.mult).then_inc(pool_step, 1)
                            n += 2
                            pool.wait_ge(pool_step, n)
                            pool.tensor_tensor(out[:, t, :, s], rtmp[:, 0, t], rtmp[:, 1, t], op).then_inc(pool_step, 1)
                            n += 1
                            pool.wait_ge(pool_step, n)
                    for z in range(2):
                        for t in range(TT):
                            ins = pool.tensor_copy(kz[:, t, :, z, z * HD:(z + 1) * HD], rq[:, t, 8:10, :])
                    ins.then_inc(rope_done, 1)

            stage("part3")
            for slot in SCHEDULE:
                for name in slot:
                    stage(name)
            wait_full(pool, "gate_a", 3)
            pool.memset(acc[:, 1, :], 0.0).then_inc(acc_zero, 1)
            pool.wait_ge(x1_ready, 2 * TT)
            pool.memset(y[:, :, :], 0.0).then_inc(y_zero, 1)

        @block.scalar
        def _(act):
            steps = [0]

            def step(ins):
                ins.then_inc(act_step, 1)
                steps[0] += 1
                act.wait_ge(act_step, steps[0])

            for name, stack, row, n in ROWS:
                src = a[name] if name in ("c",) else a[name][0]
                if len(src.shape) == 1:
                    src = src.rearrange("(r n) -> r n", n=P)
                else:
                    src = src.rearrange("k (r n) -> (k r) n", n=P)
                if row == VA_C and stack == 0:
                    act.wait_ge(rows_zero, 1)
                act.dma_start(vrow[row:row + n, stack, :], src).then_inc(vrow_in, 16)
            for name, col, n in PRM:
                src = a[name] if name == "inv_freq" else a[name][0]
                act.dma_start(prm[:, col:col + n], src.partition_broadcast(P)).then_inc(prm_in, 16)
            act.dma_start(posi[:, :], a["positions"][0].rearrange("(t p) -> p t", p=P),
                          allow_slow_non_contiguous=True).then_inc(pos_in, 16)

            junk = rst[:, :, :, :].rearrange("p b t n -> p (b t n)")

            def root(ap, n, done):
                act.activation(ap, ap, ACT.Sqrt, bias=epsc[:, 0:1], scale=1.0 / n).then_inc(done, 1)

            wait_full(act, "vecT", 0)
            taken(act.activation(vcol[:, :, :], mx[fill_of("vecT", 0)[0]][:, 0:2 * P].rearrange("p (v n) -> p v n", v=2), ACT.Copy), "vecT", 0)
            wait_taken(act, "vecT", 0)
            act.activation(cact[:, :], vcol[:, 0, VA_C:VA_C + KT], ACT.Silu).then_inc(silu_c_ready, 1)
            act.wait_ge(x_in, 16)
            act.wait_ge(eps_set, 1)
            for t in range(TT):
                step(act.activation(xT[:, 0:D // SEQ, :].rearrange("p k n -> p (k n)"), x0[:, t, :], ACT.Square, accum_out=st[:, t:t + 1]))
            root(st[:, 0:2], D, x_root_ready)
            act.wait_ge(prm_in, 16 * len(PRM))
            act.activation(prm[:, P_ALOG:P_ALOG + 12], prm[:, P_ALOG:P_ALOG + 12], ACT.Exp).then_inc(x_root_ready, 1)
            for j in range(8):
                b = wait_full(act, "xT", j)
                taken(act.activation(xT[:, 2 * j:2 * j + 2, :], b[:, :].rearrange("p (k n) -> p k n", k=2), ACT.Copy), "xT", j)

            def h_part(part):
                act.wait_ge(h_ready, part + 1)
                act.activation(hhi[:, 4 * part:4 * part + 4, :], xT[:, 4 * part:4 * part + 4, :], ACT.Copy).then_inc(h_hi_ready, 1)
            def split(slot, w, hh, buf, h, n_in, first=False):
                if hh == 0:
                    act.wait_ge(raw_in[slot], n_in)
                if not first:
                    act.wait_ge(halves_done, h - (AHEAD - 1))
                src = raw[:, slot, :].rearrange("p (k n) -> p k n", k=GK)[:, 2 * hh:2 * hh + 2, 0:w]
                act.activation(whi[:, buf, :, 0:w], src, ACT.Copy).then_inc(hi_ready, 1)

            def split_at(h):
                ci, gi, hh = HALVES[h]
                pos = POS_OF["w", ci, gi]
                split(pos % RING, CHUNKS[ci][2], hh, h % AHEAD, h, 16 * (pos // RING + 1), h < AHEAD)
                if ci == 0 and hh == 1:
                    h_part(gi)

            staged = {}
            for i, c in enumerate(STAGED):
                before = [s for s in STAGED[:i] if STG_OF[s] == STG_OF[c]]
                staged[c] = before[-1] if before else None

            def evacuate(ci):
                name, _, w = CHUNKS[ci]
                if name == "ch":
                    return
                act.wait_ge(halves_done, H_OF[ci, GROUPS - 1, 1] + 1)
                if name in STG_OF:
                    if staged[name]:
                        wait_full(act, ("mul_" if staged[name] == "cb" else "conv_") + staged[name], 1)
                    dst = stg[:, STG_OF[name], :, :]
                else:
                    dst = ptm[:, :, TM_AT[name]:TM_AT[name] + w]
                pair = pair_of(ci)[0]
                if ci == 2:
                    for t in range(TT):
                        ins = act.activation(dst[:, t], sums_of(ci, w)[t], ACT.Copy)
                    ins.then_inc(gemm_free[pair], 1)
                else:
                    act.activation(dst, gps[pair][:, :, 0:w], ACT.Copy).then_inc(gemm_free[pair], 1)

            def copy_out(dst, name, i, func=ACT.Copy, **kw):
                b = wait_full(act, name, i)
                shape = dst.shape
                src = b[:, :] if len(shape) == 2 else b[:, 0:shape[1] * shape[2]].rearrange("p (h n) -> p h n", h=shape[1])
                taken(act.activation(dst, src, func, **kw), name, i)

            def stage(name):
                if name.startswith("evac"):
                    evacuate(int(name[4:]))
                elif name.startswith("conv_"):
                    c = name[5:]
                    for i in range(2):
                        b = wait_full(act, name, i)
                        for jj in range(2):
                            j = 2 * i + jj
                            if c == "cc":
                                w = vcol[:, 0, VA_SC + 2 * 4 + j:VA_SC + 2 * 4 + j + 1]
                                dst = mixT[:, 12 + j, :]
                            else:
                                tile0 = CONV[c][0]
                                w = tap_col(c, 3, j)
                                dst = cvo[:, tile0 + j, :]
                            ins = act.activation(dst, b[:, jj * SEQ:(jj + 1) * SEQ], ACT.Copy, scale=w)
                        ins.then_inc(last_tap_ready, 1)
                elif name.startswith("silu_"):
                    c = name[5:]
                    if c == "gz":
                        wait_chunk_taken(act, CHUNK["gz"])
                        act.activation(ptm[:, :, T_GZ:T_GZ + GW], ptm[:, :, T_GZ:T_GZ + GW], ACT.Silu).then_inc(gz_silu_ready, 1)
                    elif c == "sz":
                        wait_chunk_taken(act, CHUNK["s2"])
                        act.activation(ptm[:, :, T_SZ:T_SZ + GW], ptm[:, :, T_SZ:T_SZ + GW], ACT.Silu).then_inc(sz_silu_ready, 1)
                    else:
                        tile0 = CONV[c][0]
                        wait_taken(act, "conv_" + c, 1)
                        if c[0] == "g":
                            act.activation(cvo[:, tile0:tile0 + 4, :], cvo[:, tile0:tile0 + 4, :], ACT.Silu).then_inc(silu_done, 1)
                        else:
                            for j in range(4):
                                t_ = tile0 + j
                                ins = act.activation(cvo[:, t_, :], cvo[:, t_, :], ACT.Silu,
                                                     bias=vcol[:, 0, VA_CONVB + t_ - 12:VA_CONVB + t_ - 11])
                            ins.then_inc(silu_done, 1)
                elif name == "softplus":
                    act.wait_ge(log_decay_step, 1)
                    act.activation(dec[:, 8, :, 8:12], ptm[:, :, T_B:T_B + 4], ACT.Exp, scale=-1.0)
                    act.activation(dec[:, 2], dec[:, 1], ACT.Exp, scale=-1.0).then_inc(softplus_exp_step, 1)
                elif name == "angles":
                    act.wait_ge(angles_ready, 1)
                    act.activation(trig[:, 0], ang[:, 1], ACT.Sin)
                    act.activation(trig[:, 1], ang[:, 3], ACT.Sin).then_inc(trig_ready, 1)
                elif name == "softplus_u":
                    act.wait_ge(log_decay_step, 2)
                    act.activation(dec[:, 6], dec[:, 3], ACT.Ln).then_inc(softplus_exp_step, 1)
                elif name == "sums":
                    b = wait_full(act, name, 0)
                    taken(act.activation(sums[:, :, :, :].rearrange("p s t n -> p (s t n)"), b[:, 0:len(SUM_MASKS) * 24], ACT.Exp), name, 0)
                elif name.startswith("decay"):
                    t = int(name[5])
                    copy_out(Dm[:, t], name, 0, ACT.Exp)
                    copy_out(Dt[:, t], name, 1, ACT.Exp)
                elif name in ("tm_q", "tm_k"):
                    if name == "tm_q":
                        act.wait_ge(l2_sums_ready, 1)
                    for t in range(TT):
                        b = wait_full(act, name, t)
                        act.activation(tm[:, "qk".index(name[3]), t], slab(b), ACT.Copy)
                        taken(act.activation(Ym[:, t], slab(b), ACT.Square), name, t)
                elif name == "l2stat":
                    act.wait_ge(l2_sums_ready, 2)
                    act.activation(st[:, 20:36], st[:, 4:20], ACT.Sqrt, bias=epsc[:, 0:1]).then_inc(l2_root_ready, 1)
                elif name == "kqT":
                    for t in range(TT):
                        copy_out(knT[:, t], name, t)
                    for t in range(TT):
                        copy_out(qnT[:, t], name, 2 + t)
                elif name.startswith("invY"):
                    for t in range(TT):
                        copy_out(Ym[:, t], name, t)
                elif name == "qdT":
                    for t in range(TT):
                        copy_out(qdT[:, t], name, t)
                elif name == "uw":
                    for t in range(TT):
                        copy_out(U[:, t], name, 2 * t)
                        copy_out(WT[:, t], name, 2 * t + 1)
                elif name in ("gdn_v1", "gdn_v2", "gdn_v3"):
                    c = int(name[5])
                    r0 = (c % 2) * 64
                    b = wait_full(act, name, 1)
                    taken(act.activation(O[r0:r0 + 64, c // 2], slab(b)[r0:r0 + 64], ACT.Copy), name, 1)
                elif name == "gdn_gate":
                    wait_taken(act, "gdn_o0", 0)
                    wait_taken(act, "gdn_o1", 0)
                    act.activation(Xt[:, :, :, :], O[:, :, :, :], ACT.Square).then_inc(gdn_squared, 1)
                    act.wait_ge(gdn_squares_ready, 1)
                    root(st[:, 36:44], P, gdn_root_ready)
                elif name == "gdn_out":
                    for t in range(TT):
                        copy_out(mixT[:, 0:4, t * P:(t + 1) * P], name, t, scale=vcol[:, 0, VA_GDNN:VA_GDNN + 1])
                elif name == "ssm_tm":
                    for t in range(TT):
                        b = wait_full(act, name, t)
                        taken(act.activation(xs[:, t, :], b[:, :], ACT.Copy), name, t)
                    copy_out(btm[:, :, :], name, 2)
                elif name == "ssm_s":
                    copy_out(stt_[:, :, :], name, 0)
                elif name.startswith("ssm_e"):
                    copy_out(Es[:, int(name[5]) % 2], name, 0, ACT.Exp)
                elif name == "ssm_gate":
                    act.wait_ge(ssm_gated_raw, 1)
                    act.activation(ytmp[:, :, :], yb[:, :, :], ACT.Square).then_inc(ssm_squared, 1)
                    act.wait_ge(ssm_squares_ready, 1)
                    root(st[:, 44:48], SEQ, ssm_root_ready)
                elif name == "att_T":
                    for t in range(TT):
                        copy_out(qT2[:, t], name, t)
                    for t in range(TT):
                        copy_out(kzT[:, :, t * P:(t + 1) * P], name, 2 + t)
                elif name.startswith("att_s"):
                    f = int(name[5])
                    n, heads, blocks = att_part(f)
                    w = len(blocks) * P
                    act.wait_ge(sink_ready, f + 1)
                    act.activation(ats[:, f, 8:8 + len(heads)], ats[:, f, 8:8 + len(heads)], ACT.Exp)
                    for i in range(len(heads)):
                        s = sc[:, f % 2, i * w:(i + 1) * w]
                        ins = act.activation(s, s, ACT.Exp, bias=ats[:, f, 4 + i:5 + i], accum_out=ats[:, f, 12 + i:13 + i])
                    ins.then_inc(probs_ready, 1)
                elif name.startswith("att_t"):
                    copy_out(PT[:, int(name[5]) % 2], name, 0)
                elif name == "att_out":
                    for t in range(TT):
                        copy_out(mixT[:, 8:12, t * P:(t + 1) * P], name, t)
                elif name.startswith("split"):
                    kg = int(name[5])
                    for i in range(2):
                        wait_taken(act, SPLIT_AFTER[kg], i)
                    wait_taken(act, "ssm_out", 1)
                    act.activation(ahi[:, 4 * kg:4 * kg + 4, :], mixT[:, 4 * kg:4 * kg + 4, :], ACT.Copy).then_inc(mix_hi, 1)

            h1 = SLOTS
            h2 = h1 + 8 * GROUPS
            n2 = 16 * (N_RINGED // RING + 1)

            def split_out(n):
                if n < 8 * GROUPS:
                    pos = POS_OF["out", n // 8, n // 2 % GROUPS]
                    split(pos % RING, NB, n % 2, (h1 + n) % AHEAD, h1 + n, 16 * (pos // RING + 1))
                else:
                    split_mlp(0, n - 8 * GROUPS)

            def split_mlp(q, n):
                turns, n = divmod(n, 16 * GROUPS)
                pos = MLP_POS["w", n // 2]
                split(pos % RING, NB, n % 2, (h2 + n) % AHEAD, q * (16 * GROUPS) + (h2 + n + turns * 16 * GROUPS),
                      q * (4 * len(MLP_ITEMS)) + (n2 + 16 * (pos // RING) + turns * 4 * len(MLP_ITEMS)))

            for h in range(AHEAD):
                split_at(h)
            for h in range(SLOTS):
                if h + AHEAD < SLOTS:
                    split_at(h + AHEAD)
                else:
                    split_out(h + AHEAD - SLOTS)
                for name in with_moves(h):
                    stage(name)

            for n in range(8 * GROUPS):
                if n < 8 * GROUPS - 1:
                    split_out(n + AHEAD)
                if n == 4 * GROUPS:
                    act.activation(st[:, 60:61], epsc[:, 0:1], ACT.Sqrt)
                if n == 0:
                    act.wait_ge(mix_lo, 4)
                    act.dma_start(grow[:, :], a["norm_post_mix"][0].partition_broadcast(P)).then_inc(norm_row_in, 16)
                    act.dma_start(x1[:, :, :], x_v).then_inc(x_again_in, 16)
                if n % (2 * GROUPS) == 2 * GROUPS - 1:
                    c = n // (2 * GROUPS)
                    act.wait_ge(halves_done, h1 + n + 1)
                    for t in range(TT):
                        act.activation(rst[:, c % 2, t, :], sums_of(NCH + c, NB)[t], ACT.Square,
                                       accum_out=yss[:, t, c:c + 1]).then_inc(y_squared, 1)

            act.wait_ge(y_sums_ready, 1)
            root(st[:, 48:50], D, y_root_ready)
            for cp in range(2):
                for t in range(TT):
                    act.wait_ge(x1_ready, cp * TT + t + 1)
                    step(act.activation(junk[:, 0:D // 2], x1[:, t, cp * (D // 2):(cp + 1) * (D // 2)], ACT.Square,
                                        accum_out=st[:, 52 + 2 * cp + t:53 + 2 * cp + t]))
            act.sem_inc(x1_squared, 1)
            act.wait_ge(x1_sums_ready, 1)
            root(st[:, 50:52], D, x1_root_ready)
            b = wait_full(act, "r2", 0)
            taken(act.activation(rrow[:, :], b[:, 0:SEQ], ACT.Copy), "r2", 0)
            act.dma_start(grow[:, :], a["norm_post_mlp"][0].partition_broadcast(P)).then_inc(norm_row_in, 16)
            wait_taken(act, "mod2", 0)
            for j in range(8):
                act.wait_ge(x1T_scaled, j + 1)
                for kk in range(2):
                    k = 2 * j + kk
                    ins = act.activation(hhi[:, k, :], hful[:, j % 2, kk, :], ACT.Identity, bias=modc[:, 2, k:k + 1])
                ins.then_inc(h2_hi, 1)
                if j == 3:
                    split_mlp(0, AHEAD - 1)

            def mlp_turn(q, last):
                def relu(c):
                    pair = pair_of(NCH + 4 + c)[0]
                    act.wait_ge(halves_done, q * (16 * GROUPS) + (h2 + 2 * GROUPS * (c + 1)))
                    f = 2 * ((c + 2) % 4) + 1
                    b, n = mlp_fill(f)
                    act.wait_ge(bank_full[b], q * 2 + (n + 1 - (2 if c < 2 else 0)))
                    act.activation(rst[:, c % 2], gps[pair][:, :, :], ACT.Relu).then_inc(gemm_free[pair], 1)

                def squares(c):
                    act.wait_ge(y_chunk_ready, c - 3)
                    for t in range(TT):
                        act.activation(rst[:, c % 2, t, :], y[:, t, (c - 4) * NB:(c - 3) * NB], ACT.Square,
                                       accum_out=yss[:, t, c - 4:c - 3]).then_inc(y_squared, 1)

                for n in range(16 * GROUPS):
                    if not last or n + AHEAD < 16 * GROUPS:
                        split_mlp(q, n + AHEAD)
                    c, at = divmod(n, 2 * GROUPS)
                    if at == 2 * GROUPS - 1:
                        if c < 4:
                            relu(c)
                    if at == 3 and 1 <= c <= 4:
                        for f in (2 * c - 2, 2 * c - 1):
                            b, m = mlp_fill(f)
                            act.wait_ge(bank_full[b], q * 2 + (m + 1))
                            act.activation(ahi[:, 2 * f:2 * f + 2, :], mx[b][:, :].rearrange("p (k n) -> p k n", k=2),
                                           ACT.Copy).then_inc(act_hi_ready, 1)
                    if last and at == 1 and c > 4:
                        squares(c - 1)
                if last:
                    squares(7)

            with act.Fori(0, QUARTERS - 1) as q:
                mlp_turn(q, False)
            mlp_turn(QUARTERS - 1, True)
            act.wait_ge(y_sums_ready, 2)
            root(st[:, 48:50], D, y_root_ready)

        @block.vector
        def _(dve):
            steps = [0]

            def step(ins):
                ins.then_inc(vec_step, 1)
                steps[0] += 1
                dve.wait_ge(vec_step, steps[0])

            def ada(a_, k, pos):
                if k == 0:
                    dve.wait_ge(acc_seed[a_ % 2], 16 * (a_ // 2 + 1))
                else:
                    dve.wait_ge(ada_used, (a_ - 2) * KT + k)
                dve.wait_ge(raw_in[pos % RING], 16 * (pos // RING + 1))
                dve.scalar_tensor_tensor(out=acc[:, a_ % 2, :], in0=raw[:, pos % RING, :], scalar=cact[:, k:k + 1],
                                         in1=acc[:, a_ % 2, :], op0=ALU.mult, op1=ALU.add).then_inc(ada_used, 1)
                if k == KT - 1:
                    dve.wait_ge(ada_used, (a_ - 1) * KT)
                    dve.sem_inc(acc_full, 1)

            def split(slot, w, hh, buf, h, n_in):
                if hh == 0:
                    dve.wait_ge(raw_in[slot], n_in)
                dve.wait_ge(hi_ready, h + 1)
                src = raw[:, slot, :].rearrange("p (k n) -> p k n", k=GK)[:, 2 * hh:2 * hh + 2, 0:w]
                dve.tensor_tensor(wlo[:, buf, :, 0:w], src, whi[:, buf, :, 0:w].bitcast(F32), ALU.subtract)\
                    .then_inc(lo_ready, 1)

            def ada_pair(q, j):
                if q == 0 and j == 0:
                    dve.wait_ge(silu_c_ready, 1)
                    dve.wait_ge(acc_seed[0], 16)
                    dve.wait_ge(acc_seed[1], 16)
                first = q * 2 * GROUPS + j
                for i in range(2):
                    dve.wait_ge(part_in[(first + i) % PARTS], 16 * ((first + i) // PARTS + 1))
                n = part_steps(q, j) - (2 * GK - 1)
                for k in range(GK):
                    for i in range(2):
                        if j or k:
                            dve.wait_ge(ada_part_step, n - 1)
                        sums_ = acc[:, i, q * NB:(q + 1) * NB]
                        row = j // 2 * GK + k
                        dve.scalar_tensor_tensor(out=sums_, in0=part[:, (first + i) % PARTS, k * NB:(k + 1) * NB],
                                                 scalar=cact[:, row:row + 1], in1=sums_, op0=ALU.mult,
                                                 op1=ALU.add).then_inc(ada_part_step, 1)
                        n += 1

            def h_part(q):
                name = f"part{q}"
                b = wait_full(dve, name, 0)
                ks = slice(q * GK, (q + 1) * GK)
                dve.tensor_copy(modc[:, 0, ks], b[:, 0:GK])
                taken(dve.scalar_tensor_tensor(out=modc[:, 1, ks], in0=b[:, GK:2 * GK], scalar=1.0,
                                               in1=vcol[:, 0, VA_PRE_MIX + q * GK:VA_PRE_MIX + (q + 1) * GK],
                                               op0=ALU.add, op1=ALU.mult), name, 0)
                wait_taken(dve, name, 0)
                for k in range(q * GK, (q + 1) * GK):
                    wait_taken(dve, "xT", k // 2)
                    ins = dve.tensor_scalar(xT[:, k, :], xT[:, k, :], modc[:, 1, k:k + 1], modc[:, 0, k:k + 1], ALU.mult, ALU.add)
                ins.then_inc(h_ready, 1)
                dve.wait_ge(h_hi_ready, q + 1)
                lower(hlo[:, ks, :], xT[:, ks, :], hhi[:, ks, :]).then_inc(h_lo_ready, 1)

            def between(item):
                at = STREAM.index(item) + 1
                while at < len(STREAM) and STREAM[at][0] in ("ada", "part"):
                    kind, i, j = STREAM[at]
                    if kind == "ada":
                        ada(i, j, POS_OF[STREAM[at]])
                    elif j % 2 == 0:
                        ada_pair(i, j)
                    at += 1

            def split_at(h):
                ci, gi, hh = HALVES[h]
                pos = POS_OF["w", ci, gi]
                split(pos % RING, CHUNKS[ci][2], hh, h % AHEAD, h, 16 * (pos // RING + 1))
                if hh:
                    if ci == 0:
                        h_part(gi)
                    between(("w", ci, gi))

            def lower(dst_lo, src, src_hi):
                return dve.tensor_tensor(dst_lo, src, src_hi.bitcast(F32), ALU.subtract)

            def taps(name, i, dst, w_of, n_taps):
                b = wait_full(dve, name, i)
                for back in range(1, n_taps):
                    for jj in range(2):
                        d = dst(2 * i + jj)[:, back:SEQ]
                        ins = dve.scalar_tensor_tensor(out=d, in0=b[:, jj * SEQ:(jj + 1) * SEQ - back],
                                                       scalar=w_of(n_taps - 1 - back, 2 * i + jj), in1=d, op0=ALU.mult, op1=ALU.add)
                        if back == n_taps - 1 and jj == 1:
                            taken(ins, name, i)
                        elif jj == 1:
                            step(ins)

            def stage(name):
                if name == "evac" + str(CHUNK["ch"]):
                    ci = CHUNK["ch"]
                    dve.wait_ge(halves_done, H_OF[ci, GROUPS - 1, 1] + 1)
                    wait_chunk_taken(dve, CHUNK["cc"])
                    s = stg[:, STG_OF["cc"]]
                    pair = pair_of(ci)[0]
                    dve.tensor_tensor(s, gps[pair][:, :, :], s, ALU.mult).then_inc(gemm_free[pair], 1)
                elif name.startswith("mod"):
                    n = int(name[3])
                    b = wait_full(dve, name, 0)
                    if n == 2:
                        taken(dve.tensor_copy(modc[:, n, :], b[:, 0:KT]), name, 0)
                    else:
                        row = VA_PRE_MLP
                        taken(dve.scalar_tensor_tensor(out=modc[:, 3, :], in0=b[:, 0:KT], scalar=1.0,
                                                       in1=vcol[:, 0, row:row + KT], op0=ALU.add, op1=ALU.mult), name, 0)
                elif name.startswith("conv_"):
                    c = name[5:]
                    for i in range(2):
                        dve.wait_ge(last_tap_ready, 2 * (CONV_ORDER + ["cc"]).index(c) + i + 1)
                        if c == "cc":
                            taps(name, i, lambda j: mixT[:, 12 + j, :],
                                 lambda tap, j: vcol[:, 0, VA_SC + tap * 4 + j:VA_SC + tap * 4 + j + 1], 3)
                        else:
                            tile0 = CONV[c][0]
                            taps(name, i, lambda j: cvo[:, tile0 + j, :], lambda tap, j: tap_col(c, tap, j), 4)
                elif name == "mul_cb":
                    for i in range(2):
                        b = wait_full(dve, name, i)
                        wait_taken(dve, "conv_cc", i)
                        d = mixT[:, 12 + 2 * i:14 + 2 * i, :]
                        taken(dve.tensor_tensor(d, b[:, :].rearrange("p (k n) -> p k n", k=2), d, ALU.mult), name, i)
                elif name == "softplus":
                    wait_chunk_taken(dve, CHUNK["s1"])
                    wait_chunk_taken(dve, CHUNK["a1"])
                    dve.wait_ge(x_root_ready, 2)
                    z, ax = dec[:, 0], dec[:, 1]
                    for col, n, at in ((T_A, 4, 0), (T_DT, 8, 4)):
                        ins = dve.tensor_tensor(z[:, :, at:at + n], ptm[:, :, col:col + n],
                                                prm[:, P_DTB + at:P_DTB + at + n].unsqueeze(1).broadcast_to([P, TT, n]), ALU.add)
                    step(ins)
                    dve.scalar_tensor_tensor(out=ax, in0=z, scalar=-1.0, in1=z, op0=ALU.mult, op1=ALU.max).then_inc(log_decay_step, 1)
                elif name == "angles":
                    dve.wait_ge(pos_in, 16)
                    dve.wait_ge(prm_in, 16 * len(PRM))
                    step(dve.tensor_copy(posf[:, :], posi[:, :]))
                    for t in range(TT):
                        ins = dve.tensor_scalar(ang[:, 0, t, :], prm[:, P_FREQ:P_FREQ + 32], posf[:, t:t + 1], None, ALU.mult)
                    step(ins)
                    for quarter, dst in ((0.25, 1), (0.0, 3)):
                        step(dve.tensor_scalar(ang[:, 2], ang[:, 0], 1.0 / TWO_PI, quarter, ALU.mult, ALU.add))
                        step(dve.tensor_copy(angi[:, :, :], ang[:, 2]))
                        step(dve.tensor_copy(ang[:, 2], angi[:, :, :]))
                        step(dve.scalar_tensor_tensor(out=ang[:, dst], in0=ang[:, 2], scalar=-PI2_A, in1=ang[:, 0], op0=ALU.mult, op1=ALU.add))
                        step(dve.scalar_tensor_tensor(out=ang[:, dst], in0=ang[:, 2], scalar=-PI2_B, in1=ang[:, dst], op0=ALU.mult, op1=ALU.add))
                        step(dve.scalar_tensor_tensor(out=ang[:, dst], in0=ang[:, 2], scalar=-PI2_C, in1=ang[:, dst], op0=ALU.mult, op1=ALU.add))
                        step(dve.tensor_scalar(ang[:, dst], ang[:, dst], quarter * TWO_PI, PI_LOW, ALU.add, ALU.min))
                        ins = dve.tensor_scalar(ang[:, dst], ang[:, dst], -PI_LOW, None, ALU.max)
                        if dst == 3:
                            ins.then_inc(angles_ready, 1)
                        else:
                            step(ins)
                elif name == "softplus_u":
                    u, e = dec[:, 3], dec[:, 2]
                    dve.wait_ge(softplus_exp_step, 1)
                    dve.tensor_scalar(dec[:, 8, :, 8:12], dec[:, 8, :, 8:12], 1.0, None, ALU.add)
                    dve.tensor_scalar(u, e, 1.0, None, ALU.add).then_inc(log_decay_step, 1)
                elif name == "softplus_log":
                    z, ax, e, u, num, den, ln, sp = (dec[:, i] for i in range(8))
                    dve.wait_ge(log_decay_step, 2)
                    step(dve.tensor_scalar(den, u, -1.0, None, ALU.add))
                    step(dve.tensor_scalar(num, den, 0.0, None, ALU.is_equal))
                    step(dve.tensor_tensor(den, den, num, ALU.add))
                    step(dve.reciprocal(den, den))
                    dve.wait_ge(softplus_exp_step, 2)
                    step(dve.tensor_tensor(num, num, ln, ALU.add))
                    step(dve.tensor_tensor(num, num, e, ALU.mult))
                    step(dve.tensor_tensor(num, num, den, ALU.mult))
                    dve.reciprocal(dec[:, 8, :, 0:4], dec[:, 8, :, 8:12])
                    step(dve.scalar_tensor_tensor(out=sp, in0=z, scalar=0.0, in1=num, op0=ALU.max, op1=ALU.add))
                    dve.scalar_tensor_tensor(out=dec[:, 9], in0=sp, scalar=-1.0,
                                             in1=prm[:, P_ALOG:P_ALOG + 12].unsqueeze(1).broadcast_to([P, TT, 12]),
                                             op0=ALU.mult, op1=ALU.mult).then_inc(log_decay_step, 1)
                elif name == "sums":
                    wait_taken(dve, "sums", 0)
                    dve.wait_ge(log_decay_step, 3)
                    dve.tensor_tensor(dec[:, 8, :, 4:8], dec[:, 8, :, 0:4], sums[:, CS_GDN, :, 0:H], ALU.mult).then_inc(kbg_factor_ready, 1)
                elif name in ("tm_q", "tm_k"):
                    w = "qk".index(name[3])
                    for t in range(TT):
                        wait_taken(dve, name, t)
                        ins = dve.tensor_reduce(st[:, 4 + 8 * w + 4 * t:8 + 8 * w + 4 * t], Ym[:, t], AX, ALU.add)
                    ins.then_inc(l2_sums_ready, 1)
                elif name == "tm_v":
                    for t in range(TT):
                        b = wait_full(dve, name, t)
                        taken(dve.tensor_tensor(tm[:, 2, t], slab(b), over_cols(dec[:, 8, t, 0:4], P), ALU.mult), name, t)
                elif name == "l2scale":
                    dve.wait_ge(l2_root_ready, 1)
                    step(dve.reciprocal(st[:, 20:36], st[:, 20:36]))
                    for w in (0, 1):
                        n = tm[:, w].rearrange("p t h n -> p (t h) n")
                        r = over_cols(st[:, 20 + 8 * w:28 + 8 * w], P)
                        if w == 0:
                            step(dve.tensor_scalar(st[:, 20:28], st[:, 20:28], float(P) ** -0.5, None, ALU.mult))
                        dve.tensor_tensor(n, n, r, ALU.mult).then_inc(qk_normed, 1)
                elif name == "kk":
                    for t in range(TT):
                        dve.wait_ge(decay_masked, 2 * t + 1)
                        b = wait_full(dve, name, t)
                        for h in range(H):
                            ins = dve.scalar_tensor_tensor(out=Dm[:, t, h], in0=b[:, h * P:(h + 1) * P], scalar=dec[:, 8, t, h:h + 1],
                                                           in1=Dm[:, t, h], op0=ALU.mult, op1=ALU.mult)
                        taken(ins, name, t)
                elif name == "qk":
                    for t in range(TT):
                        dve.wait_ge(decay_masked, 2 * t + 2)
                        b = wait_full(dve, name, t)
                        taken(dve.tensor_tensor(Dt[:, t], slab(b), Dt[:, t], ALU.mult), name, t)
                elif name == "lv0":
                    for t in range(TT):
                        dve.wait_ge(level_ready, t + 1)
                        b = wait_full(dve, name, t)
                        step(dve.scalar_tensor_tensor(out=Xt[:, t], in0=slab(b), scalar=-1.0, in1=over_heads(c_(IDENT)),
                                                      op0=ALU.mult, op1=ALU.add))
                        step(dve.tensor_tensor(Xm[:, t], Dm[:, t], over_heads(c_(LV0)), ALU.mult))
                        step(dve.scalar_tensor_tensor(out=Xm[:, t], in0=Xm[:, t], scalar=-1.0, in1=over_heads(c_(IDENT)),
                                                      op0=ALU.mult, op1=ALU.add))
                        dve.sem_inc(bank_free[fill_of(name, t)[0]], 1)
                        dve.sem_inc(inverse_ready, 1)
                elif name.startswith("invX"):
                    lv = int(name[4])
                    for t in range(TT):
                        b = wait_full(dve, name, t)
                        ins = dve.tensor_tensor(Xt[:, t], Xt[:, t], slab(b), ALU.subtract)
                        taken(ins, name, t)
                        if lv < 5:
                            b = wait_full(dve, name, 2 + t)
                            taken(dve.tensor_tensor(Xm[:, t], Xm[:, t], slab(b), ALU.subtract), name, 2 + t)
                            wait_taken(dve, name, 2 + t)
                        wait_taken(dve, name, t)
                        dve.sem_inc(inverse_ready, 1)
                elif name.startswith("gdn_v"):
                    c = int(name[5])
                    t, r0 = c // 2, (c % 2) * 64
                    wait_taken(dve, "uw", 2 * t)
                    if c == 0:
                        dve.wait_ge(vz_zeroed, 2)
                        dve.tensor_copy(VZ[0:64, 0], U[0:64, 0]).then_inc(v_new_ready, 1)
                    else:
                        if c == 2:
                            wait_full(dve, "gdn_o0", 0)
                        b = wait_full(dve, name, 0)
                        step(dve.tensor_tensor(VZ[r0:r0 + 64, c % 2], U[r0:r0 + 64, t], slab(b)[r0:r0 + 64], ALU.subtract))
                        dve.sem_inc(bank_free[fill_of(name, 0)[0]], 1)
                        dve.sem_inc(v_new_ready, 1)
                elif name.startswith("gdn_s"):
                    c = int(name[5])
                    b = wait_full(dve, name, 0)
                    if c == 0:
                        taken(dve.tensor_copy(Sm[:, :, :], slab(b)), name, 0)
                    else:
                        wait_taken(dve, f"gdn_s{c - 1}", 0)
                        for h in range(H):
                            ins = dve.scalar_tensor_tensor(out=Sm[:, h], in0=Sm[:, h], scalar=sums[:, TOT0 + c % 2, c // 2, h:h + 1],
                                                           in1=b[:, h * P:(h + 1) * P], op0=ALU.mult, op1=ALU.add)
                        taken(ins, name, 0)
                elif name in ("gdn_o0", "gdn_o1"):
                    t = int(name[5])
                    b = wait_full(dve, name, 0)
                    dve.wait_ge(vz_zeroed, 2)
                    wait_taken(dve, f"gdn_v{2 * t + 1}", 1)
                    if t:
                        wait_taken(dve, "gdn_v2", 1)
                    taken(dve.tensor_tensor(O[:, t], O[:, t], slab(b), ALU.add), name, 0)
                elif name == "gdn_gate":
                    dve.wait_ge(gdn_squared, 1)
                    dve.tensor_reduce(st[:, 36:44], Xt[:, :, :, :].rearrange("p t h n -> p (t h) n"), AX, ALU.add).then_inc(gdn_squares_ready, 1)
                    dve.wait_ge(gdn_root_ready, 1)
                    step(dve.reciprocal(st[:, 36:44], st[:, 36:44]))
                    o = O[:, :, :, :].rearrange("p t h n -> p (t h) n")
                    step(dve.tensor_tensor(o, o, over_cols(st[:, 36:44], P), ALU.mult))
                    dve.wait_ge(gz_silu_ready, 1)
                    o = O[:, :, :, :].rearrange("p t h n -> p t (h n)")
                    dve.tensor_tensor(o, o, ptm[:, :, T_GZ:T_GZ + GW], ALU.mult).then_inc(gdn_gated, 1)
                elif name == "ssm_tm":
                    for t in range(TT):
                        wait_taken(dve, name, t)
                    x3 = xs[:, :, :].rearrange("p t (h n) -> p t h n", h=SH)
                    for t in range(TT):
                        dve.tensor_tensor(yb[:, t, :].rearrange("p (h n) -> p h n", h=SH), x3[:, t],
                                          over_cols(prm[:, P_SD:P_SD + 8], HD), ALU.mult)
                    for t in range(TT):
                        ins = dve.tensor_tensor(xdt[:, t], x3[:, t], over_cols(dec[:, 7, t, 4:12], HD), ALU.mult)
                    step(ins)
                    dve.tensor_tensor(xdd[:, :, :], xdt[:, 0], over_cols(sums[:, REST_SSM, 0, 4:12], HD), ALU.mult).then_inc(xdt_ready, 1)
                elif name == "ssm_cb":
                    b = wait_full(dve, name, 0)
                    taken(dve.tensor_tensor(CBm[:, :, :], slab(b), over_heads(c_(UINC)), ALU.mult), name, 0)
                elif name == "ssm_o":
                    b = wait_full(dve, name, 0)
                    step(dve.tensor_tensor(ytmp[:, 0, :].rearrange("p (h n) -> p h n", h=SH), b[:, :].rearrange("p (h n) -> p h n", h=SH),
                                           over_cols(sums[:, CS_SSM, 1, 4:12], HD), ALU.mult))
                    taken(dve.tensor_tensor(yb[:, 1, :], yb[:, 1, :], ytmp[:, 0, :], ALU.add), name, 0)
                elif name.startswith("ssm_e"):
                    i = int(name[5])
                    t, g = i // 2, i % 2
                    wait_taken(dve, "ssm_cb", 0)
                    wait_taken(dve, name, 0)
                    dve.tensor_tensor(Es[:, i % 2], Es[:, i % 2], over_heads(CBm[:, 2 * t + g, :]), ALU.mult).then_inc(ssm_weights_ready, 1)
                elif name.startswith("ssm_y"):
                    i = int(name[5])
                    t, g = i // 2, i % 2
                    b = wait_full(dve, name, 0)
                    wait_taken(dve, "ssm_o", 0)
                    d = yb[:, t, g * SEQ:(g + 1) * SEQ]
                    taken(dve.tensor_tensor(d, d, b[:, 0:SEQ], ALU.add), name, 0)
                elif name == "ssm_gate":
                    for i in range(4):
                        wait_taken(dve, f"ssm_y{i}", 0)
                    dve.wait_ge(sz_silu_ready, 1)
                    dve.tensor_tensor(yb[:, :, :], yb[:, :, :], ptm[:, :, T_SZ:T_SZ + GW], ALU.mult).then_inc(ssm_gated_raw, 1)
                    dve.wait_ge(ssm_squared, 1)
                    dve.tensor_reduce(st[:, 44:48], ytmp[:, :, :].rearrange("p t (g n) -> p (t g) n", g=2), AX, ALU.add).then_inc(ssm_squares_ready, 1)
                    dve.wait_ge(ssm_root_ready, 1)
                    step(dve.reciprocal(st[:, 44:48], st[:, 44:48]))
                    o = yb[:, :, :].rearrange("p t (g n) -> p (t g) n", g=2)
                    dve.tensor_tensor(o, o, over_cols(st[:, 44:48], SEQ), ALU.mult).then_inc(ssm_gated, 1)
                elif name == "ssm_out":
                    for t in range(TT):
                        b = wait_full(dve, name, t)
                        taken(dve.tensor_tensor(mixT[:, 4:8, t * P:(t + 1) * P], slab(b), over_cols(vcol[:, 0, VA_SSMN:VA_SSMN + 4], P),
                                                ALU.mult), name, t)
                elif name.startswith("att_s"):
                    f = int(name[5])
                    n, heads, blocks = att_part(f)
                    nh, w = len(heads), len(blocks) * P
                    b = wait_full(dve, name, 0)
                    mask = cst[:, AMC, :] if len(blocks) == 1 else cst[:, AMP:AMC + 1, :].rearrange("p a n -> p (a n)")
                    s = sc[:, f % 2, :].rearrange("p (h n) -> p h n", h=nh)
                    step(dve.scalar_tensor_tensor(out=s, in0=slab(b, nh), scalar=float(HD) ** -0.5, in1=over_heads(mask, nh),
                                                  op0=ALU.mult, op1=ALU.add))
                    dve.sem_inc(bank_free[fill_of(name, 0)[0]], 1)
                    step(dve.tensor_reduce(ats[:, f, 0:nh], s, AX, ALU.max))
                    sink = prm[:, P_SINK + heads[0]:P_SINK + heads[0] + nh]
                    step(dve.tensor_tensor(ats[:, f, 0:nh], ats[:, f, 0:nh], sink, ALU.max))
                    step(dve.tensor_scalar(ats[:, f, 4:4 + nh], ats[:, f, 0:nh], -1.0, None, ALU.mult))
                    dve.tensor_tensor(ats[:, f, 8:8 + nh], ats[:, f, 4:4 + nh], sink, ALU.add).then_inc(sink_ready, 1)
                elif name.startswith("att_t"):
                    f = int(name[5])
                    nh = len(att_part(f)[1])
                    dve.wait_ge(probs_ready, f + 1)
                    step(dve.tensor_tensor(ats[:, f, 12:12 + nh], ats[:, f, 12:12 + nh], ats[:, f, 8:8 + nh], ALU.add))
                    step(dve.reciprocal(ats[:, f, 12:12 + nh], ats[:, f, 12:12 + nh]))
                elif name.startswith("split"):
                    kg = int(name[5])
                    wait_full(dve, "att_T", 3)
                    dve.wait_ge(mix_hi, kg + 1)
                    ks = slice(4 * kg, 4 * kg + 4)
                    lower(alo[:, ks, :], mixT[:, ks, :], ahi[:, ks, :]).then_inc(mix_lo, 1)
                elif name.startswith("att_v"):
                    f = int(name[5])
                    n, heads, blocks = att_part(f)
                    nh = len(heads)
                    b = wait_full(dve, name, 0)
                    taken(dve.tensor_tensor(yc[:, n, heads[0] * HD:(heads[0] + nh) * HD].rearrange("p (h n) -> p h n", h=nh),
                                            b[:, 0:nh * HD].rearrange("p (h n) -> p h n", h=nh),
                                            over_cols(ats[:, f, 12:12 + nh], HD), ALU.mult), name, 0)

            ada_pair(0, 0)
            dve.wait_ge(x_root_ready, 1)
            step(dve.reciprocal(st[:, 0:2], st[:, 0:2]))
            for t in range(TT):
                dve.tensor_scalar(x0[:, t, :], x0[:, t, :], st[:, t:t + 1], None, ALU.mult).then_inc(x_normed, 1)

            for g in range(1, GROUPS):
                ada_pair(0, 2 * g)
            h1 = SLOTS
            h2 = h1 + 8 * GROUPS
            n2 = 16 * (N_RINGED // RING + 1)

            def split_out(n):
                if n < 8 * GROUPS:
                    item = ("out", n // 8, n // 2 % GROUPS)
                    pos = POS_OF[item]
                    split(pos % RING, NB, n % 2, (h1 + n) % AHEAD, h1 + n, 16 * (pos // RING + 1))
                    if n % 2:
                        between(item)
                else:
                    split_mlp(0, n - 8 * GROUPS)

            def split_mlp(q, n):
                turns, n = divmod(n, 16 * GROUPS)
                pos = MLP_POS["w", n // 2]
                per_turn = 4 * len(MLP_ITEMS)
                split(pos % RING, NB, n % 2, (h2 + n) % AHEAD, q * (16 * GROUPS) + (h2 + n + turns * 16 * GROUPS),
                      q * per_turn + (n2 + 16 * (pos // RING) + turns * per_turn))
                c, at = divmod(n, 2 * GROUPS)
                if at == 3 and 1 <= c <= 4:
                    k = q * 4 + (c - 1)
                    pos = MLP_POS["ada", c - 1]
                    if c == 1:
                        dve.wait_ge(acc_seed[1], 16 * 3)
                    dve.wait_ge(ada_used, q * 4 + (3 * KT + c - 1))
                    dve.wait_ge(raw_in[pos % RING], q * per_turn + (n2 + 16 * (pos // RING)))
                    dve.scalar_tensor_tensor(out=acc[:, 1, :], in0=raw[:, pos % RING, :], scalar=cact[:, bass.ds(k, 1)],
                                             in1=acc[:, 1, :], op0=ALU.mult, op1=ALU.add).then_inc(ada_used, 1)

            def gate_rows(j, bank, n_in):
                dve.wait_ge(norm_row_in, n_in)
                g = grow[:, j * NB:(j + 1) * NB]
                return dve.tensor_tensor(g, bank[:, :], g, ALU.mult)

            for h in range(AHEAD):
                split_at(h)
            for h in range(SLOTS):
                if h + AHEAD < SLOTS:
                    split_at(h + AHEAD)
                else:
                    split_out(h + AHEAD - SLOTS)
                for name in with_moves(h):
                    stage(name)

            for n in range(8 * GROUPS):
                if n < 8 * GROUPS - 1:
                    split_out(n + AHEAD)
                if n == 4:
                    for j in range(4):
                        b = wait_full(dve, "gate_a", j)
                        taken(gate_rows(j, b, 16), "gate_a", j)
                if n % (2 * GROUPS) == 2 * GROUPS - 1:
                    c = n // (2 * GROUPS)
                    pair = pair_of(NCH + c)[0]
                    wait_taken(dve, "gate_a", c)
                    dve.wait_ge(halves_done, h1 + n + 1)
                    dve.wait_ge(y_squared, 2 * (c + 1))
                    if c == 3:
                        dve.tensor_reduce(st[:, 48:50], yss[:, :, :], AX, ALU.add).then_inc(y_sums_ready, 1)
                    cols = slice(c * NB, (c + 1) * NB)
                    for t in range(TT):
                        ins = dve.tensor_tensor(y[:, t, cols], gps[pair][:, t, :], grow[:, cols], ALU.mult)
                    ins.then_inc(gemm_free[pair], 1)

            wait_chunk_taken(dve, NCH + 2)
            wait_chunk_taken(dve, NCH + 3)
            dve.wait_ge(y_root_ready, 1)
            step(dve.reciprocal(st[:, 48:50], st[:, 48:50]))
            dve.wait_ge(x_again_in, 16)
            for cp in range(2):
                cols = slice(cp * (D // 2), (cp + 1) * (D // 2))
                for t in range(TT):
                    dve.scalar_tensor_tensor(out=x1[:, t, cols], in0=y[:, t, cols], scalar=st[:, 48 + t:49 + t], in1=x1[:, t, cols],
                                             op0=ALU.mult, op1=ALU.add).then_inc(x1_ready, 1)
            stage("mod4")
            dve.wait_ge(x1_squared, 1)
            dve.tensor_tensor(st[:, 50:52], st[:, 52:54], st[:, 54:56], ALU.add).then_inc(x1_sums_ready, 1)
            dve.wait_ge(x1_root_ready, 1)
            step(dve.reciprocal(st[:, 50:52], st[:, 50:52]))
            for t in range(TT):
                ins = dve.tensor_scalar(rdiag[:, t, :], c_(IDENT), st[:, 50 + t:51 + t], None, ALU.mult)
            ins.then_inc(rdiag_ready, 1)
            wait_taken(dve, "r2", 0)
            wait_taken(dve, "mod4", 0)

            def h2_low(j):
                dve.wait_ge(h2_hi, j + 1)
                for kk in range(2):
                    k = 2 * j + kk
                    ins = dve.scalar_tensor_tensor(out=hlo[:, k, :], in0=hful[:, j % 2, kk, :], scalar=modc[:, 2, k:k + 1],
                                                   in1=hhi[:, k, :].bitcast(F32), op0=ALU.add, op1=ALU.subtract)
                ins.then_inc(h2_lo, 1)
            for j in range(8):
                b = wait_full(dve, *h2T(j))
                if j >= 2:
                    dve.wait_ge(h2_lo, j - 1)
                for kk in range(2):
                    k = 2 * j + kk
                    ins = dve.scalar_tensor_tensor(out=hful[:, j % 2, kk, :], in0=b[:, kk * SEQ:(kk + 1) * SEQ],
                                                   scalar=modc[:, 3, k:k + 1], in1=rrow[:, :], op0=ALU.mult, op1=ALU.mult)
                ins.then_inc(x1T_scaled, 1)
                dve.wait_ge(x1T_scaled, j + 1)
                dve.sem_inc(bank_free[fill_of(*h2T(j))[0]], 1)
                if j:
                    h2_low(j - 1)
                if j == 4:
                    split_mlp(0, AHEAD - 1)
            h2_low(7)

            dve.wait_ge(y_zero, 1)

            def mlp_turn(q, last):
                def down(c):
                    pair = pair_of(NCH + 4 + c)[0]
                    dve.wait_ge(halves_done, q * (16 * GROUPS) + (h2 + 2 * GROUPS * (c + 1)))
                    d = y[:, :, (c - 4) * NB:(c - 3) * NB]
                    dve.tensor_tensor(d, d, gps[pair][:, :, :], ALU.add).then_inc(gemm_free[pair], 1)
                    if last:
                        dve.wait_ge(gemm_free[pair], q * 4 + (pair_of(NCH + 4 + c)[1] + 1))
                        dve.sem_inc(y_chunk_ready, 1)

                def gated(c):
                    dve.wait_ge(y_squared, 8 + 2 * (c - 3))
                    d = y[:, :, (c - 4) * NB:(c - 3) * NB]
                    step(dve.tensor_tensor(d, d, grow[:, (c - 4) * NB:(c - 3) * NB].unsqueeze(1).broadcast_to([P, TT, NB]), ALU.mult))

                for n in range(16 * GROUPS):
                    if not last or n + AHEAD < 16 * GROUPS:
                        split_mlp(q, n + AHEAD)
                    c, at = divmod(n, 2 * GROUPS)
                    if at == 2 * GROUPS - 1:
                        if c < 4:
                            pair, before = pair_of(NCH + 4 + c)
                            dve.wait_ge(gemm_free[pair], q * 4 + (before + 1))
                            r = rst[:, c % 2]
                            dve.tensor_tensor(r, r, r, ALU.mult).then_inc(relu_squared, 1)
                        else:
                            down(c)
                    if at == 3 and 1 <= c <= 4:
                        for f in (2 * c - 2, 2 * c - 1):
                            dve.wait_ge(act_hi_ready, q * 8 + (f + 1))
                            ks = slice(2 * f, 2 * f + 2)
                            b = mlp_fill(f)[0]
                            lower(alo[:, ks, :], mx[b][:, :].rearrange("p (k n) -> p k n", k=2), ahi[:, ks, :])\
                                .then_inc(bank_free[b], 1)
                    if last and c == 4 and at == 4:
                        dve.wait_ge(ada_used, 4 * KT)
                        dve.sem_inc(acc_full, 1)
                    if last and c == 5 and at == 6:
                        for j in range(4):
                            b, m = mlp_fill(8 * QUARTERS + j)
                            dve.wait_ge(bank_full[b], m + 1)
                            step(gate_rows(j, mx[b], 32))
                    if last and c >= 6 and at == 4:
                        gated(c - 2)
                    if last and c == 7 and at == 6:
                        gated(6)

            with dve.Fori(0, QUARTERS - 1) as q:
                mlp_turn(q, False)
            mlp_turn(QUARTERS - 1, True)

            dve.wait_ge(y_squared, 8 + 8)
            dve.tensor_reduce(st[:, 48:50], yss[:, :, :], AX, ALU.add).then_inc(y_sums_ready, 1)
            d = y[:, :, 3 * NB:4 * NB]
            step(dve.tensor_tensor(d, d, grow[:, 3 * NB:4 * NB].unsqueeze(1).broadcast_to([P, TT, NB]), ALU.mult))
            dve.wait_ge(y_root_ready, 2)
            step(dve.reciprocal(st[:, 48:50], st[:, 48:50]))
            for t in range(TT):
                for cp in range(2):
                    cols = slice(cp * (D // 2), (cp + 1) * (D // 2))
                    dve.scalar_tensor_tensor(out=y[:, t, cols], in0=y[:, t, cols], scalar=st[:, 48 + t:49 + t], in1=x1[:, t, cols],
                                             op0=ALU.mult, op1=ALU.add).then_inc(out_ready, 1)


_INS = ['x', 'c', 'positions', 'ada_w', 'ada_b', 'norm_pre_mix', 'norm_post_mix', 'norm_pre_mlp', 'norm_post_mlp',
        'w_in', 'w_out', 'gdn_conv_w', 'gdn_a_log', 'gdn_dt_bias', 'gdn_norm_w', 'ssm_conv_w', 'ssm_conv_b',
        'ssm_a_log', 'ssm_dt_bias', 'ssm_d', 'ssm_norm_w', 'attn_sinks', 'sc_conv_w', 'w_up', 'w_down']


def shape_constants():
    import numpy as np
    i = np.arange(P)
    r, c = i[:, None], i[None, :]
    same = (r // 64) == (c // 64)
    m = np.zeros((NCONST, P, P), np.float32)
    m[IDENT] = r == c
    m[UINC] = r <= c
    m[UINCB] = (r <= c) & same
    m[SGT] = r > c
    m[SGTB] = (r > c) & same
    m[CH0] = r < 64
    m[CH1] = r >= 64
    for lv in range(6):
        s = 2 ** lv
        m[LV0 + lv] = ((r // (2 * s)) == (c // (2 * s))) & ((r // s) % 2 == 1) & ((c // s) % 2 == 0)
    m[ONES] = 1
    m[AMP] = np.where(c > r, 0, -1e30)
    m[AMC] = np.where(c <= r, 0, -1e30)
    e = np.arange(0, HD, 2, dtype=np.float32) / np.float32(HD)
    return np.ascontiguousarray(m.transpose(1, 0, 2).reshape(P, NCONST * P)), np.power(np.float32(10000.0), -e).astype(np.float32)


def kernel(**inputs):
    import numpy as _np
    import concourse.bacc as _bacc
    from concourse import mybir as _mybir
    from concourse.bass_utils import run_bass_kernel_spmd as _run

    nc = _bacc.Bacc("TRN2", target_bir_lowering=False, num_devices=1, dynamic_dma_scratch_size=1024)
    arrays = {name: _np.ascontiguousarray(inputs[name]) for name in _INS}
    arrays["consts"], arrays["inv_freq"] = shape_constants()
    aps = {}
    for name, value in arrays.items():
        aps[name] = nc.dram_tensor(name, value.shape, _mybir.dt.from_np(value.dtype), kind="ExternalInput").ap()
    aps["out"] = nc.dram_tensor("out", (1, SEQ, D), F32, kind="ExternalOutput").ap()
    build(nc, aps)
    r = _run(nc, [arrays], core_ids=[0])
    return r.results[0]["out"]
```
